# Optimizing a Trainium2 kernel written in Bass

```python
import math
import jax
import jax.numpy as jnp
from jax import lax
import numpy as np

D_MODEL = 1024
BATCH = 1
SEQ = 256
DEPTH = 2
DEC_BATCH = 8
DEC_SEQ = 8
PAST_LEN = 2048
PAGE_SIZE = 128

D_PLE = 256
N_BRANCH = 4
BRANCH_W = D_MODEL // N_BRANCH
CONV_W = 4
CHUNK = 64
EPS = 1e-6

GDN_H = 4
GDN_DK = 64
GDN_DV = BRANCH_W // GDN_H
GDN_QK = GDN_H * GDN_DK
GDN_CONV_CH = 2 * GDN_QK + BRANCH_W
HG_H = 4
HG_DK = 64
HG_DV = BRANCH_W // HG_H
HG_QK = HG_H * HG_DK
SSD_H = 4
SSD_P = BRANCH_W // SSD_H
SSD_G = 2
SSD_N = 128
SSD_CONV_CH = BRANCH_W + 2 * SSD_G * SSD_N
ML_H = 4
ML_DK = 32
ML_DV = BRANCH_W // ML_H
ML_QK = ML_H * ML_DK
D_FF = ((8 * D_MODEL // 3 + 255) // 256) * 256
N_EXPERTS = 8
TOP_K = 2
N_DENSE = (DEPTH + 1) // 2
N_MOE = DEPTH // 2

IN_SPLITS = (GDN_CONV_CH, GDN_H, GDN_H, BRANCH_W,
             HG_QK, HG_QK, BRANCH_W, BRANCH_W,
             BRANCH_W, SSD_CONV_CH, SSD_H,
             ML_QK, ML_QK, BRANCH_W, ML_H, ML_H, BRANCH_W,
             N_BRANCH * D_MODEL)
N_IN = sum(IN_SPLITS)

STATE_KEYS = ('gdn_conv', 'gdn', 'hgrn', 'ssd_conv', 'ssd', 'ml_c', 'ml_n', 'ml_m')
MIXER_KEYS = ('w_in', 'gdn_conv_w', 'gdn_a_log', 'gdn_dt_bias', 'gdn_norm', 'hgrn_norm',
              'ssd_conv_w', 'ssd_conv_b', 'ssd_a_log', 'ssd_dt_bias', 'ssd_d', 'ssd_norm',
              'ml_ig_b', 'ml_fg_b', 'ml_norm', 'w_branch', 'w_out')

kernel_name = 'hybrid_gdn_hgrn2_ssd_mlstm_step'

F32 = jnp.float32

def rmsnorm(x, g):
    xf = x.astype(F32)
    y = xf * lax.rsqrt(jnp.mean(xf * xf, axis=-1, keepdims=True) + EPS)
    return (y * g.astype(F32)).astype(x.dtype)

def l2norm(x):
    x = x.astype(F32)
    return x * lax.rsqrt(jnp.sum(x * x, axis=-1, keepdims=True) + EPS)

def masked_exp(d, mask):
    return jnp.where(mask, jnp.exp(jnp.where(mask, d, 0.0)), 0.0)

def split_cols(t):
    offs, acc = [], 0
    for s in IN_SPLITS[:-1]:
        acc += s
        offs.append(acc)
    return jnp.split(t, offs, axis=-1)

def to_heads(t, h):
    b, l, _ = t.shape
    return t.reshape(b, l, h, -1).transpose(0, 2, 1, 3)

def from_heads(t):
    b, h, l, d = t.shape
    return t.transpose(0, 2, 1, 3).reshape(b, l, h * d)

def gate_heads(t):
    return t.astype(F32).transpose(0, 2, 1)

def chunk_len(l):
    return l if l <= CHUNK else math.gcd(l, CHUNK)

def to_chunks(t, c):
    b, h, l = t.shape[:3]
    t = t.reshape((b, h, l // c, c) + t.shape[3:])
    return jnp.moveaxis(t, 2, 0)

def from_chunks(t):
    n, b, h, c, d = t.shape
    return jnp.moveaxis(t, 0, 2).reshape(b, h, n * c, d)

def causal_conv(x, buf, w, b=None):
    l = x.shape[1]
    xp = jnp.concatenate([buf.astype(x.dtype), x], axis=1)
    y = w[0] * xp[:, :l]
    for j in range(1, CONV_W):
        y = y + w[j] * xp[:, j:j + l]
    if b is not None:
        y = y + b
    return jax.nn.silu(y), xp[:, l:]

def gdn_scan(q, k, v, g, beta, s0):
    c = chunk_len(q.shape[2])
    tri = jnp.tril(jnp.ones((c, c), dtype=bool))
    strict = jnp.tril(jnp.ones((c, c), dtype=bool), -1)
    eye = jnp.eye(c, dtype=F32)
    dv = v.shape[-1]

    def step(s, blk):
        qc, kc, vc, gc, bc = blk
        gam = jnp.cumsum(gc, axis=-1)
        dec = masked_exp(gam[..., :, None] - gam[..., None, :], tri)
        a = jnp.where(strict, bc[..., :, None] * jnp.einsum('bhtk,bhsk->bhts', kc, kc) * dec, 0.0)
        rhs = jnp.concatenate([bc[..., None] * vc, (bc * jnp.exp(gam))[..., None] * kc], axis=-1)
        sol = lax.linalg.triangular_solve(eye + a, rhs, left_side=True, lower=True, unit_diagonal=True)
        u = sol[..., :dv] - jnp.einsum('bhtk,bhkv->bhtv', sol[..., dv:], s)
        att = jnp.einsum('bhtk,bhsk->bhts', qc, kc) * dec
        o = (jnp.exp(gam)[..., None] * jnp.einsum('bhtk,bhkv->bhtv', qc, s)
             + jnp.einsum('bhts,bhsv->bhtv', att, u))
        w_end = jnp.exp(gam[..., -1:] - gam)
        s = (jnp.exp(gam[..., -1])[..., None, None] * s
             + jnp.einsum('bhsk,bhsv->bhkv', kc * w_end[..., None], u))
        return s, o

    xs = tuple(to_chunks(t.astype(F32), c) for t in (q, k, v, g, beta))
    s, o = lax.scan(step, s0.astype(F32), xs)
    return from_chunks(o), s

def hgrn_scan(q, k, v, logf, s0):
    c = chunk_len(q.shape[2])
    tri = jnp.tril(jnp.ones((c, c), dtype=bool))

    def step(s, blk):
        qc, kc, vc, lf = blk
        b = jnp.cumsum(lf, axis=2)
        dec = masked_exp(b[:, :, :, None, :] - b[:, :, None, :, :], tri[:, :, None])
        att = jnp.sum(qc[:, :, :, None, :] * kc[:, :, None, :, :] * dec, axis=-1)
        o = (jnp.einsum('bhtk,bhkv->bhtv', qc * jnp.exp(b), s)
             + jnp.einsum('bhts,bhsv->bhtv', att, vc))
        s = (jnp.exp(b[:, :, -1, :])[..., None] * s
             + jnp.einsum('bhsk,bhsv->bhkv', kc * jnp.exp(b[:, :, -1:, :] - b), vc))
        return s, o

    xs = tuple(to_chunks(t.astype(F32), c) for t in (q, k, v, logf))
    s, o = lax.scan(step, s0.astype(F32), xs)
    return from_chunks(o), s

def ssd_scan(x, dt, da, bm, cm, h0):
    c = chunk_len(x.shape[2])
    tri = jnp.tril(jnp.ones((c, c), dtype=bool))

    def step(h, blk):
        xc, dtc, dac, bc, cc = blk
        cum = jnp.cumsum(dac, axis=-1)
        dec = masked_exp(cum[..., :, None] - cum[..., None, :], tri)
        att = jnp.einsum('bhtn,bhsn->bhts', cc, bc) * dec * dtc[..., None, :]
        y = (jnp.exp(cum)[..., None] * jnp.einsum('bhtn,bhpn->bhtp', cc, h)
             + jnp.einsum('bhts,bhsp->bhtp', att, xc))
        w_end = dtc * jnp.exp(cum[..., -1:] - cum)
        h = (jnp.exp(cum[..., -1])[..., None, None] * h
             + jnp.einsum('bhsp,bhsn->bhpn', xc * w_end[..., None], bc))
        return h, y

    xs = tuple(to_chunks(t.astype(F32), c) for t in (x, dt, da, bm, cm))
    h, y = lax.scan(step, h0.astype(F32), xs)
    return from_chunks(y), h

def mlstm_scan(q, k, v, ig, logf, c0, n0, m0):
    c = chunk_len(q.shape[2])
    tri = jnp.tril(jnp.ones((c, c), dtype=bool))

    def step(carry, blk):
        cm, nm, mm = carry
        qc, kc, vc, igc, lfc = blk
        b = jnp.cumsum(lfc, axis=-1)
        m = b + jnp.maximum(mm[..., None], lax.cummax(igc - b, axis=2))
        w_in = jnp.exp(b + mm[..., None] - m)
        logw = b[..., :, None] - b[..., None, :] + igc[..., None, :] - m[..., :, None]
        wts = masked_exp(logw, tri) * jnp.einsum('bhtk,bhsk->bhts', qc, kc)
        num = (w_in[..., None] * jnp.einsum('bhtk,bhkv->bhtv', qc, cm)
               + jnp.einsum('bhts,bhsv->bhtv', wts, vc))
        nq = w_in * jnp.einsum('bhtk,bhk->bht', qc, nm) + jnp.sum(wts, axis=-1)
        h = num / jnp.maximum(jnp.abs(nq), jnp.exp(-m))[..., None]
        m_end = m[..., -1]
        w_end = jnp.exp(b[..., -1:] - b + igc - m_end[..., None])
        a_end = jnp.exp(b[..., -1] + mm - m_end)
        cm = a_end[..., None, None] * cm + jnp.einsum('bhsk,bhsv->bhkv', kc * w_end[..., None], vc)
        nm = a_end[..., None] * nm + jnp.einsum('bhsk,bhs->bhk', kc, w_end)
        return (cm, nm, m_end), h

    xs = tuple(to_chunks(t.astype(F32), c) for t in (q, k, v, ig, logf))
    (cm, nm, mm), h = lax.scan(step, (c0.astype(F32), n0.astype(F32), m0.astype(F32)), xs)
    return from_chunks(h), cm, nm, mm

def mixer_block(u, st, w, lb):
    dty = u.dtype
    (gdn_in, gdn_b, gdn_a, gdn_z, hg_q, hg_f, hg_v, hg_g,
     ssd_z, ssd_in, ssd_dt, ml_q, ml_k, ml_v, ml_i, ml_f, ml_o, gates) = split_cols(u @ w['w_in'])

    qkv, gdn_conv_new = causal_conv(gdn_in, st['gdn_conv'], w['gdn_conv_w'])
    gq, gk, gv = jnp.split(qkv, [GDN_QK, 2 * GDN_QK], axis=-1)
    gq = l2norm(to_heads(gq, GDN_H)) * (GDN_DK ** -0.5)
    gk = l2norm(to_heads(gk, GDN_H))
    beta = jax.nn.sigmoid(gate_heads(gdn_b))
    g_log = (-jnp.exp(w['gdn_a_log'].astype(F32))[:, None]
             * jax.nn.softplus(gate_heads(gdn_a) + w['gdn_dt_bias'].astype(F32)[:, None]))
    o_a, s_gdn = gdn_scan(gq, gk, to_heads(gv, GDN_H), g_log, beta, st['gdn'])
    o_a = rmsnorm(o_a.astype(dty), w['gdn_norm']) * jax.nn.silu(to_heads(gdn_z, GDN_H))

    f_pre = hg_f.astype(F32)
    lbf = lb.astype(F32)
    log_f = jnp.log(lbf + (1.0 - lbf) * jax.nn.sigmoid(f_pre))
    k_in = (1.0 - lbf) * jax.nn.sigmoid(-f_pre)
    o_b, s_hg = hgrn_scan(to_heads(hg_q, HG_H), to_heads(k_in, HG_H), to_heads(hg_v, HG_H),
                          to_heads(log_f, HG_H), st['hgrn'])
    o_b = rmsnorm(o_b.astype(dty), w['hgrn_norm']) * jax.nn.silu(to_heads(hg_g, HG_H))

    xbc, ssd_conv_new = causal_conv(ssd_in, st['ssd_conv'], w['ssd_conv_w'], w['ssd_conv_b'])
    sx, sb, sc = jnp.split(xbc, [BRANCH_W, BRANCH_W + SSD_G * SSD_N], axis=-1)
    sx = to_heads(sx, SSD_H)
    sb = jnp.repeat(to_heads(sb, SSD_G), SSD_H // SSD_G, axis=1)
    sc = jnp.repeat(to_heads(sc, SSD_G), SSD_H // SSD_G, axis=1)
    dt = jax.nn.softplus(gate_heads(ssd_dt) + w['ssd_dt_bias'].astype(F32)[:, None])
    da = -jnp.exp(w['ssd_a_log'].astype(F32))[:, None] * dt
    y_c, h_ssd = ssd_scan(sx, dt, da, sb, sc, st['ssd'])
    y_c = from_heads(y_c.astype(dty) + w['ssd_d'][:, None, None] * sx)
    o_c = rmsnorm(y_c * jax.nn.silu(ssd_z), w['ssd_norm'])

    ig = gate_heads(ml_i) + w['ml_ig_b'].astype(F32)[:, None]
    lf = jax.nn.log_sigmoid(gate_heads(ml_f) + w['ml_fg_b'].astype(F32)[:, None])
    h_d, c_ml, n_ml, m_ml = mlstm_scan(to_heads(ml_q, ML_H), to_heads(ml_k, ML_H) * (ML_DK ** -0.5),
                                       to_heads(ml_v, ML_H), ig, lf, st['ml_c'], st['ml_n'], st['ml_m'])
    o_d = rmsnorm(h_d.astype(dty), w['ml_norm']) * jax.nn.sigmoid(to_heads(ml_o, ML_H))

    br = jnp.stack([from_heads(o_a), from_heads(o_b), o_c, from_heads(o_d)], axis=2)
    gate = jax.nn.sigmoid(gates.reshape(gates.shape[:2] + (N_BRANCH, D_MODEL)))
    merged = jnp.sum(gate * jnp.einsum('blnw,nwd->blnd', br, w['w_branch']), axis=2)
    out = merged @ w['w_out']
    new = {'gdn_conv': gdn_conv_new.astype(dty), 'gdn': s_gdn.astype(dty), 'hgrn': s_hg.astype(dty),
           'ssd_conv': ssd_conv_new.astype(dty), 'ssd': h_ssd.astype(dty), 'ml_c': c_ml.astype(dty),
           'ml_n': n_ml.astype(dty), 'ml_m': m_ml.astype(dty)}
    return out, new

def swiglu(x, wg, wu, wd):
    return (jax.nn.silu(x @ wg) * (x @ wu)) @ wd

def moe_swiglu(x, w_router, wg, wu, wd):
    logits = (x @ w_router).astype(F32)
    top_v, top_i = lax.top_k(logits, TOP_K)
    top_w = jax.nn.softmax(top_v, axis=-1)
    combine = jnp.einsum('blk,blke->ble', top_w, jax.nn.one_hot(top_i, N_EXPERTS, dtype=F32)).astype(x.dtype)
    y = jnp.zeros_like(x)
    for e in range(N_EXPERTS):
        y = y + combine[..., e:e + 1] * swiglu(x, wg[e], wu[e], wd[e])
    return y

def trunk(x, p, states, prm):
    sm = jax.nn.softmax(prm['hgrn_lb'].astype(F32), axis=0)
    lb_all = jnp.cumsum(sm, axis=0) - sm[0]
    h = x
    outs = {k: [] for k in STATE_KEYS}
    for l in range(DEPTH):
        st = {k: states[k][l] for k in STATE_KEYS}
        wl = {k: prm[k][l] for k in MIXER_KEYS}
        mix, new = mixer_block(rmsnorm(h, prm['g_mix'][l]), st, wl, lb_all[l])
        h = h + mix
        u = rmsnorm(h, prm['g_ffn'][l])
        j = l // 2
        if l % 2 == 0:
            h = h + swiglu(u, prm['w_ff_gate'][j], prm['w_ff_up'][j], prm['w_ff_down'][j])
        else:
            h = h + moe_swiglu(u, prm['w_router'][j], prm['w_ex_gate'][j], prm['w_ex_up'][j], prm['w_ex_down'][j])
        pg = jax.nn.sigmoid(rmsnorm(h, prm['g_ple'][l]) @ prm['w_ple_gate'][l])
        h = h + pg * (p[l] @ prm['w_ple'][l])
        for k in STATE_KEYS:
            outs[k].append(new[k])
    y = rmsnorm(h, prm['g_final'])
    return y, {k: jnp.stack(outs[k]) for k in STATE_KEYS}

def setup_inputs(seed: int = 0) -> dict:
    key = jax.random.key(seed)
    keys = iter(jax.random.split(key, 96))

    def nrm(shape, scale=1.0):
        return scale * jax.random.normal(next(keys), shape, jnp.float32)

    def unif(shape, lo, hi):
        return jax.random.uniform(next(keys), shape, jnp.float32, lo, hi)

    def dt_bias(shape):
        dt = jnp.exp(unif(shape, math.log(1e-3), math.log(1e-1)))
        return dt + jnp.log(-jnp.expm1(-dt))

    def gain(shape):
        return 1.0 + nrm(shape, 0.05)

    return {
        'x_prompt': nrm((BATCH, SEQ, D_MODEL)),
        'x_sample': nrm((DEC_BATCH, DEC_SEQ, D_MODEL)),
        'state_gdn_conv': nrm((DEPTH, DEC_BATCH, CONV_W - 1, GDN_CONV_CH)),
        'state_gdn': nrm((DEPTH, DEC_BATCH, GDN_H, GDN_DK, GDN_DV), 0.1),
        'state_hgrn': nrm((DEPTH, DEC_BATCH, HG_H, HG_DK, HG_DV), 0.5),
        'state_ssd_conv': nrm((DEPTH, DEC_BATCH, CONV_W - 1, SSD_CONV_CH)),
        'state_ssd': nrm((DEPTH, DEC_BATCH, SSD_H, SSD_P, SSD_N), 0.1),
        'state_mlstm_c': nrm((DEPTH, DEC_BATCH, ML_H, ML_DK, ML_DV)),
        'state_mlstm_n': nrm((DEPTH, DEC_BATCH, ML_H, ML_DK)),
        'state_mlstm_m': nrm((DEPTH, DEC_BATCH, ML_H)),
        'p_prompt': nrm((DEPTH, BATCH, SEQ, D_PLE)),
        'p_sample': nrm((DEPTH, DEC_BATCH, DEC_SEQ, D_PLE)),
        'g_mix': gain((DEPTH, D_MODEL)),
        'w_in': nrm((DEPTH, D_MODEL, N_IN), D_MODEL ** -0.5),
        'gdn_conv_w': nrm((DEPTH, CONV_W, GDN_CONV_CH), CONV_W ** -0.5),
        'gdn_a_log': jnp.log(unif((DEPTH, GDN_H), 1.0, 16.0)),
        'gdn_dt_bias': dt_bias((DEPTH, GDN_H)),
        'gdn_norm': gain((DEPTH, GDN_DV)),
        'hgrn_lb': nrm((DEPTH, HG_QK), 0.5),
        'hgrn_norm': gain((DEPTH, HG_DV)),
        'ssd_conv_w': nrm((DEPTH, CONV_W, SSD_CONV_CH), CONV_W ** -0.5),
        'ssd_conv_b': nrm((DEPTH, SSD_CONV_CH), 0.02),
        'ssd_a_log': jnp.log(unif((DEPTH, SSD_H), 1.0, 16.0)),
        'ssd_dt_bias': dt_bias((DEPTH, SSD_H)),
        'ssd_d': gain((DEPTH, SSD_H)),
        'ssd_norm': gain((DEPTH, BRANCH_W)),
        'ml_ig_b': nrm((DEPTH, ML_H), 0.1),
        'ml_fg_b': 3.0 + nrm((DEPTH, ML_H), 0.1),
        'ml_norm': gain((DEPTH, ML_DV)),
        'w_branch': nrm((DEPTH, N_BRANCH, BRANCH_W, D_MODEL), BRANCH_W ** -0.5),
        'w_out': nrm((DEPTH, D_MODEL, D_MODEL), D_MODEL ** -0.5),
        'g_ffn': gain((DEPTH, D_MODEL)),
        'w_ff_gate': nrm((N_DENSE, D_MODEL, D_FF), D_MODEL ** -0.5),
        'w_ff_up': nrm((N_DENSE, D_MODEL, D_FF), D_MODEL ** -0.5),
        'w_ff_down': nrm((N_DENSE, D_FF, D_MODEL), D_FF ** -0.5),
        'w_router': nrm((N_MOE, D_MODEL, N_EXPERTS), D_MODEL ** -0.5),
        'w_ex_gate': nrm((N_MOE, N_EXPERTS, D_MODEL, D_FF), D_MODEL ** -0.5),
        'w_ex_up': nrm((N_MOE, N_EXPERTS, D_MODEL, D_FF), D_MODEL ** -0.5),
        'w_ex_down': nrm((N_MOE, N_EXPERTS, D_FF, D_MODEL), D_FF ** -0.5),
        'w_ple': nrm((DEPTH, D_PLE, D_MODEL), D_PLE ** -0.5),
        'w_ple_gate': nrm((DEPTH, D_MODEL, D_MODEL), D_MODEL ** -0.5),
        'g_ple': gain((DEPTH, D_MODEL)),
        'g_final': gain((D_MODEL,)),
    }

def reference(x_prompt, x_sample, state_gdn_conv, state_gdn, state_hgrn, state_ssd_conv, state_ssd,
              state_mlstm_c, state_mlstm_n, state_mlstm_m, p_prompt, p_sample,
              g_mix, w_in, gdn_conv_w, gdn_a_log, gdn_dt_bias, gdn_norm, hgrn_lb, hgrn_norm,
              ssd_conv_w, ssd_conv_b, ssd_a_log, ssd_dt_bias, ssd_d, ssd_norm,
              ml_ig_b, ml_fg_b, ml_norm, w_branch, w_out, g_ffn,
              w_ff_gate, w_ff_up, w_ff_down, w_router, w_ex_gate, w_ex_up, w_ex_down,
              w_ple, w_ple_gate, g_ple, g_final):
    prm = {'g_mix': g_mix, 'w_in': w_in, 'gdn_conv_w': gdn_conv_w, 'gdn_a_log': gdn_a_log,
           'gdn_dt_bias': gdn_dt_bias, 'gdn_norm': gdn_norm, 'hgrn_lb': hgrn_lb, 'hgrn_norm': hgrn_norm,
           'ssd_conv_w': ssd_conv_w, 'ssd_conv_b': ssd_conv_b, 'ssd_a_log': ssd_a_log,
           'ssd_dt_bias': ssd_dt_bias, 'ssd_d': ssd_d, 'ssd_norm': ssd_norm,
           'ml_ig_b': ml_ig_b, 'ml_fg_b': ml_fg_b, 'ml_norm': ml_norm,
           'w_branch': w_branch, 'w_out': w_out, 'g_ffn': g_ffn,
           'w_ff_gate': w_ff_gate, 'w_ff_up': w_ff_up, 'w_ff_down': w_ff_down,
           'w_router': w_router, 'w_ex_gate': w_ex_gate, 'w_ex_up': w_ex_up, 'w_ex_down': w_ex_down,
           'w_ple': w_ple, 'w_ple_gate': w_ple_gate, 'g_ple': g_ple, 'g_final': g_final}
    bp = x_prompt.shape[0]
    dty = x_prompt.dtype
    st_p = {'gdn_conv': jnp.zeros((DEPTH, bp, CONV_W - 1, GDN_CONV_CH), dty),
            'gdn': jnp.zeros((DEPTH, bp, GDN_H, GDN_DK, GDN_DV), dty),
            'hgrn': jnp.zeros((DEPTH, bp, HG_H, HG_DK, HG_DV), dty),
            'ssd_conv': jnp.zeros((DEPTH, bp, CONV_W - 1, SSD_CONV_CH), dty),
            'ssd': jnp.zeros((DEPTH, bp, SSD_H, SSD_P, SSD_N), dty),
            'ml_c': jnp.zeros((DEPTH, bp, ML_H, ML_DK, ML_DV), dty),
            'ml_n': jnp.zeros((DEPTH, bp, ML_H, ML_DK), dty),
            'ml_m': jnp.zeros((DEPTH, bp, ML_H), dty)}
    st_s = {'gdn_conv': state_gdn_conv, 'gdn': state_gdn, 'hgrn': state_hgrn,
            'ssd_conv': state_ssd_conv, 'ssd': state_ssd, 'ml_c': state_mlstm_c,
            'ml_n': state_mlstm_n, 'ml_m': state_mlstm_m}
    y_prompt, npr = trunk(x_prompt, p_prompt, st_p, prm)
    y_sample, nsm = trunk(x_sample, p_sample, st_s, prm)
    return (y_prompt, y_sample,
            npr['gdn_conv'], npr['gdn'], npr['hgrn'], npr['ssd_conv'], npr['ssd'],
            npr['ml_c'], npr['ml_n'], npr['ml_m'],
            nsm['gdn_conv'], nsm['gdn'], nsm['hgrn'], nsm['ssd_conv'], nsm['ssd'],
            nsm['ml_c'], nsm['ml_n'], nsm['ml_m'])


_drawn_inputs = setup_inputs


def setup_inputs(seed=0):
    import zlib

    import numpy as np

    out = dict(_drawn_inputs(seed))
    spreads = {}
    factors = {'g_ple': 3.038}
    for name, (base, spread) in spreads.items():
        noise = np.random.default_rng([zlib.crc32(name.encode()), seed]).standard_normal(out[name].shape)
        drawn = base * np.exp(spread * noise) if base else spread * noise
        out[name] = jnp.asarray(drawn.astype(out[name].dtype))
    for name, factor in factors.items():
        out[name] = (out[name] * factor).astype(out[name].dtype)
    return out
```

```python
from contextlib import ExitStack

import numpy as np

import concourse.bass as bass
from concourse import mybir

F32 = mybir.dt.float32
U32 = mybir.dt.uint32
ALU = mybir.AluOpType
ACT = mybir.ActivationFunctionType
AX = mybir.AxisListType

DM, SEQ, NB, DS, DEPTH = 1024, 256, 8, 8, 2
T = SEQ + NB * DS
KT = DM // 128
FF = ((8 * DM // 3 + 255) // 256) * 256
FT = FF // 128
NE = 8
BL = 64
NBLK = T // BL
NPB = SEQ // BL
EPS = 1e-6
R = 5
SLAB = 8 * 256
XPW = 3 + SEQ + NB * (3 + DS)

PROJ = ["gdn_in0", "gdn_in1", "gdn_in2", "ml_qk", "hg_q", "hg_v", "ml_v", "gdn_z", "hg_g", "ssd_z",
        "hg_f", "ml_o", "ssd_in0", "ssd_in1", "ssd_in2"]
N_PROJ = len(PROJ)
N_GATED = 4 * 5
N_OUT = 4
DOWN = [(0, 0, 8), (0, 8, 15), (0, 15, 22), (1, 0, 8), (1, 8, 15), (1, 15, 22), (2, 0, 8), (2, 8, 15), (2, 15, 22),
        (3, 0, 6), (3, 6, 12), (3, 12, 17), (3, 17, 22)]
N_FF = 2 * (FF // 256) + len(DOWN)
assert N_FF % R == 0

CST = {}
for _n, _w in (("E", 2 * 8 * 64), ("LM", 2 * 7 * 64), ("TRIM", T), ("ID", 128), ("BLK", 128), ("ONES", 128),
               ("BT", NB * 64), ("BM", NB), ("RESET", 64), ("IOTA", 8), ("EPS", 2)):
    CST[_n] = (sum(w for _, w in CST.values()), _w)
N_CST = sum(w for _, w in CST.values())
PAR = {}
for _n, _w in (("g_mix", 8), ("g_ffn", 8), ("g_ple", 8), ("g_final", 8), ("gcw", 24), ("gcb", 6), ("scw", 24),
               ("scb", 6), ("gnorm", 1), ("hnorm", 1), ("mnorm", 1), ("snorm", 2), ("ssd_d", 2), ("gb", 10),
               ("alog", 4), ("lb", 4)):
    PAR[_n] = (sum(w for _, w in PAR.values()), _w)
N_PAR = sum(w for _, w in PAR.values())


class Steps:

    def __init__(self, sem, names):
        self.sem, self.names, self.count = sem, names.split(), 0

    def at(self, rnd, name):
        return self.sem, rnd * len(self.names) + self.names.index(name) + 1

    def did(self, rnd, name):
        self.count += 1
        assert self.at(rnd, name)[1] == self.count, (name, self.count)
        return self.sem, 1


def trunk_kernel(nc, xT, pT, cst_d, par_d, slabs, wsm_d, wr_d, st_conv, st_gdn, st_hg, st_ssd, st_mlc, st_mln, st_mlm,
                 y_d, o_conv, o_gdn_p, o_gdn_s, o_hg_p, o_hg_s, o_ssd_p, o_ssd_s, o_mlc_p, o_mlc_s,
                 o_mln_p, o_mln_s, o_mlm_p, o_mlm_s):
    ctx = ExitStack()
    with ctx:
        def sb(name, shape, dt=F32):
            return ctx.enter_context(nc.sbuf_tensor(name, shape, dt))

        def sem(name):
            return ctx.enter_context(nc.semaphore(name))

        PJ, Q0, Q1, Q2 = [ctx.enter_context(nc.psum_tensor(n, [128, 2, 512], F32)) for n in ("PJ", "Q0", "Q1", "Q2")]

        ring = sb("ring", [128, R, SLAB])
        cst = sb("cst", [128, N_CST])
        par = sb("par", [128, DEPTH, N_PAR])
        h = sb("h", [128, KT, T])
        u = sb("u", [128, KT, T])
        BR = sb("BR", [128, 4, 2, T])
        wsm = sb("wsm", [128, KT, 20])
        wr = sb("wr", [128, KT, NE])
        NT = 640
        N_MIX = 11 * NT + 6 * XPW + 12 * T + 4 * NT + 13 * NT
        mix = sb("mix", [128, N_MIX])
        stg = sb("stg", [128, 2, NB, 64])
        sth = sb("sth", [128, 2, NB, 64])
        sts = sb("sts", [128, 2, NB, 128])
        stm = sb("stm", [128, 2, NB, 64])
        stn = sb("stn", [128, 2, NB])
        stmm = sb("stmm", [128, 2, NB])
        sconv = sb("sconv", [128, 2, 6, NB, 3])
        cs = sb("cs", [128, 2, 6, 1 + NB, 3])
        rstd = sb("rstd", [128, T])
        Sp = sb("Sp", [128, 2, 2, 128])
        nst = sb("nst", [128, 2, 2])
        mm = sb("mm", [128, NPB + 1, 2])
        mms = sb("mms", [128, 2, NB])
        smb = sb("smb", [128, 5, 2, NBLK])
        beta = sb("beta", [128, 2, NBLK])
        sp3 = sb("sp3", [128, 6, 3 * 2 * NBLK])
        cf = sb("cf", [128, 3, 2])
        G = sb("G", [128, NBLK, 6])
        gt = sb("gt", [128, 2, NBLK, 6])
        egt = sb("egt", [128, 2, NBLK, 6])
        sm1 = sb("sm1", [128, 2, NBLK])
        xtk = sb("xtk", [128, 2, NBLK])
        wend = sb("wend", [128, 2, NBLK])
        msel = sb("msel", [128, 2, NB])
        egc = sb("egc", [128, 2, NPB + NB])
        lbt = sb("lbt", [128, 8, 2])
        lbv = sb("lbv", [128, DEPTH, 2, 2])
        rt = sb("rt", [128, 3, 64])
        ridx = sb("ridx", [128, 3, 8], U32)

        at = [0]

        def part(n):
            a = mix[:, at[0]:at[0] + n]
            at[0] += n
            return a

        def pairs(a):
            return a.rearrange("p (q t) -> p q t", q=2)

        hgq, hgv, mlq, mlk, mlv, gz, hgg, sz, sf, sfn, mlo = [pairs(part(NT)) for _ in range(11)]
        XP = part(6 * XPW).rearrange("p (c t) -> p c t", c=6)
        C6 = [part(6 * T).rearrange("p (c t) -> p c t", c=6) for _ in range(2)]
        GR = [pairs(part(NT)) for _ in range(3)]
        XROW = pairs(part(NT))
        scr = part(13 * NT)

        def sl(i, n=1):
            return scr[:, i * NT:(i + n) * NT]

        def tt(i):
            return pairs(sl(i))

        def c_(name):
            o, w = CST[name]
            return cst[:, o:o + w]

        E = c_("E").rearrange("p (k j t) -> p k j t", k=2, j=8)
        LM = c_("LM").rearrange("p (k j t) -> p k j t", k=2, j=7)
        TRIM, ID, BLK, ONES = c_("TRIM"), c_("ID"), c_("BLK"), c_("ONES")
        BT = c_("BT").rearrange("p (b t) -> p b t", b=NB)
        BM, RESET, IOTA, EPSC = c_("BM"), c_("RESET"), c_("IOTA"), c_("EPS")

        def pr(l, name):
            o, w = PAR[name]
            return par[:, l, o:o + w]

        LN = (slice(0, 64), slice(64, 128))

        def kind(blk):
            return 0 if blk < NPB else 1

        def tk(blk):
            return slice(blk * BL, (blk + 1) * BL)

        def units(blks=range(NBLK)):
            return [(b, q, i) for b in blks for q in range(2) for i in range(2)]

        def bt(a):
            return a.rearrange("p q (b t) -> p q b t", t=BL)

        def bcol(a):
            return a.unsqueeze(3).to_broadcast([128, 2, NBLK, BL])

        def gcol(t, w, m):
            return t[:, w, :, 2 * m:2 * m + 2].rearrange("p b q -> p q b")

        slab_in = [sem(f"slab_in{i}") for i in range(R)]
        slab_used = sem("slab_used")
        consts_in, layer_in, ple_in, out_sem = sem("consts_in"), sem("layer_in"), sem("ple_in"), sem("out_sem")
        h_done = sem("h_done")
        N_NORM = 3 * DEPTH + 1
        norm_act = Steps(sem("norm_act"), "sq root")
        norm_pe = Steps(sem("norm_pe"), "ss")
        norm_dve = Steps(sem("norm_dve"), "rstd u")
        setup_dve = Steps(sem("setup_dve"), "max sub sum rcp sm lb one")
        setup_act = Steps(sem("setup_act"), "exp")
        proj_pe, proj_ev = sem("proj_pe"), sem("proj_ev")
        halo, conv_tap, conv_silu, conv_new = sem("halo"), sem("conv_tap"), sem("conv_silu"), sem("conv_new")
        gp_pe = Steps(sem("gp_pe"), "small gam gr0 gr1 gr2 ig")
        gp_act = Steps(sem("gp_act"), "beta ea abs e ln egt gr0 gr1 gr2")
        gp_dve = Steps(sem("gp_dve"), "smb spc spi u1 d z dz lz rd le lp sp cf G gt xrow")
        gd_pe = Steps(sem("gd_pe"), "l2 ktok vtok kk qk " + " ".join(f"w{j} tu{j}" for j in range(6)) + " skt sv "
                      + " ".join(f"p{c} o{c} k{c}" for c in range(NPB)) + " ps os ks nss")
        gd_act = Steps(sem("gd_act"), "sq rootq rootk dexp egrow skt osq root")
        gd_dve = Steps(sem("gd_dve"), "rn qk dsub dmin D bg kb kw vb lt qkd init qe " + " ".join(
            f"al{j} wb{j} t{j} u{j}" for j in range(6)) + " sv zero " + " ".join(f"u{c}_ s{c}" for c in range(NPB))
            + " sx us ux sd ss o rn2 on br")
        hg_pe = Steps(sem("hg_pe"), "lftok vtok " + "x0 " + " ".join(f"x{i + 1} a{i}" for i in range(9)) + " a9 kw "
                      + " ".join(f"o{c} k{c}" for c in range(NPB)) + " os ks nss")
        hg_act = Steps(sem("hg_act"), "lf lft vt " + " ".join(f"x{i} e{i}" for i in range(10)) + " kw osq root")
        hg_dve = Steps(sem("hg_dve"), "pre kin " + "z0 " + " ".join(f"z{i + 1} m{i} r{i}" for i in range(9)) + " m9 r9" + " zero "
                       + " ".join(f"s{c}" for c in range(NPB)) + " ux sd ss o rn2 on br")
        sd_pe = Steps(sem("sd_pe"), "xtok btok cb " + " ".join(f"t{c} y{c} k{c}" for c in range(NPB))
                      + " t_0 y_0 k_0 t_1 y_1 k_1 nss")
        sd_act = Steps(sem("sd_act"), "dexp egrow xt btp bts " + " ".join(f"t{c}" for c in range(NPB)) + " t_0 t_1 osq root")
        sd_dve = Steps(sem("sd_dve"), "dsub dmin D wdt xw att0 att xx zero " + " ".join(f"s{c}" for c in range(NPB))
                       + " sd0 ss0 sd1 ss1 y0 y1 y2 yz rn2 br")
        ml_pe = Steps(sem("ml_pe"), "vtok ktok kq " + " ".join(f"o{c} k{c}" for c in range(NPB)) + " os ks nss")
        ml_act = Steps(sem("ml_act"), "vt wexp win wend emt dab osq root")
        ml_dve = Steps(sem("ml_dve"), "m0 " + " ".join(f"sc{c} mm{c}" for c in range(NPB))
                       + " inj scs mms xtk sub min selm sel we0 wpre mt qw wt0 wt kw kw0 zero "
                       + " ".join(f"s{c}" for c in range(NPB)) + " ux sd sn0 ss o dmx drc oo rn2 on br")
        gat_pe = sem("gat_pe")
        gat_act, gat_dve = sem("gat_act"), sem("gat_dve")
        out_pe = sem("out_pe")
        out_ev = sem("out_ev")
        ff_pe, ff_act, ff_dve = sem("ff_pe"), sem("ff_act"), sem("ff_dve")
        gat_mul = sem("gat_mul")
        pads = Steps(sem("pads"), "zero")
        dn_pe, dn_dve, dn_mul = sem("dn_pe"), sem("dn_dve"), sem("dn_mul")
        rt_pe = Steps(sem("rt_pe"), "logit crow0 crow1")
        rt_dve = Steps(sem("rt_dve"), "lg max idx idf d s r w2 oh0 oh1 oh2 comb crow0 crow1")
        rt_act = Steps(sem("rt_act"), "e")

        hid = mix[:, 0:FT * T].rearrange("p (f t) -> p f t", f=FT)
        ffs = mix[:, FT * T:(FT + 2) * T].rearrange("p (f t) -> p f t", f=2)
        ytmp = mix[:, (FT + 2) * T:(FT + 4) * T].rearrange("p (f t) -> p f t", f=2)
        crow = mix[:, (FT + 4) * T:(FT + 4 + NE) * T].rearrange("p (e t) -> p e t", e=NE)
        assert (FT + 4 + NE) * T <= N_MIX
        merged = scr[:, 0:KT * T].rearrange("p (k t) -> p k t", k=KT)
        prod = scr[:, KT * T:2 * KT * T].rearrange("p (k t) -> p k t", k=KT)
        sgs = scr[:, 2 * KT * T:(2 * KT + 4) * T].rearrange("p (k t) -> p k t", k=4)
        pt = pairs(scr[:, 11 * NT:12 * NT])
        assert (2 * KT + 4) * T <= 11 * NT
        sqh = scr[:, KT * T:2 * KT * T].rearrange("p (k t) -> p k t", k=KT)

        PER_LAYER = [N_PROJ + N_GATED + N_OUT + n * N_FF + 5 for n in (1, NE)]
        BASE = [0, PER_LAYER[0]]
        TOTAL = sum(PER_LAYER)
        dst_sections = [2, 2]
        N_OUTS = [0]

        def slab(n):
            return ring[:, n % R, :].rearrange("p (k c) -> p k c", k=8)

        def slab2(n):
            return ring[:, n % R, :].rearrange("p (k c) -> p k c", k=2)

        block = ctx.enter_context(nc.Block())

        @block.sync
        def _(sp):
            def load(n, e=None):
                off = 0 if e is None else e
                if n >= R:
                    sp.wait_ge(slab_used, n - R + 1 if e is None else e * N_FF + (n - R + 1))
                src = slabs[n] if e is None else slabs[bass.ds(e * N_FF + n, 1), :, :].rearrange("a p c -> (a p) c")
                sp.dma_start(ring[:, n % R, :], src).then_inc(slab_in[n % R], 16)

            pre = N_PROJ + N_GATED + N_OUT
            for n in range(BASE[1] + pre):
                load(n)
            first = BASE[1] + pre
            with sp.Fori(0, NE) as e:
                for i in range(N_FF):
                    load(first + i, e)
            for n in range(first + NE * N_FF, TOTAL):
                load(n)

        @block.gpsimd
        def _(pool):
            for k in range(KT):
                pool.dma_start(h[:, k, :], xT[k]).then_inc(consts_in, 16)
            pool.dma_start(cst[:], cst_d).then_inc(consts_in, 16)
            pool.dma_start(par[:], par_d.rearrange("l p c -> p l c")).then_inc(consts_in, 16)
            pool.dma_start(wr[:], wr_d).then_inc(consts_in, 16)
            for l in range(DEPTH):
                if l:
                    pool.wait_ge(h_done, 3 * l)
                    pool.wait_ge(out_sem, 16 * N_OUTS[0])
                pool.dma_start(wsm[:], wsm_d[l]).then_inc(layer_in, 16)
                pool.dma_start(sconv[:], st_conv[l]).then_inc(layer_in, 16)
                pool.dma_start(stg[:], st_gdn[l]).then_inc(layer_in, 16)
                pool.dma_start(sth[:], st_hg[l]).then_inc(layer_in, 16)
                pool.dma_start(sts[:], st_ssd[l]).then_inc(layer_in, 16)
                pool.dma_start(stm[:], st_mlc[l]).then_inc(layer_in, 16)
                pool.dma_start(stn[:], st_mln[l]).then_inc(layer_in, 16)
                pool.dma_start(stmm[:], st_mlm[l]).then_inc(layer_in, 16)

                def store(dst, src):
                    N_OUTS[0] += 1
                    pool.dma_start(dst, src).then_inc(out_sem, 16)

                pool.wait_ge(*gd_dve.at(l, f"s{NPB - 1}"))
                store(o_gdn_p[l], Sp[:, NPB % 2, :, 0:64])
                pool.wait_ge(*gd_dve.at(l, "ss"))
                store(o_gdn_s[l], stg[:])
                pool.wait_ge(*hg_dve.at(l, f"s{NPB - 1}"))
                store(o_hg_p[l], Sp[:, NPB % 2, :, 0:64])
                pool.wait_ge(*hg_dve.at(l, "ss"))
                store(o_hg_s[l], sth[:])
                pool.wait_ge(*sd_dve.at(l, f"s{NPB - 1}"))
                store(o_ssd_p[l], Sp[:, NPB % 2, :, :])
                pool.wait_ge(*sd_dve.at(l, "ss1"))
                store(o_ssd_s[l], sts[:])
                pool.wait_ge(*ml_dve.at(l, f"s{NPB - 1}"))
                store(o_mlc_p[l], Sp[:, NPB % 2, :, 0:64])
                store(o_mln_p[l], nst[:, NPB % 2, :])
                store(o_mlm_p[l], mm[:, NPB, :])
                pool.wait_ge(*ml_dve.at(l, "ss"))
                store(o_mlc_s[l], stm[:])
                store(o_mln_s[l], stn[:])
                store(o_mlm_s[l], mms[:])
                pool.wait_ge(conv_new, 4 * (l + 1))
                store(o_conv[l], cs[:])
                pool.wait_ge(*ml_dve.at(l, "br"))
                pool.dma_start(pt, pT[l]).then_inc(ple_in, 16)
            pool.wait_ge(*norm_dve.at(N_NORM - 1, "u"))
            for k in range(KT):
                pool.dma_start(y_d[k], u[:, k, :]).then_inc(out_sem, 16)
                N_OUTS[0] += 1
            pool.wait_ge(out_sem, 16 * N_OUTS[0])

        N_CONSTS = 16 * (KT + 3)
        PER_L_IN = 16 * 8

        @block.tensor
        def _(pe):
            mmul = nc.tensor.matmul

            def take(n, e=None):
                pe.wait_ge(slab_in[n % R], 16 * (n // R + 1) if e is None else e * (16 * (N_FF // R)) + 16 * (n // R + 1))

            def norm(k):
                pe.wait_ge(*norm_act.at(k, "sq"))
                if k == 0:
                    pe.wait_ge(consts_in, N_CONSTS)
                for i in range(KT):
                    last = mmul(Q0[:, 0, 0:T], ONES, sqh[:, i, :], start=(i == 0), stop=(i == KT - 1))
                last.then_inc(*norm_pe.did(k, "ss"))
                pe.wait_ge(*norm_dve.at(k, "u"))

            def linear(n, j, out, rhs, k0=0, k1=KT, start=True, stop=True):
                w = slab(n)
                for k in range(k0, k1):
                    last = mmul(out, w[:, k - k0, j * 128:(j + 1) * 128], rhs[:, k, :],
                                start=(start and k == k0), stop=(stop and k == k1 - 1))
                return last

            def tokens(out, src):
                for b, q, i in units():
                    last = mmul(out[LN[i], q, tk(b)], src[LN[i], q, tk(b)], ID[LN[i], LN[i]], start=True, stop=True)
                return last

            def each(out, lhs, rhs, blks=range(NBLK)):
                for b, q, i in units(blks):
                    last = mmul(out[LN[i], q, tk(b)], lhs[LN[i], q, tk(b)], rhs[LN[i], q, tk(b)], start=True, stop=True)
                return last

            def head_norm(src_done, steps, l, sq):
                pe.wait_ge(*src_done)
                for q in range(2):
                    last = mmul(Q1[:, q, 0:T], BLK, sq[:, q, :], start=True, stop=True)
                last.then_inc(*steps.did(l, "nss"))

            for l in range(DEPTH):
                n0 = BASE[l]
                norm(3 * l)
                for s in range(N_PROJ):
                    take(n0 + s)
                    for j in range(2):
                        m = l * 2 * N_PROJ + 2 * s + j
                        if m >= 2:
                            pe.wait_ge(proj_ev, m - 1)
                        linear(n0 + s, j, PJ[:, j, 0:T], u).then_inc(proj_pe, 1)
                    pe.wait_ge(proj_pe, l * 2 * N_PROJ + 2 * s + 2)
                    pe.sem_inc(slab_used, 1)
                pe.wait_ge(layer_in, PER_L_IN * (l + 1))
                SMP = Q1[:, 0, 0:50].rearrange("p (b g) -> p b g", b=NBLK)
                for b in range(NBLK):
                    for i in range(2):
                        for k in range(KT):
                            last = mmul(SMP[LN[i], b, :], u[:, k, tk(b)], wsm[:, k, i::2], start=(k == 0), stop=(k == KT - 1))
                last.then_inc(*gp_pe.did(l, "small"))
                pe.wait_ge(*gp_dve.at(l, "G"))
                GT = Q1[:, 1, 0:60].rearrange("p (w b g) -> p w b g", w=2, b=NBLK)
                for w in range(2):
                    for kd, b0, b1 in ((0, 0, NPB), (1, NPB, NBLK)):
                        for i in range(2):
                            last = mmul(GT[LN[i], w, b0:b1, :].rearrange("p b g -> p (b g)"), E[LN[i], kd, 6 + w, :],
                                        G[LN[i], b0:b1, :].rearrange("p b g -> p (b g)"), start=True, stop=True)
                last.then_inc(*gp_pe.did(l, "gam"))
                for m, out in ((0, Q0), (1, Q2), (2, Q0)):
                    if m == 2:
                        pe.wait_ge(*gp_act.at(l, "gr0"))
                    for b, q, i in units():
                        last = mmul(out[LN[i], q, tk(b)], G[LN[i], b, 2 * m + q:2 * m + q + 1].to_broadcast([64, 64]),
                                    E[LN[i], kind(b), 6, :], start=True, stop=True)
                    last.then_inc(*gp_pe.did(l, f"gr{m}"))
                pe.wait_ge(*gp_act.at(l, "gr1"))
                for b, q, i in units():
                    last = mmul(Q2[LN[i], q, tk(b)], smb[LN[i], 3, q, b:b + 1].to_broadcast([64, 64]), ID[LN[i], LN[i]],
                                start=True, stop=True)
                last.then_inc(*gp_pe.did(l, "ig"))

                C = C6[0]
                pe.wait_ge(*gd_act.at(l, "sq"))
                pe.wait_ge(*gp_act.at(l, "gr2"))
                pe.wait_ge(*gp_dve.at(l, "gt"))
                sq4 = sl(0, 2).rearrange("p (c t) -> p c t", c=4)
                for c in range(4):
                    last = mmul((Q0, Q1)[c // 2][:, c % 2, 0:T], BLK, sq4[:, c, :], start=True, stop=True)
                last.then_inc(*gd_pe.did(l, "l2"))
                pe.wait_ge(*gd_dve.at(l, "qk"))
                pe.wait_ge(*gp_dve.at(l, "xrow"))
                qT, kT, vT = C[:, 0:2, :], C[:, 2:4, :], C[:, 4:6, :]
                tokens(Q0, kT).then_inc(*gd_pe.did(l, "ktok"))
                tokens(Q1, vT).then_inc(*gd_pe.did(l, "vtok"))
                each(Q2, kT, kT).then_inc(*gd_pe.did(l, "kk"))
                pe.wait_ge(*gd_dve.at(l, "kw"))
                each(Q0, kT, qT).then_inc(*gd_pe.did(l, "qk"))
                pe.wait_ge(*gd_dve.at(l, "qkd"))
                LT, QKD, VB, KB, KW, Tm, U, W, AL, SV, SKT = [tt(i) for i in (3, 4, 5, 6, 7, 8, 9, 10, 11, 0, 1)]
                QE, UU = tt(2), tt(12)
                for j in range(6):
                    blks = range(NBLK) if j < 3 else range(NPB)
                    pe.wait_ge(*gd_dve.at(l, f"al{j}"))
                    pe.wait_ge(*gd_dve.at(l, f"u{j - 1}" if j else "init"))
                    each(Q0, AL, Tm, blks).then_inc(*gd_pe.did(l, f"w{j}"))
                    pe.wait_ge(*gd_dve.at(l, f"wb{j}"))
                    each(Q1, U, W, blks)
                    each(Q2, W, U, blks).then_inc(*gd_pe.did(l, f"tu{j}"))
                pe.wait_ge(*gd_dve.at(l, "u5"))
                each(Q0, KB, U).then_inc(*gd_pe.did(l, "skt"))
                each(Q1, U, VB).then_inc(*gd_pe.did(l, "sv"))
                pe.wait_ge(*gd_act.at(l, "skt"))
                pe.wait_ge(*gd_dve.at(l, "sv"))
                pe.wait_ge(*gd_dve.at(l, "zero"))
                for c in range(NPB):
                    S = Sp[:, c % 2, :, 0:64]
                    if c:
                        pe.wait_ge(*gd_dve.at(l, f"s{c - 1}"))
                    for q in range(2):
                        for i in range(2):
                            last = mmul(Q2[LN[i], q, 0:64], SKT[LN[i], q, tk(c)], S[LN[i], q, :], start=True, stop=True)
                    last.then_inc(*gd_pe.did(l, f"p{c}"))
                    pe.wait_ge(*gd_dve.at(l, f"u{c}_"))
                    for q in range(2):
                        for i in range(2):
                            mmul(Q0[LN[i], q, tk(c)], UU[LN[i], q, tk(c)], QKD[LN[i], q, tk(c)], start=True, stop=False)
                            last = mmul(Q0[LN[i], q, tk(c)], S[LN[i], q, :], QE[LN[i], q, tk(c)], start=False, stop=True)
                    last.then_inc(*gd_pe.did(l, f"o{c}"))
                    for q in range(2):
                        for i in range(2):
                            last = mmul(Q1[LN[i], q, 0:64], KW[LN[i], q, tk(c)], UU[LN[i], q, tk(c)], start=True, stop=True)
                    last.then_inc(*gd_pe.did(l, f"k{c}"))
                SX = sl(5, 2)[:, 0:1024].rearrange("p (q b t) -> p q b t", q=2, b=NB)
                UX = sl(10, 2)[:, 0:1024].rearrange("p (q b t) -> p q b t", q=2, b=NB)
                pe.wait_ge(*gd_dve.at(l, "sx"))
                pe.wait_ge(layer_in, PER_L_IN * (l + 1))
                for q in range(2):
                    for i in range(2):
                        for b in range(NB):
                            last = mmul(Q2[LN[i], q, 0:64], SX[LN[i], q, b, :], stg[LN[i], q, b, :], start=(b == 0), stop=(b == NB - 1))
                last.then_inc(*gd_pe.did(l, "ps"))
                pe.wait_ge(*gd_dve.at(l, "us"))

                def sample_out(Q, V_, A_, S_, X_):
                    for q in range(2):
                        for i in range(2):
                            mmul(Q[LN[i], q, SEQ:T], V_[LN[i], q, SEQ:T], A_[LN[i], q, SEQ:T], start=True, stop=False)
                            for b in range(NB):
                                cols = slice(SEQ + DS * b, SEQ + DS * (b + 1))
                                last = mmul(Q[LN[i], q, cols], S_[LN[i], q, b, :], X_[LN[i], q, cols], start=False, stop=(b == NB - 1))
                    return last

                def sample_state(Q, K_, X_):
                    for q in range(2):
                        for i in range(2):
                            last = mmul(Q[LN[i], q, :], K_[LN[i], q, SEQ:T], X_[LN[i], q, :, :].rearrange("p b v -> p (b v)"),
                                        start=True, stop=True)
                    return last

                sample_out(Q0, UU, QKD, stg, QE).then_inc(*gd_pe.did(l, "os"))
                pe.wait_ge(*gd_dve.at(l, "ux"))
                sample_state(Q1, KW, UX).then_inc(*gd_pe.did(l, "ks"))
                pe.wait_ge(*gd_dve.at(l, "ss"))
                head_norm(gd_act.at(l, "osq"), gd_pe, l, tt(3))

                LFT, VT, ATT, QEh, KWC, KWh = tt(0), tt(1), tt(2), tt(3), tt(4), tt(5)
                ZQ = sl(8, 2)[:, 0:768].rearrange("p (r j t) -> p r j t", r=2, j=6)
                ZK = sl(10, 2)[:, 0:768].rearrange("p (r j t) -> p r j t", r=2, j=6)
                pe.wait_ge(*hg_act.at(l, "lf"))
                pe.wait_ge(*gd_act.at(l, "root"))
                tokens(Q0, sf).then_inc(*hg_pe.did(l, "lftok"))
                tokens(Q1, hgv).then_inc(*hg_pe.did(l, "vtok"))
                pe.wait_ge(*hg_act.at(l, "vt"))
                for n in range(11):
                    if n < 10:
                        b, q = n // 2, n % 2
                        if n >= 2:
                            pe.wait_ge(*hg_act.at(l, f"e{n - 2}"))
                        for i in range(2):
                            last = mmul(Q2[LN[i], n % 2, :], LFT[LN[i], q, tk(b)], E[LN[i], kind(b), :, :].rearrange("p j t -> p (j t)"),
                                        start=True, stop=True)
                        last.then_inc(*hg_pe.did(l, f"x{n}"))
                    if n:
                        n, b, q = n - 1, (n - 1) // 2, (n - 1) % 2
                        pe.wait_ge(*hg_dve.at(l, f"z{n}"))
                        if n >= 2:
                            pe.wait_ge(*hg_dve.at(l, f"m{n - 2}"))
                        for i in range(2):
                            for j in range(6):
                                mmul(Q1[LN[i], n % 2, j * 64:(j + 1) * 64], ZK[LN[i], n % 2, j, :], ZQ[LN[i], n % 2, j, :], start=True, stop=True)
                            last = mmul(Q1[LN[i], n % 2, 384:448], sfn[LN[i], q, tk(b)], hgq[LN[i], q, tk(b)], start=True, stop=True)
                        last.then_inc(*hg_pe.did(l, f"a{n}"))
                tokens(Q0, KWC).then_inc(*hg_pe.did(l, "kw"))
                pe.wait_ge(*hg_act.at(l, "kw"))
                pe.wait_ge(*hg_dve.at(l, "r9"))
                pe.wait_ge(*hg_dve.at(l, "zero"))

                def chunk(c, steps, dve, V_, A_, X_, K_):
                    S = Sp[:, c % 2, :, 0:64]
                    if c:
                        pe.wait_ge(*dve.at(l, f"s{c - 1}"))
                    for q in range(2):
                        for i in range(2):
                            mmul(Q0[LN[i], q, tk(c)], V_[LN[i], q, tk(c)], A_[LN[i], q, tk(c)], start=True, stop=False)
                            last = mmul(Q0[LN[i], q, tk(c)], S[LN[i], q, :], X_[LN[i], q, tk(c)], start=False, stop=True)
                    if steps is ml_pe:
                        for q in range(2):
                            for i in range(2):
                                mmul(Q2[LN[i], q, tk(c)], ONES[LN[i], 0:64], A_[LN[i], q, tk(c)], start=True, stop=False)
                                last = mmul(Q2[LN[i], q, tk(c)], nst[LN[i], c % 2, q:q + 1].to_broadcast([64, 64]),
                                            X_[LN[i], q, tk(c)], start=False, stop=True)
                    last.then_inc(*steps.did(l, f"o{c}"))
                    for q in range(2):
                        for i in range(2):
                            last = mmul(Q1[LN[i], q, 0:64], K_[LN[i], q, tk(c)], V_[LN[i], q, tk(c)], start=True, stop=True)
                            if steps is ml_pe:
                                last = mmul(Q1[LN[i], q, 64:65], K_[LN[i], q, tk(c)], ONES[LN[i], 0:1], start=True, stop=True)
                    last.then_inc(*steps.did(l, f"k{c}"))

                for c in range(NPB):
                    chunk(c, hg_pe, hg_dve, VT, ATT, QEh, KWh)
                sample_out(Q0, VT, ATT, sth, QEh).then_inc(*hg_pe.did(l, "os"))
                pe.wait_ge(*hg_dve.at(l, "ux"))
                sample_state(Q1, KWh, UX).then_inc(*hg_pe.did(l, "ks"))
                pe.wait_ge(*hg_dve.at(l, "ss"))
                head_norm(hg_act.at(l, "osq"), hg_pe, l, tt(7))

                C = C6[1]
                XT, XW, AT, BTK = tt(0), tt(1), tt(2), sl(4, 2).rearrange("p (q b n) -> p q b n", q=2, b=NBLK)
                XWX = sl(6, 2)[:, 0:1024].rearrange("p (q b t) -> p q b t", q=2, b=NB)
                HT = sl(8)[:, 0:256].rearrange("p (q t) -> p q t", q=2)
                HTS = sl(9, 2)[:, 0:1024].rearrange("p (b t) -> p b t", b=NB)
                pe.wait_ge(conv_silu, 12 * (l + 1))
                pe.wait_ge(*hg_act.at(l, "root"))
                pe.wait_ge(*hg_dve.at(l, "o"))
                tokens(Q0, C[:, 0:2, :]).then_inc(*sd_pe.did(l, "xtok"))
                for b, q, i in units():
                    out = Q1[LN[i], q, b * 128:(b + 1) * 128] if b < NPB else Q2[LN[i], q, 0:128]
                    last = mmul(out, C[:, 2 + q, tk(b)], ID[:, :], start=True, stop=True)
                last.then_inc(*sd_pe.did(l, "btok"))
                pe.wait_ge(*sd_dve.at(l, "xw"))
                pe.wait_ge(*sd_act.at(l, "bts"))
                for b, q, i in units():
                    last = mmul(Q0[LN[i], q, tk(b)], C[:, 2 + q, tk(b)], C[:, 4 + q, tk(b)], start=True, stop=True)
                last.then_inc(*sd_pe.did(l, "cb"))
                pe.wait_ge(*sd_dve.at(l, "xx"))
                pe.wait_ge(*sd_dve.at(l, "zero"))
                for c in range(NPB):
                    S = Sp[:, c % 2, :, :]
                    if c:
                        pe.wait_ge(*sd_dve.at(l, f"s{c - 1}"))
                    for q in range(2):
                        last = nc.tensor.transpose(Q2[:, q, 0:128], S[:, q, :], ID[:, :])
                    last.then_inc(*sd_pe.did(l, f"t{c}"))
                    pe.wait_ge(*sd_act.at(l, f"t{c}"))
                    for q in range(2):
                        mmul(Q1[:, q, tk(c)], HT[:, q, :], C[:, 4 + q, tk(c)], start=True, stop=True)
                        for i in range(2):
                            last = mmul(Q0[LN[i], q, tk(c)], XT[LN[i], q, tk(c)], AT[LN[i], q, tk(c)], start=True, stop=True)
                    last.then_inc(*sd_pe.did(l, f"y{c}"))
                    for q in range(2):
                        for i in range(2):
                            last = mmul(Q2[LN[i], q, 128:256], XW[LN[i], q, tk(c)], BTK[LN[i], q, c, :], start=True, stop=True)
                    last.then_inc(*sd_pe.did(l, f"k{c}"))
                Q2f = Q2[:, :, :].rearrange("p a (b n) -> p (a b) n", n=128)
                for q in range(2):
                    pe.wait_ge(*sd_dve.at(l, "ss0" if q else f"s{NPB - 1}"))
                    for b in range(NB):
                        last = nc.tensor.transpose(Q2f[:, b, :], sts[:, q, b, :], ID[:, :])
                    last.then_inc(*sd_pe.did(l, f"t_{q}"))
                    pe.wait_ge(*sd_act.at(l, f"t_{q}"))
                    for b in range(NB):
                        cols = slice(SEQ + DS * b, SEQ + DS * (b + 1))
                        last = mmul(Q1[:, q, cols], HTS[:, b, :], C[:, 4 + q, cols], start=True, stop=True)
                    for i in range(2):
                        last = mmul(Q0[LN[i], q, SEQ:T], XT[LN[i], q, SEQ:T], AT[LN[i], q, SEQ:T], start=True, stop=True)
                    last.then_inc(*sd_pe.did(l, f"y_{q}"))
                    for b in range(NB):
                        for i in range(2):
                            last = mmul(Q2f[LN[i], b, :], XWX[LN[i], q, b, :], BTK[LN[i], q, NPB, :], start=True, stop=True)
                    last.then_inc(*sd_pe.did(l, f"k_{q}"))
                pe.wait_ge(*sd_act.at(l, "osq"))
                pe.wait_ge(*sd_dve.at(l, "yz"))
                for q in range(2):
                    last = mmul(Q1[:, 0, 0:T], ONES, tt(10)[:, q, :], start=(q == 0), stop=(q == 1))
                last.then_inc(*sd_pe.did(l, "nss"))

                VTm, WT, QW, KWm = tt(0), tt(2), tt(3), tt(4)
                pe.wait_ge(*sd_act.at(l, "root"))
                pe.wait_ge(*sd_dve.at(l, "y1"))
                pe.wait_ge(*sd_dve.at(l, "ss1"))
                tokens(Q0, mlv).then_inc(*ml_pe.did(l, "vtok"))
                tokens(Q1, mlk).then_inc(*ml_pe.did(l, "ktok"))
                each(Q2, mlk, mlq).then_inc(*ml_pe.did(l, "kq"))
                pe.wait_ge(*ml_dve.at(l, "kw0"))
                pe.wait_ge(*ml_act.at(l, "vt"))
                pe.wait_ge(*ml_dve.at(l, "zero"))
                for c in range(NPB):
                    chunk(c, ml_pe, ml_dve, VTm, WT, QW, KWm)
                sample_out(Q0, VTm, WT, stm, QW)
                for q in range(2):
                    for i in range(2):
                        mmul(Q2[LN[i], q, SEQ:T], ONES[LN[i], 0:64], WT[LN[i], q, SEQ:T], start=True, stop=False)
                        for b in range(NB):
                            cols = slice(SEQ + DS * b, SEQ + DS * (b + 1))
                            last = mmul(Q2[LN[i], q, cols], stn[LN[i], q, b:b + 1].to_broadcast([64, 64]), QW[LN[i], q, cols],
                                        start=False, stop=(b == NB - 1))
                last.then_inc(*ml_pe.did(l, "os"))
                pe.wait_ge(*ml_dve.at(l, "ux"))
                sample_state(Q1, KWm, UX)
                for q in range(2):
                    for i in range(2):
                        last = mmul(PJ[LN[i], q, 0:NB], KWm[LN[i], q, SEQ:T], BM[LN[i], :], start=True, stop=True)
                last.then_inc(*ml_pe.did(l, "ks"))
                pe.wait_ge(*ml_dve.at(l, "ss"))
                head_norm(ml_act.at(l, "osq"), ml_pe, l, tt(7))

                def gated(n1, g0, src, wait):
                    pe.wait_ge(*wait)
                    take(n1)
                    w = slab2(n1)
                    for t in range(KT):
                        m = 16 * g0 + t
                        if t >= 2:
                            pe.wait_ge(gat_act, m - 1)
                        for k in range(2):
                            last = mmul(PJ[:, t % 2, 0:T], w[:, k, t * 128:(t + 1) * 128], src[:, k, :], start=(k == 0), stop=(k == 1))
                        last.then_inc(gat_pe, 1)
                    pe.wait_ge(gat_pe, 16 * g0 + 8)
                    pe.sem_inc(slab_used, 1)
                    for s in range(4):
                        take(n1 + 1 + s)
                        for j in range(2):
                            m = 16 * g0 + 8 + 2 * s + j
                            if s:
                                pe.wait_ge(gat_act, m - 1)
                            linear(n1 + 1 + s, j, Q2[:, j, 0:T], u).then_inc(gat_pe, 1)
                        pe.wait_ge(gat_pe, 16 * g0 + 8 + 2 * s + 2)
                        pe.sem_inc(slab_used, 1)

                n1 = n0 + N_PROJ
                for n in range(4):
                    gated(n1 + 5 * n, 5 * l + n, BR[:, n], ml_dve.at(l, "br") if n == 0 else (gat_act, 16 * (5 * l + n)))
                n2 = n1 + N_GATED
                pe.wait_ge(gat_dve, 8 * (5 * l + 4))
                for s in range(N_OUT):
                    take(n2 + s)
                    for j in range(2):
                        m = 8 * l + 2 * s + j
                        if s:
                            pe.wait_ge(out_ev, m - 1)
                        linear(n2 + s, j, PJ[:, j, 0:T], merged).then_inc(out_pe, 1)
                    pe.wait_ge(out_pe, 8 * l + 2 * s + 2)
                    pe.sem_inc(slab_used, 1)
                norm(3 * l + 1)
                n3 = n2 + N_OUT

                def swiglu(n3, f0, e=None):
                    def val(c, per):
                        return c if e is None else e * per + c

                    for c in range(FT // 2):
                        take(n3 + 2 * c, e)
                        take(n3 + 2 * c + 1, e)
                        for j in range(2):
                            f = 2 * c + j
                            Q = (Q0, Q1)[f % 2]
                            if f0 or f >= 2:
                                pe.wait_ge(ff_dve, val(f0 * FT + f - 1, FT))
                            linear(n3 + 2 * c, j, Q[:, 0, 0:T], u).then_inc(ff_pe, 1)
                            linear(n3 + 2 * c + 1, j, Q[:, 1, 0:T], u).then_inc(ff_pe, 1)
                        pe.wait_ge(ff_pe, val(f0 * 2 * FT + 4 * c + 4, 2 * FT))
                        pe.sem_inc(slab_used, 2)
                    pe.wait_ge(ff_dve, val(f0 * FT + FT, FT))
                    for d, (s, k0, k1) in enumerate(DOWN):
                        n = n3 + FT + d
                        take(n, e)
                        Q = (PJ, Q2)[s % 2]
                        if k0 == 0 and (f0 or s >= 2):
                            pe.wait_ge(dn_dve, val(f0 * 8 + 2 * s - 2, 8))
                        for j in range(2):
                            last = linear(n, j, Q[:, j, 0:T], hid, k0, k1, start=(k0 == 0), stop=(k1 == FT))
                        last.then_inc(dn_pe, 1)
                        pe.wait_ge(dn_pe, val(f0 * len(DOWN) + d + 1, len(DOWN)))
                        pe.sem_inc(slab_used, 1)

                if l == 0:
                    swiglu(n3, 0)
                    n4 = n3 + N_FF
                else:
                    for t, (t0, t1) in enumerate(((0, 128), (128, 256), (256, T))):
                        for k in range(KT):
                            last = mmul(PJ[0:t1 - t0, 0, t * 8:(t + 1) * 8], u[:, k, t0:t1], wr[:, k, :], start=(k == 0), stop=(k == KT - 1))
                    last.then_inc(*rt_pe.did(0, "logit"))
                    pe.wait_ge(*rt_dve.at(0, "comb"))
                    for half in range(2):
                        if half:
                            pe.wait_ge(*rt_dve.at(0, "crow0"))
                        for e4 in range(4):
                            ex = 4 * half + e4
                            Q = (Q0, Q1)[e4 // 2]
                            for t, (t0, t1) in enumerate(((0, 128), (128, 256), (256, T))):
                                w = t1 - t0
                                last = mmul(Q[:, e4 % 2, t0:t1], rt[0:w, t, 56 + ex:57 + ex].to_broadcast([w, 128]), ID[0:w, 0:w],
                                            start=True, stop=True)
                        last.then_inc(*rt_pe.did(0, f"crow{half}"))
                    pe.wait_ge(*rt_dve.at(0, "crow1"))
                    with pe.Fori(0, NE) as e:
                        swiglu(n3, 1, e)
                    n4 = n3 + NE * N_FF
                norm(3 * l + 2)
                pe.wait_ge(ple_in, 16 * (l + 1))
                gated(n4, 5 * l + 4, pt, norm_dve.at(3 * l + 2, "u"))
            norm(N_NORM - 1)

        @block.scalar
        def _(act):
            av = nc.scalar.activation

            def norm(k):
                if k == 0:
                    act.wait_ge(consts_in, N_CONSTS)
                else:
                    act.wait_ge(h_done, k)
                av(sqh[:, :, :], h[:, :, :], ACT.Square).then_inc(*norm_act.did(k, "sq"))
                act.wait_ge(*norm_act.at(k, "sq"))
                act.wait_ge(*norm_pe.at(k, "ss"))
                av(rstd[:, :], Q0[:, 0, 0:T], ACT.Sqrt, bias=EPSC[:, 0:1], scale=1.0 / DM).then_inc(*norm_act.did(k, "root"))
                act.wait_ge(*norm_act.at(k, "root"))

            tiles = []
            for i in range(6):
                tiles.append(("xp", i))
            tiles += [("mlq", 0), ("mlk", 0)]
            for name in ("hgq", "hgv", "mlv", "gz", "hgg", "sz", "f", "o"):
                tiles += [(name, 0), (name, 1)]
            for i in range(6):
                tiles.append(("xps", i))
            dst = {"hgq": hgq, "hgv": hgv, "mlv": mlv, "gz": gz, "hgg": hgg, "sz": sz, "o": mlo}

            def conv_act(l, g, c):
                m = (2 * l + g) * 6 + c
                act.wait_ge(conv_tap, 8 * (m + 1))
                av(C6[g][:, c, :], cacc[:, m % 2, :], ACT.Silu).then_inc(conv_silu, 1)

            cacc = XROW

            def head_norm(l, steps, dve, pe_, o, sq, rn, src):
                act.wait_ge(*dve.at(l, src))
                av(sq, o, ACT.Square).then_inc(*steps.did(l, "osq"))
                act.wait_ge(*steps.at(l, "osq"))
                act.wait_ge(*pe_.at(l, "nss"))
                av(rn, Q1[:, :, 0:T], ACT.Sqrt, bias=EPSC[:, 0:1], scale=1.0 / 64).then_inc(*steps.did(l, "root"))
                act.wait_ge(*steps.at(l, "root"))

            for l in range(DEPTH):
                if l == 0:
                    act.wait_ge(*setup_dve.at(0, "sub"))
                    av(lbt[:, 3:5, :], lbt[:, 1:3, :], ACT.Exp).then_inc(*setup_act.did(0, "exp"))
                    act.wait_ge(*setup_act.at(0, "exp"))
                norm(3 * l)
                for i, (name, j) in enumerate(tiles):
                    m = l * 30 + i
                    act.wait_ge(proj_pe, m + 1)
                    P = PJ[:, m % 2, 0:T]
                    if name in ("xp", "xps"):
                        g = name == "xps"
                        if i == 0:
                            act.wait_ge(*pads.at(l, "zero"))
                            if l:
                                act.wait_ge(conv_new, 4 * l)
                        if g and j == 0:
                            act.wait_ge(conv_new, 4 * l + 2)
                            act.wait_ge(conv_tap, 96 * l + 48)
                        av(XP[:, j, 3:3 + SEQ], P[:, 0:SEQ], ACT.Copy)
                        last = av(XP[:, j, 3 + SEQ:XPW].rearrange("p (b t) -> p b t", b=NB)[:, :, 3:3 + DS],
                                  P[:, SEQ:T].rearrange("p (b t) -> p b t", b=NB), ACT.Copy)
                    elif name in ("mlq", "mlk"):
                        for hd in range(4):
                            d = (mlq if name == "mlq" else mlk)[64 * (hd % 2):64 * (hd % 2) + 32, hd // 2, :]
                            last = av(d, PJ[32 * hd:32 * hd + 32, m % 2, 0:T], ACT.Copy, scale=1.0 if name == "mlq" else 32 ** -0.5)
                    elif name == "f":
                        av(sf[:, j, :], P, ACT.Sigmoid)
                        last = av(sfn[:, j, :], P, ACT.Sigmoid, scale=-1.0)
                    else:
                        fn = {"gz": ACT.Silu, "hgg": ACT.Silu, "sz": ACT.Silu, "o": ACT.Sigmoid}.get(name, ACT.Copy)
                        last = av(dst[name][:, j, :], P, fn)
                    last.then_inc(proj_ev, 1)
                    if 12 <= i < 18:
                        conv_act(l, 0, i - 12)
                for c in range(6):
                    conv_act(l, 1, c)
                act.wait_ge(*gp_dve.at(l, "smb"))
                av(beta[:, :, :], smb[:, 0, :, :], ACT.Sigmoid).then_inc(*gp_act.did(l, "beta"))
                act.wait_ge(*gp_act.at(l, "beta"))
                av(sm1[:, :, 0:2], pr(l, "alog").rearrange("p (a q) -> p a q", a=2), ACT.Exp).then_inc(*gp_act.did(l, "ea"))
                act.wait_ge(*gp_act.at(l, "ea"))
                act.wait_ge(*gp_dve.at(l, "spi"))
                av(sp3[:, 1, :], sp3[:, 0, :], ACT.Abs).then_inc(*gp_act.did(l, "abs"))
                act.wait_ge(*gp_act.at(l, "abs"))
                av(sp3[:, 2, :], sp3[:, 1, :], ACT.Exp, scale=-1.0).then_inc(*gp_act.did(l, "e"))
                act.wait_ge(*gp_act.at(l, "e"))
                act.wait_ge(*gp_dve.at(l, "u1"))
                av(sp3[:, 4, :], sp3[:, 3, :], ACT.Ln).then_inc(*gp_act.did(l, "ln"))
                act.wait_ge(*gp_act.at(l, "ln"))
                act.wait_ge(*gp_dve.at(l, "gt"))
                av(egt[:, :, :, :], gt[:, :, :, :], ACT.Exp).then_inc(*gp_act.did(l, "egt"))
                act.wait_ge(*gp_act.at(l, "egt"))
                for m, Q in ((0, Q0), (1, Q2), (2, Q0)):
                    act.wait_ge(*gp_pe.at(l, f"gr{m}"))
                    av(GR[m], Q[:, :, 0:T], ACT.Copy).then_inc(*gp_act.did(l, f"gr{m}"))
                    act.wait_ge(*gp_act.at(l, f"gr{m}"))

                C = C6[0]
                act.wait_ge(conv_silu, 12 * l + 6)
                sq4 = sl(0, 2).rearrange("p (c t) -> p c t", c=4)
                av(sq4, C[:, 0:4, :], ACT.Square).then_inc(*gd_act.did(l, "sq"))
                act.wait_ge(*gd_act.at(l, "sq"))
                act.wait_ge(*gd_pe.at(l, "l2"))
                av(sq4[:, 0:2, :], Q0[:, :, 0:T], ACT.Sqrt, bias=EPSC[:, 1:2], scale=64.0).then_inc(*gd_act.did(l, "rootq"))
                act.wait_ge(*gd_act.at(l, "rootq"))
                av(sq4[:, 2:4, :], Q1[:, :, 0:T], ACT.Sqrt, bias=EPSC[:, 0:1], scale=1.0).then_inc(*gd_act.did(l, "rootk"))
                act.wait_ge(*gd_act.at(l, "rootk"))
                act.wait_ge(*gd_dve.at(l, "dmin"))
                av(tt(2), tt(2), ACT.Exp).then_inc(*gd_act.did(l, "dexp"))
                act.wait_ge(*gd_act.at(l, "dexp"))
                act.wait_ge(*gp_act.at(l, "gr2"))
                av(GR[0], GR[0], ACT.Exp).then_inc(*gd_act.did(l, "egrow"))
                act.wait_ge(*gd_act.at(l, "egrow"))
                act.wait_ge(*gd_pe.at(l, "skt"))
                av(tt(1), Q0[:, :, 0:T], ACT.Copy).then_inc(*gd_act.did(l, "skt"))
                act.wait_ge(*gd_act.at(l, "skt"))
                head_norm(l, gd_act, gd_dve, gd_pe, tt(9), tt(3), tt(8), "o")

                act.wait_ge(*hg_dve.at(l, "pre"))
                av(sf, sf, ACT.Ln).then_inc(*hg_act.did(l, "lf"))
                act.wait_ge(*hg_act.at(l, "lf"))
                act.wait_ge(*hg_pe.at(l, "lftok"))
                av(tt(0), Q0[:, :, 0:T], ACT.Copy).then_inc(*hg_act.did(l, "lft"))
                act.wait_ge(*hg_act.at(l, "lft"))
                act.wait_ge(*hg_pe.at(l, "vtok"))
                av(tt(1), Q1[:, :, 0:T], ACT.Copy).then_inc(*hg_act.did(l, "vt"))
                act.wait_ge(*hg_act.at(l, "vt"))
                X = sl(6, 2)[:, 0:1024].rearrange("p (r j t) -> p r j t", r=2, j=8)
                for n in range(10):
                    b, q = n // 2, n % 2
                    act.wait_ge(*hg_pe.at(l, f"x{n}"))
                    if n >= 2:
                        act.wait_ge(*hg_dve.at(l, f"z{n - 2}"))
                    av(X[:, n % 2], Q2[:, n % 2, :].rearrange("p (j t) -> p j t", j=8), ACT.Exp).then_inc(*hg_act.did(l, f"x{n}"))
                    act.wait_ge(*hg_act.at(l, f"x{n}"))
                    o, i_ = (egc[:, q, b:b + 1], X[:, n % 2, 6, BL - 1:BL]) if b < NPB else (egc[:, q, NPB:], X[:, n % 2, 6, DS - 1::DS])
                    av(o, i_, ACT.Copy).then_inc(*hg_act.did(l, f"e{n}"))
                    act.wait_ge(*hg_act.at(l, f"e{n}"))
                act.wait_ge(*hg_pe.at(l, "kw"))
                av(tt(5), Q0[:, :, 0:T], ACT.Copy).then_inc(*hg_act.did(l, "kw"))
                act.wait_ge(*hg_act.at(l, "kw"))
                head_norm(l, hg_act, hg_dve, hg_pe, tt(6), tt(7), tt(8), "o")

                act.wait_ge(*sd_dve.at(l, "dmin"))
                av(tt(3), tt(3), ACT.Exp).then_inc(*sd_act.did(l, "dexp"))
                act.wait_ge(*sd_act.at(l, "dexp"))
                av(GR[1], GR[1], ACT.Exp).then_inc(*sd_act.did(l, "egrow"))
                act.wait_ge(*sd_act.at(l, "egrow"))
                act.wait_ge(*sd_pe.at(l, "xtok"))
                act.wait_ge(*sd_dve.at(l, "xw"))
                av(tt(0), Q0[:, :, 0:T], ACT.Copy).then_inc(*sd_act.did(l, "xt"))
                act.wait_ge(*sd_act.at(l, "xt"))
                BTK = sl(4, 2).rearrange("p (q b n) -> p q b n", q=2, b=NBLK)
                act.wait_ge(*sd_pe.at(l, "btok"))
                av(BTK[:, :, 0:NPB, :], Q1[:, :, :].rearrange("p q (b n) -> p q b n", n=128), ACT.Copy).then_inc(*sd_act.did(l, "btp"))
                act.wait_ge(*sd_act.at(l, "btp"))
                av(BTK[:, :, NPB, :], Q2[:, :, 0:128], ACT.Copy).then_inc(*sd_act.did(l, "bts"))
                act.wait_ge(*sd_act.at(l, "bts"))
                HT = sl(8)[:, 0:256].rearrange("p (q t) -> p q t", q=2)
                HTS = sl(9, 2)[:, 0:1024].rearrange("p (b t) -> p b t", b=NB)
                for c in range(NPB):
                    act.wait_ge(*sd_pe.at(l, f"t{c}"))
                    av(HT, Q2[:, :, 0:128], ACT.Copy).then_inc(*sd_act.did(l, f"t{c}"))
                    act.wait_ge(*sd_act.at(l, f"t{c}"))
                for q in range(2):
                    act.wait_ge(*sd_pe.at(l, f"t_{q}"))
                    av(HTS, Q2[:, :, :].rearrange("p a (b n) -> p (a b) n", n=128), ACT.Copy).then_inc(*sd_act.did(l, f"t_{q}"))
                    act.wait_ge(*sd_act.at(l, f"t_{q}"))
                act.wait_ge(*sd_dve.at(l, "yz"))
                av(tt(10), tt(9), ACT.Square).then_inc(*sd_act.did(l, "osq"))
                act.wait_ge(*sd_act.at(l, "osq"))
                act.wait_ge(*sd_pe.at(l, "nss"))
                av(tt(8)[:, 0, :], Q1[:, 0, 0:T], ACT.Sqrt, bias=EPSC[:, 0:1], scale=1.0 / 256).then_inc(*sd_act.did(l, "root"))
                act.wait_ge(*sd_act.at(l, "root"))

                act.wait_ge(*ml_pe.at(l, "vtok"))
                act.wait_ge(*sd_dve.at(l, "br"))
                av(tt(0), Q0[:, :, 0:T], ACT.Copy).then_inc(*ml_act.did(l, "vt"))
                act.wait_ge(*ml_act.at(l, "vt"))
                act.wait_ge(*ml_dve.at(l, "min"))
                av(tt(2), tt(2), ACT.Exp).then_inc(*ml_act.did(l, "wexp"))
                act.wait_ge(*ml_act.at(l, "wexp"))
                act.wait_ge(*ml_dve.at(l, "wpre"))
                av(tt(5), tt(5), ACT.Exp).then_inc(*ml_act.did(l, "win"))
                act.wait_ge(*ml_act.at(l, "win"))
                av(wend[:, :, :], wend[:, :, :], ACT.Exp).then_inc(*ml_act.did(l, "wend"))
                act.wait_ge(*ml_act.at(l, "wend"))
                act.wait_ge(*ml_dve.at(l, "mt"))
                av(tt(6), tt(6), ACT.Exp, scale=-1.0).then_inc(*ml_act.did(l, "emt"))
                act.wait_ge(*ml_act.at(l, "emt"))
                act.wait_ge(*ml_pe.at(l, "os"))
                av(tt(7), Q2[:, :, 0:T], ACT.Abs).then_inc(*ml_act.did(l, "dab"))
                act.wait_ge(*ml_act.at(l, "dab"))
                head_norm(l, ml_act, ml_dve, ml_pe, tt(9), tt(7), tt(8), "oo")

                def gated(g0):
                    for t in range(16):
                        m = 16 * g0 + t
                        act.wait_ge(gat_pe, m + 1)
                        if t < 8:
                            if t == 0 and g0:
                                act.wait_ge(gat_dve, 8 * g0)
                            av(prod[:, t, :], PJ[:, t % 2, 0:T], ACT.Copy).then_inc(gat_act, 1)
                        else:
                            if t >= 12:
                                act.wait_ge(gat_dve, 8 * g0 + t - 11)
                            av(sgs[:, t % 4, :], Q2[:, t % 2, 0:T], ACT.Sigmoid).then_inc(gat_act, 1)

                act.wait_ge(*ml_dve.at(l, "br"))
                for n in range(4):
                    gated(5 * l + n)
                norm(3 * l + 1)

                def swiglu(f0, e=None):
                    for f in range(FT):
                        act.wait_ge(ff_pe, f0 * 2 * FT + 2 * f + 1 if e is None else e * (2 * FT) + (f0 * 2 * FT + 2 * f + 1))
                        if f0 or f >= 2:
                            act.wait_ge(ff_dve, f0 * FT + f - 1 if e is None else e * FT + (f0 * FT + f - 1))
                        av(ffs[:, f % 2, :], (Q0, Q1)[f % 2][:, 0, 0:T], ACT.Silu).then_inc(ff_act, 1)

                if l == 0:
                    swiglu(0)
                else:
                    act.wait_ge(*rt_dve.at(0, "d"))
                    av(rt[:, :, 24:25], rt[:, :, 24:25], ACT.Exp).then_inc(*rt_act.did(0, "e"))
                    act.wait_ge(*rt_act.at(0, "e"))
                    with act.Fori(0, NE) as e:
                        swiglu(1, e)
                norm(3 * l + 2)
                gated(5 * l + 4)
            norm(N_NORM - 1)

        @block.vector
        def _(dve):
            v = nc.vector

            def norm(k):
                dve.wait_ge(*norm_act.at(k, "root"))
                v.reciprocal(rstd[:, :], rstd[:, :]).then_inc(*norm_dve.did(k, "rstd"))
                dve.wait_ge(*norm_dve.at(k, "rstd"))
                l = min(k // 3, DEPTH - 1)
                g = pr(l, "g_final" if k == N_NORM - 1 else ("g_mix", "g_ffn", "g_ple")[k % 3])
                for i in range(KT):
                    last = v.scalar_tensor_tensor(out=u[:, i, :], in0=h[:, i, :], scalar=g[:, i:i + 1], in1=rstd[:, :],
                                                  op0=ALU.mult, op1=ALU.mult)
                last.then_inc(*norm_dve.did(k, "u"))
                dve.wait_ge(*norm_dve.at(k, "u"))

            dve.wait_ge(consts_in, N_CONSTS)
            lb = pr(0, "lb").rearrange("p (d q) -> p d q", d=2)
            v.tensor_tensor(lbt[:, 0, :], lb[:, 0, :], lb[:, 1, :], ALU.max).then_inc(*setup_dve.did(0, "max"))
            dve.wait_ge(*setup_dve.at(0, "max"))
            v.tensor_tensor(lbt[:, 1:3, :], lb, lbt[:, 0:1, :].to_broadcast([128, 2, 2]), ALU.subtract).then_inc(*setup_dve.did(0, "sub"))
            dve.wait_ge(*setup_dve.at(0, "sub"))
            dve.wait_ge(*setup_act.at(0, "exp"))
            v.tensor_tensor(lbt[:, 5, :], lbt[:, 3, :], lbt[:, 4, :], ALU.add).then_inc(*setup_dve.did(0, "sum"))
            dve.wait_ge(*setup_dve.at(0, "sum"))
            v.reciprocal(lbt[:, 6, :], lbt[:, 5, :]).then_inc(*setup_dve.did(0, "rcp"))
            dve.wait_ge(*setup_dve.at(0, "rcp"))
            v.memset(lbv[:, 0, 0, :], 0.0)
            v.tensor_tensor(lbv[:, 1, 0, :], lbt[:, 4, :], lbt[:, 6, :], ALU.mult).then_inc(*setup_dve.did(0, "sm"))
            dve.wait_ge(*setup_dve.at(0, "sm"))
            v.tensor_scalar(lbv[:, :, 1, :], lbv[:, :, 0, :], -1.0, 1.0, ALU.mult, ALU.add).then_inc(*setup_dve.did(0, "lb"))
            dve.wait_ge(*setup_dve.at(0, "lb"))
            v.memset(cf[:, 2, :], -1.0).then_inc(*setup_dve.did(0, "one"))
            dve.wait_ge(*setup_dve.at(0, "one"))

            cacc = XROW
            muls = [0]

            for l in range(DEPTH):
                norm(3 * l)
                v.memset(XP[:, :, 0:3], 0.0)
                for i in range(2):
                    v.memset(mlq[64 * i + 32:64 * i + 64, :, :], 0.0)
                    last = v.memset(mlk[64 * i + 32:64 * i + 64, :, :], 0.0)
                last.then_inc(*pads.did(l, "zero"))
                dve.wait_ge(*pads.at(l, "zero"))
                dve.wait_ge(layer_in, PER_L_IN * (l + 1))

                def conv(g):
                    cw = pr(l, "scw" if g else "gcw").rearrange("p (c j) -> p c j", c=6)
                    cb = pr(l, "scb" if g else "gcb")
                    if g:
                        dve.wait_ge(conv_tap, 96 * l + 48)
                        dve.wait_ge(conv_new, 4 * l + 2)
                    samp = XP[:, :, 3 + SEQ:XPW].rearrange("p c (b t) -> p c b t", b=NB)
                    for c in range(6):
                        last = v.tensor_copy(samp[:, c, :, 0:3], sconv[:, g, c, :, :])
                    last.then_inc(halo, 1)
                    dve.wait_ge(halo, 2 * l + g + 1)
                    for c in range(6):
                        m = (2 * l + g) * 6 + c
                        dve.wait_ge(proj_ev, 30 * l + (24 if g else 0) + c + 1)
                        if m >= 2:
                            dve.wait_ge(conv_silu, m - 1)
                        if c == 0 and g == 0 and l:
                            dve.wait_ge(*ml_dve.at(l - 1, "br"))
                        ap_, as_ = cacc[:, m % 2, 0:SEQ], cacc[:, m % 2, SEQ:T].rearrange("p (b t) -> p b t", b=NB)
                        for j in range(4):
                            if j:
                                dve.wait_ge(conv_tap, 8 * m + 2 * j - 1)
                            if j == 0:
                                v.tensor_scalar(ap_, XP[:, c, 0:SEQ], cw[:, c, 0:1], cb[:, c:c + 1], ALU.mult, ALU.add).then_inc(conv_tap, 1)
                                v.tensor_scalar(as_, samp[:, c, :, 0:DS], cw[:, c, 0:1], cb[:, c:c + 1], ALU.mult, ALU.add).then_inc(conv_tap, 1)
                            else:
                                v.scalar_tensor_tensor(out=ap_, in0=XP[:, c, j:j + SEQ], scalar=cw[:, c, j:j + 1], in1=ap_,
                                                       op0=ALU.mult, op1=ALU.add).then_inc(conv_tap, 1)
                                dve.wait_ge(conv_tap, 8 * m + 2 * j)
                                v.scalar_tensor_tensor(out=as_, in0=samp[:, c, :, j:j + DS], scalar=cw[:, c, j:j + 1], in1=as_,
                                                       op0=ALU.mult, op1=ALU.add).then_inc(conv_tap, 1)
                    v.tensor_copy(cs[:, g, :, 0, :], XP[:, :, SEQ:SEQ + 3]).then_inc(conv_new, 1)
                    for c in range(6):
                        last = v.tensor_copy(cs[:, g, c, 1:, :], samp[:, c, :, DS:DS + 3])
                    last.then_inc(conv_new, 1)

                conv(0)
                conv(1)

                dve.wait_ge(*gp_pe.at(l, "small"))
                SMP = Q1[:, 0, 0:50].rearrange("p (b g q) -> p g q b", b=NBLK, g=5)
                gb = pr(l, "gb").rearrange("p (g q) -> p g q", g=5)
                v.tensor_tensor(smb[:, :, :, :], SMP, gb.unsqueeze(3).to_broadcast([128, 5, 2, NBLK]), ALU.add).then_inc(*gp_dve.did(l, "smb"))
                dve.wait_ge(*gp_dve.at(l, "smb"))
                smf = smb[:, :, :, :].rearrange("p g q b -> p (g q b)")
                w = 2 * NBLK
                spi, e_, u1, ln, d = sp3[:, 0, :], sp3[:, 2, :], sp3[:, 3, :], sp3[:, 4, :], sp3[:, 5, :]
                v.tensor_copy(spi[:, 0:2 * w], smf[:, w:3 * w]).then_inc(*gp_dve.did(l, "spc"))
                dve.wait_ge(*gp_dve.at(l, "spc"))
                v.tensor_scalar(spi[:, 2 * w:3 * w], smf[:, 4 * w:5 * w], -1.0, None, ALU.mult).then_inc(*gp_dve.did(l, "spi"))
                dve.wait_ge(*gp_dve.at(l, "spi"))
                dve.wait_ge(*gp_act.at(l, "e"))
                v.tensor_scalar(u1, e_, 1.0, None, ALU.add).then_inc(*gp_dve.did(l, "u1"))
                dve.wait_ge(*gp_dve.at(l, "u1"))
                v.tensor_scalar(d, u1, -1.0, None, ALU.add).then_inc(*gp_dve.did(l, "d"))
                dve.wait_ge(*gp_dve.at(l, "d"))
                z = sp3[:, 1, :]
                v.tensor_scalar(z, d, 0.0, None, ALU.is_equal).then_inc(*gp_dve.did(l, "z"))
                dve.wait_ge(*gp_dve.at(l, "z"))
                dve.wait_ge(*gp_act.at(l, "ln"))
                v.tensor_tensor(d, d, z, ALU.add).then_inc(*gp_dve.did(l, "dz"))
                dve.wait_ge(*gp_dve.at(l, "dz"))
                v.tensor_tensor(ln, ln, z, ALU.add).then_inc(*gp_dve.did(l, "lz"))
                dve.wait_ge(*gp_dve.at(l, "lz"))
                v.reciprocal(d, d).then_inc(*gp_dve.did(l, "rd"))
                dve.wait_ge(*gp_dve.at(l, "rd"))
                v.tensor_tensor(ln, ln, e_, ALU.mult).then_inc(*gp_dve.did(l, "le"))
                dve.wait_ge(*gp_dve.at(l, "le"))
                v.tensor_tensor(ln, ln, d, ALU.mult).then_inc(*gp_dve.did(l, "lp"))
                dve.wait_ge(*gp_dve.at(l, "lp"))
                v.scalar_tensor_tensor(out=spi, in0=spi, scalar=0.0, in1=ln, op0=ALU.max, op1=ALU.add).then_inc(*gp_dve.did(l, "sp"))
                dve.wait_ge(*gp_dve.at(l, "sp"))
                dve.wait_ge(*gp_act.at(l, "ea"))
                v.tensor_scalar(cf[:, 0:2, :], sm1[:, :, 0:2], -1.0, None, ALU.mult).then_inc(*gp_dve.did(l, "cf"))
                dve.wait_ge(*gp_dve.at(l, "cf"))
                v.tensor_tensor(G[:, :, :].rearrange("p b g -> p g b"), spi.rearrange("p (g b) -> p g b", b=NBLK),
                                cf[:, :, :].rearrange("p m q -> p (m q)").unsqueeze(2).to_broadcast([128, 6, NBLK]),
                                ALU.mult).then_inc(*gp_dve.did(l, "G"))
                dve.wait_ge(*gp_dve.at(l, "G"))
                dt = spi[:, w:2 * w].rearrange("p (q b) -> p q b", q=2)
                dve.wait_ge(*gp_pe.at(l, "gam"))
                v.tensor_copy(gt[:, :, :, :], Q1[:, 1, 0:60].rearrange("p (w b g) -> p w b g", w=2, b=NBLK)).then_inc(*gp_dve.did(l, "gt"))
                dve.wait_ge(*gp_dve.at(l, "gt"))
                dve.wait_ge(*gp_pe.at(l, "ig"))
                dve.wait_ge(*gp_act.at(l, "gr2"))
                dve.wait_ge(conv_silu, 12 * (l + 1))
                v.tensor_tensor(XROW, Q2[:, :, 0:T], GR[2], ALU.subtract).then_inc(*gp_dve.did(l, "xrow"))
                dve.wait_ge(*gp_dve.at(l, "xrow"))

                def decay(steps, act_, D, m):
                    v.tensor_tensor(bt(D), bt(GR[m]), bcol(gcol(gt, 0, m)), ALU.subtract).then_inc(*steps.did(l, "dsub"))
                    dve.wait_ge(*steps.at(l, "dsub"))
                    v.tensor_scalar(D, D, 0.0, None, ALU.min).then_inc(*steps.did(l, "dmin"))
                    dve.wait_ge(*steps.at(l, "dmin"))
                    dve.wait_ge(*act_.at(l, "dexp"))
                    v.tensor_tensor(D, D, TRIM.unsqueeze(1).to_broadcast([128, 2, T]), ALU.mult).then_inc(*steps.did(l, "D"))
                    dve.wait_ge(*steps.at(l, "D"))

                def norm_gate(steps, act_, o, rn, w_, z_, br):
                    dve.wait_ge(*act_.at(l, "root"))
                    v.reciprocal(rn, rn).then_inc(*steps.did(l, "rn2"))
                    dve.wait_ge(*steps.at(l, "rn2"))
                    v.tensor_tensor(o, o, rn, ALU.mult).then_inc(*steps.did(l, "on"))
                    dve.wait_ge(*steps.at(l, "on"))
                    v.scalar_tensor_tensor(out=BR[:, br], in0=o, scalar=w_, in1=z_, op0=ALU.mult, op1=ALU.mult)\
                     .then_inc(*steps.did(l, "br"))
                    dve.wait_ge(*steps.at(l, "br"))

                C = C6[0]
                LT, QKD, VB, KB, KW, Tm, U, W, AL, SV, SKT = [tt(i) for i in (3, 4, 5, 6, 7, 8, 9, 10, 11, 0, 1)]
                QE, UU, D = tt(2), tt(12), tt(2)
                sq4 = sl(0, 2).rearrange("p (c t) -> p c t", c=4)
                dve.wait_ge(*gd_act.at(l, "rootk"))
                v.reciprocal(sq4, sq4).then_inc(*gd_dve.did(l, "rn"))
                dve.wait_ge(*gd_dve.at(l, "rn"))
                v.tensor_tensor(C[:, 0:4, :], C[:, 0:4, :], sq4, ALU.mult).then_inc(*gd_dve.did(l, "qk"))
                dve.wait_ge(*gd_dve.at(l, "qk"))
                decay(gd_dve, gd_act, D, 0)
                dve.wait_ge(*gp_act.at(l, "egt"))
                v.tensor_tensor(sm1[:, :, :], beta[:, :, :], gcol(egt, 0, 0), ALU.mult).then_inc(*gd_dve.did(l, "bg"))
                dve.wait_ge(*gd_dve.at(l, "bg"))
                dve.wait_ge(*gd_pe.at(l, "ktok"))
                v.tensor_tensor(bt(KB), bt(Q0[:, :, 0:T]), bcol(sm1[:, :, :]), ALU.mult).then_inc(*gd_dve.did(l, "kb"))
                dve.wait_ge(*gd_dve.at(l, "kb"))
                v.tensor_tensor(bt(KW), bt(Q0[:, :, 0:T]), bcol(gcol(egt, 1, 0)), ALU.mult).then_inc(*gd_dve.did(l, "kw"))
                dve.wait_ge(*gd_dve.at(l, "kw"))
                dve.wait_ge(*gd_pe.at(l, "vtok"))
                v.tensor_tensor(bt(VB), bt(Q1[:, :, 0:T]), bcol(beta[:, :, :]), ALU.mult).then_inc(*gd_dve.did(l, "vb"))
                dve.wait_ge(*gd_dve.at(l, "vb"))
                dve.wait_ge(*gd_pe.at(l, "kk"))
                v.tensor_tensor(LT, Q2[:, :, 0:T], D, ALU.mult).then_inc(*gd_dve.did(l, "lt"))
                dve.wait_ge(*gd_dve.at(l, "lt"))
                dve.wait_ge(*gd_pe.at(l, "qk"))
                v.tensor_tensor(QKD, Q0[:, :, 0:T], D, ALU.mult).then_inc(*gd_dve.did(l, "qkd"))
                dve.wait_ge(*gd_dve.at(l, "qkd"))
                for i in range(2):
                    idl = ID[LN[i], LN[i]].unsqueeze(1).unsqueeze(1).to_broadcast([64, 2, NBLK, 64])
                    v.tensor_copy(bt(Tm)[LN[i]], idl)
                    last = v.tensor_copy(bt(U)[LN[i]], idl)
                last.then_inc(*gd_dve.did(l, "init"))
                dve.wait_ge(*gd_dve.at(l, "init"))
                dve.wait_ge(*gd_act.at(l, "egrow"))
                v.tensor_tensor(QE, C[:, 0:2, :], GR[0], ALU.mult).then_inc(*gd_dve.did(l, "qe"))
                dve.wait_ge(*gd_dve.at(l, "qe"))
                for j in range(6):
                    nb = NBLK if j < 3 else NPB
                    n = nb * BL
                    dve.wait_ge(*gd_dve.at(l, "qe"))
                    v.tensor_tensor(bt(AL)[:, :, 0:NPB, :], bt(LT)[:, :, 0:NPB, :],
                                    LM[:, 0, j, :].unsqueeze(1).unsqueeze(1).to_broadcast([128, 2, NPB, BL]), ALU.mult)
                    last = v.tensor_tensor(AL[:, :, SEQ:T], LT[:, :, SEQ:T], LM[:, 1, j, :].unsqueeze(1).to_broadcast([128, 2, BL]), ALU.mult)
                    last.then_inc(*gd_dve.did(l, f"al{j}"))
                    dve.wait_ge(*gd_dve.at(l, f"al{j}"))
                    dve.wait_ge(*gd_pe.at(l, f"w{j}"))
                    v.tensor_tensor(bt(W)[:, :, 0:nb], bt(Q0[:, :, 0:T])[:, :, 0:nb], bcol(beta[:, :, :])[:, :, 0:nb], ALU.mult)\
                     .then_inc(*gd_dve.did(l, f"wb{j}"))
                    dve.wait_ge(*gd_dve.at(l, f"wb{j}"))
                    dve.wait_ge(*gd_pe.at(l, f"tu{j}"))
                    v.tensor_tensor(Tm[:, :, 0:n], Tm[:, :, 0:n], Q1[:, :, 0:n], ALU.subtract).then_inc(*gd_dve.did(l, f"t{j}"))
                    dve.wait_ge(*gd_dve.at(l, f"t{j}"))
                    v.tensor_tensor(U[:, :, 0:n], U[:, :, 0:n], Q2[:, :, 0:n], ALU.subtract).then_inc(*gd_dve.did(l, f"u{j}"))
                    dve.wait_ge(*gd_dve.at(l, f"u{j}"))
                dve.wait_ge(*gd_pe.at(l, "sv"))
                v.tensor_copy(SV, Q1[:, :, 0:T]).then_inc(*gd_dve.did(l, "sv"))
                dve.wait_ge(*gd_dve.at(l, "sv"))
                v.memset(Sp[:, 0, :, 0:64], 0.0).then_inc(*gd_dve.did(l, "zero"))
                dve.wait_ge(*gd_dve.at(l, "zero"))
                EG = GR[0]

                def state(c, steps, pe_, dcol, q1=Q1, w=64, o=0):
                    dve.wait_ge(*pe_.at(l, f"k{c}"))
                    for q in range(2):
                        last = v.scalar_tensor_tensor(out=Sp[:, (c + 1) % 2, q, 0:w], in0=Sp[:, c % 2, q, 0:w], scalar=dcol(q, c),
                                                      in1=q1[:, q, o:o + w], op0=ALU.mult, op1=ALU.add)
                        if steps is ml_dve:
                            last = v.scalar_tensor_tensor(out=nst[:, (c + 1) % 2, q:q + 1], in0=nst[:, c % 2, q:q + 1],
                                                          scalar=dcol(q, c), in1=q1[:, q, 64:65], op0=ALU.mult, op1=ALU.add)
                    last.then_inc(*steps.did(l, f"s{c}"))
                    dve.wait_ge(*steps.at(l, f"s{c}"))

                def end_col(EG):
                    return lambda q, c: EG[:, q, (c + 1) * BL - 1:(c + 1) * BL]

                for c in range(NPB):
                    dve.wait_ge(*gd_pe.at(l, f"p{c}"))
                    v.tensor_tensor(UU[:, :, tk(c)], SV[:, :, tk(c)], Q2[:, :, 0:64], ALU.subtract).then_inc(*gd_dve.did(l, f"u{c}_"))
                    dve.wait_ge(*gd_dve.at(l, f"u{c}_"))
                    state(c, gd_dve, gd_pe, end_col(EG))
                SX = sl(5, 2)[:, 0:1024].rearrange("p (q b t) -> p q b t", q=2, b=NB)
                UX = sl(10, 2)[:, 0:1024].rearrange("p (q b t) -> p q b t", q=2, b=NB)
                dve.wait_ge(*gd_act.at(l, "skt"))

                def spread_t(out, src):
                    return v.tensor_tensor(out, src[:, :, SEQ:T].unsqueeze(2).to_broadcast([128, 2, NB, 64]),
                                           BT.unsqueeze(1).to_broadcast([128, 2, NB, 64]), ALU.mult)

                def spread_s(out, src):
                    return v.tensor_tensor(out, src[:, :, SEQ:T].unsqueeze(2).to_broadcast([128, 2, NB, 64]),
                                           BM.unsqueeze(1).unsqueeze(3).to_broadcast([128, 2, NB, 64]), ALU.mult)

                spread_t(SX, SKT).then_inc(*gd_dve.did(l, "sx"))
                dve.wait_ge(*gd_dve.at(l, "sx"))
                dve.wait_ge(*gd_pe.at(l, "ps"))
                v.tensor_tensor(UU[:, :, SEQ:T], SV[:, :, SEQ:T], Q2[:, :, 0:64], ALU.subtract).then_inc(*gd_dve.did(l, "us"))
                dve.wait_ge(*gd_dve.at(l, "us"))
                spread_s(UX, UU).then_inc(*gd_dve.did(l, "ux"))
                dve.wait_ge(*gd_dve.at(l, "ux"))

                def sample_state(steps, pe_, S, dec, q1=Q1):
                    dve.wait_ge(*pe_.at(l, "ks"))
                    v.tensor_tensor(S[:, :, :, :], S[:, :, :, :], dec.unsqueeze(3).to_broadcast([128, 2, NB, 64]), ALU.mult)\
                     .then_inc(*steps.did(l, "sd"))
                    dve.wait_ge(*steps.at(l, "sd"))
                    return v.tensor_tensor(S[:, :, :, :], S[:, :, :, :], q1[:, :, :].rearrange("p q (b v) -> p q b v", b=NB), ALU.add)

                sample_state(gd_dve, gd_pe, stg, EG[:, :, SEQ + DS - 1::DS]).then_inc(*gd_dve.did(l, "ss"))
                dve.wait_ge(*gd_dve.at(l, "ss"))
                v.tensor_copy(tt(9), Q0[:, :, 0:T]).then_inc(*gd_dve.did(l, "o"))
                dve.wait_ge(*gd_dve.at(l, "o"))
                norm_gate(gd_dve, gd_act, tt(9), tt(8), pr(l, "gnorm"), gz, 0)
                dve.wait_ge(*gd_dve.at(l, "br"))

                for q in range(2):
                    last = v.tensor_scalar(sf[:, q, :], sf[:, q, :], lbv[:, l, 1, q:q + 1], lbv[:, l, 0, q:q + 1], ALU.mult, ALU.add)
                last.then_inc(*hg_dve.did(l, "pre"))
                dve.wait_ge(*hg_dve.at(l, "pre"))
                for q in range(2):
                    last = v.tensor_scalar(sfn[:, q, :], sfn[:, q, :], lbv[:, l, 1, q:q + 1], None, ALU.mult)
                last.then_inc(*hg_dve.did(l, "kin"))
                dve.wait_ge(*hg_dve.at(l, "kin"))
                ATT, QEh, KWC = tt(2), tt(3), tt(4)
                X = sl(6, 2)[:, 0:1024].rearrange("p (r j t) -> p r j t", r=2, j=8)
                ZQ = sl(8, 2)[:, 0:768].rearrange("p (r j t) -> p r j t", r=2, j=6)
                ZK = sl(10, 2)[:, 0:768].rearrange("p (r j t) -> p r j t", r=2, j=6)
                MA = sl(12)[:, 0:448].rearrange("p (j t) -> p j t", j=7)
                for n in range(11):
                    if n < 10:
                        b, q = n // 2, n % 2
                        dve.wait_ge(*hg_act.at(l, f"x{n}"))
                        if n >= 2:
                            dve.wait_ge(*hg_pe.at(l, f"a{n - 2}"))
                        kb_, qb_ = sfn[:, q, tk(b)].unsqueeze(1), hgq[:, q, tk(b)].unsqueeze(1)
                        v.tensor_tensor(ZK[:, n % 2], X[:, n % 2, 0:6, :], kb_.to_broadcast([128, 6, BL]), ALU.mult)
                        v.tensor_tensor(ZQ[:, n % 2], X[:, n % 2, 0:6, :], qb_.to_broadcast([128, 6, BL]), ALU.mult)
                        v.tensor_tensor(QEh[:, q, tk(b)], X[:, n % 2, 6, :], hgq[:, q, tk(b)], ALU.mult)
                        v.tensor_tensor(KWC[:, q, tk(b)], X[:, n % 2, 7, :], sfn[:, q, tk(b)], ALU.mult).then_inc(*hg_dve.did(l, f"z{n}"))
                        dve.wait_ge(*hg_dve.at(l, f"z{n}"))
                    if n:
                        n, b, q = n - 1, (n - 1) // 2, (n - 1) % 2
                        dve.wait_ge(*hg_pe.at(l, f"a{n}"))
                        v.tensor_tensor(MA, Q1[:, n % 2, 0:448].rearrange("p (j t) -> p j t", j=7), LM[:, kind(b), :, :], ALU.mult)\
                         .then_inc(*hg_dve.did(l, f"m{n}"))
                        dve.wait_ge(*hg_dve.at(l, f"m{n}"))
                        v.tensor_reduce(ATT[:, q, tk(b)], MA.rearrange("p j t -> p t j"), AX.X, ALU.add).then_inc(*hg_dve.did(l, f"r{n}"))
                        dve.wait_ge(*hg_dve.at(l, f"r{n}"))
                dve.wait_ge(out_sem, 16 * (13 * l + 2))
                v.memset(Sp[:, 0, :, 0:64], 0.0).then_inc(*hg_dve.did(l, "zero"))
                dve.wait_ge(*hg_dve.at(l, "zero"))
                dve.wait_ge(*hg_act.at(l, "e9"))
                for c in range(NPB):
                    state(c, hg_dve, hg_pe, lambda q, c: egc[:, q, c:c + 1])
                spread_s(UX, tt(1)).then_inc(*hg_dve.did(l, "ux"))
                dve.wait_ge(*hg_dve.at(l, "ux"))
                sample_state(hg_dve, hg_pe, sth, egc[:, :, NPB:]).then_inc(*hg_dve.did(l, "ss"))
                dve.wait_ge(*hg_dve.at(l, "ss"))
                v.tensor_copy(tt(6), Q0[:, :, 0:T]).then_inc(*hg_dve.did(l, "o"))
                dve.wait_ge(*hg_dve.at(l, "o"))
                norm_gate(hg_dve, hg_act, tt(6), tt(8), pr(l, "hnorm"), hgg, 1)
                dve.wait_ge(*hg_dve.at(l, "br"))

                C = C6[1]
                XT, XW, AT, D = tt(0), tt(1), tt(2), tt(3)
                XWX = sl(6, 2)[:, 0:1024].rearrange("p (q b t) -> p q b t", q=2, b=NB)
                decay(sd_dve, sd_act, D, 1)
                v.tensor_tensor(sm1[:, :, :], dt, gcol(egt, 1, 1), ALU.mult).then_inc(*sd_dve.did(l, "wdt"))
                dve.wait_ge(*sd_dve.at(l, "wdt"))
                dve.wait_ge(*sd_pe.at(l, "xtok"))
                v.tensor_tensor(bt(XW), bt(Q0[:, :, 0:T]), bcol(sm1[:, :, :]), ALU.mult).then_inc(*sd_dve.did(l, "xw"))
                dve.wait_ge(*sd_dve.at(l, "xw"))
                dve.wait_ge(*sd_pe.at(l, "cb"))
                v.tensor_tensor(AT, Q0[:, :, 0:T], D, ALU.mult).then_inc(*sd_dve.did(l, "att0"))
                dve.wait_ge(*sd_dve.at(l, "att0"))
                v.tensor_tensor(bt(AT), bt(AT), bcol(dt), ALU.mult).then_inc(*sd_dve.did(l, "att"))
                dve.wait_ge(*sd_dve.at(l, "att"))
                spread_s(XWX, XW).then_inc(*sd_dve.did(l, "xx"))
                dve.wait_ge(*sd_dve.at(l, "xx"))
                dve.wait_ge(out_sem, 16 * (13 * l + 4))
                v.memset(Sp[:, 0, :, :], 0.0).then_inc(*sd_dve.did(l, "zero"))
                dve.wait_ge(*sd_dve.at(l, "zero"))
                dve.wait_ge(*sd_act.at(l, "egrow"))
                EG = GR[1]
                for c in range(NPB):
                    state(c, sd_dve, sd_pe, end_col(EG), Q2, 128, 128)
                for q in range(2):
                    dve.wait_ge(*sd_pe.at(l, f"k_{q}"))
                    v.tensor_tensor(sts[:, q], sts[:, q], EG[:, q, SEQ + DS - 1::DS].unsqueeze(2).to_broadcast([128, NB, 128]), ALU.mult)\
                     .then_inc(*sd_dve.did(l, f"sd{q}"))
                    dve.wait_ge(*sd_dve.at(l, f"sd{q}"))
                    v.tensor_tensor(sts[:, q], sts[:, q], Q2[:, :, :].rearrange("p a (b n) -> p (a b) n", n=128), ALU.add)\
                     .then_inc(*sd_dve.did(l, f"ss{q}"))
                    dve.wait_ge(*sd_dve.at(l, f"ss{q}"))
                Y = tt(9)
                v.tensor_tensor(Y, Q1[:, :, 0:T], EG, ALU.mult).then_inc(*sd_dve.did(l, "y0"))
                dve.wait_ge(*sd_dve.at(l, "y0"))
                v.tensor_tensor(Y, Y, Q0[:, :, 0:T], ALU.add).then_inc(*sd_dve.did(l, "y1"))
                dve.wait_ge(*sd_dve.at(l, "y1"))
                for q in range(2):
                    last = v.scalar_tensor_tensor(out=Y[:, q, :], in0=C[:, q, :], scalar=pr(l, "ssd_d")[:, q:q + 1], in1=Y[:, q, :],
                                                  op0=ALU.mult, op1=ALU.add)
                last.then_inc(*sd_dve.did(l, "y2"))
                dve.wait_ge(*sd_dve.at(l, "y2"))
                v.tensor_tensor(Y, Y, sz, ALU.mult).then_inc(*sd_dve.did(l, "yz"))
                dve.wait_ge(*sd_dve.at(l, "yz"))
                dve.wait_ge(*sd_act.at(l, "root"))
                v.reciprocal(tt(8)[:, 0, :], tt(8)[:, 0, :]).then_inc(*sd_dve.did(l, "rn2"))
                dve.wait_ge(*sd_dve.at(l, "rn2"))
                for q in range(2):
                    last = v.scalar_tensor_tensor(out=BR[:, 2, q, :], in0=Y[:, q, :], scalar=pr(l, "snorm")[:, q:q + 1],
                                                  in1=tt(8)[:, 0, :], op0=ALU.mult, op1=ALU.mult)
                last.then_inc(*sd_dve.did(l, "br"))
                dve.wait_ge(*sd_dve.at(l, "br"))

                MR = tt(1)
                v.memset(mm[:, 0, :], 0.0).then_inc(*ml_dve.did(l, "m0"))
                dve.wait_ge(*ml_dve.at(l, "m0"))
                for c in range(NPB):
                    dve.wait_ge(*ml_dve.at(l, f"mm{c - 1}" if c else "m0"))
                    for q in range(2):
                        last = v.tensor_tensor_scan(MR[:, q, tk(c)], ONES[:, 0:BL], XROW[:, q, tk(c)], mm[:, c, q:q + 1], ALU.mult, ALU.max)
                    last.then_inc(*ml_dve.did(l, f"sc{c}"))
                    dve.wait_ge(*ml_dve.at(l, f"sc{c}"))
                    e0 = (c + 1) * BL - 1
                    v.tensor_tensor(mm[:, c + 1, :], MR[:, :, e0], GR[2][:, :, e0], ALU.add).then_inc(*ml_dve.did(l, f"mm{c}"))
                    dve.wait_ge(*ml_dve.at(l, f"mm{c}"))
                first = XROW[:, :, SEQ::DS]
                v.tensor_tensor(first, first, stmm[:, :, :], ALU.max).then_inc(*ml_dve.did(l, "inj"))
                dve.wait_ge(*ml_dve.at(l, "inj"))
                for q in range(2):
                    last = v.tensor_tensor_scan(MR[:, q, SEQ:T], RESET[:, :], XROW[:, q, SEQ:T], -3.0e38, ALU.add, ALU.max)
                last.then_inc(*ml_dve.did(l, "scs"))
                dve.wait_ge(*ml_dve.at(l, "scs"))
                ends = slice(SEQ + DS - 1, T, DS)
                v.tensor_tensor(mms[:, :, :], MR[:, :, ends], GR[2][:, :, ends], ALU.add).then_inc(*ml_dve.did(l, "mms"))
                dve.wait_ge(*ml_dve.at(l, "mms"))
                WT, QW, KWm, WIN, EMT = tt(2), tt(3), tt(4), tt(5), tt(6)
                v.tensor_tensor(xtk[:, :, :], smb[:, 3, :, :], gcol(gt, 0, 2), ALU.subtract).then_inc(*ml_dve.did(l, "xtk"))
                dve.wait_ge(*ml_dve.at(l, "xtk"))
                v.tensor_tensor(bt(WT), bcol(xtk[:, :, :]), bt(MR), ALU.subtract).then_inc(*ml_dve.did(l, "sub"))
                dve.wait_ge(*ml_dve.at(l, "sub"))
                v.tensor_scalar(WT, WT, 0.0, None, ALU.min).then_inc(*ml_dve.did(l, "min"))
                dve.wait_ge(*ml_dve.at(l, "min"))
                v.tensor_tensor(msel[:, :, :], MR[:, :, ends], BM.unsqueeze(1).to_broadcast([128, 2, NB]), ALU.mult).then_inc(*ml_dve.did(l, "selm"))
                dve.wait_ge(*ml_dve.at(l, "selm"))
                v.tensor_reduce(wend[:, :, NPB:NBLK], msel[:, :, :], AX.X, ALU.add).then_inc(*ml_dve.did(l, "sel"))
                dve.wait_ge(*ml_dve.at(l, "sel"))
                v.tensor_tensor(wend[:, :, 0:NPB], xtk[:, :, 0:NPB], MR[:, :, BL - 1:SEQ:BL], ALU.subtract)
                v.tensor_tensor(wend[:, :, NPB:], xtk[:, :, NPB:], wend[:, :, NPB:], ALU.subtract).then_inc(*ml_dve.did(l, "we0"))
                dve.wait_ge(*ml_dve.at(l, "we0"))
                v.tensor_tensor(bt(WIN)[:, :, 0:NPB, :], mm[:, 0:NPB, :].rearrange("p c q -> p q c").unsqueeze(3).to_broadcast([128, 2, NPB, BL]),
                                bt(MR)[:, :, 0:NPB, :], ALU.subtract)
                v.tensor_tensor(WIN[:, :, SEQ:T].rearrange("p q (b t) -> p q b t", b=NB), stmm[:, :, :].unsqueeze(3).to_broadcast([128, 2, NB, DS]),
                                MR[:, :, SEQ:T].rearrange("p q (b t) -> p q b t", b=NB), ALU.subtract).then_inc(*ml_dve.did(l, "wpre"))
                dve.wait_ge(*ml_dve.at(l, "wpre"))
                v.tensor_tensor(EMT, MR, GR[2], ALU.add).then_inc(*ml_dve.did(l, "mt"))
                dve.wait_ge(*ml_dve.at(l, "mt"))
                dve.wait_ge(*ml_act.at(l, "win"))
                v.tensor_tensor(QW, mlq, WIN, ALU.mult).then_inc(*ml_dve.did(l, "qw"))
                dve.wait_ge(*ml_dve.at(l, "qw"))
                dve.wait_ge(*ml_act.at(l, "wexp"))
                v.tensor_tensor(WT, WT, TRIM.unsqueeze(1).to_broadcast([128, 2, T]), ALU.mult).then_inc(*ml_dve.did(l, "wt0"))
                dve.wait_ge(*ml_dve.at(l, "wt0"))
                dve.wait_ge(*ml_pe.at(l, "kq"))
                v.tensor_tensor(WT, WT, Q2[:, :, 0:T], ALU.mult).then_inc(*ml_dve.did(l, "wt"))
                dve.wait_ge(*ml_dve.at(l, "wt"))
                dve.wait_ge(*ml_act.at(l, "wend"))
                v.tensor_tensor(bt(KWm), bt(Q1[:, :, 0:T]), bcol(wend[:, :, :]), ALU.mult).then_inc(*ml_dve.did(l, "kw"))
                dve.wait_ge(*ml_dve.at(l, "kw"))
                v.memset(nst[:, 0, :], 0.0).then_inc(*ml_dve.did(l, "kw0"))
                dve.wait_ge(*ml_dve.at(l, "kw0"))
                dve.wait_ge(out_sem, 16 * (13 * l + 6))
                v.memset(Sp[:, 0, :, 0:64], 0.0).then_inc(*ml_dve.did(l, "zero"))
                dve.wait_ge(*ml_dve.at(l, "zero"))
                for c in range(NPB):
                    state(c, ml_dve, ml_pe, end_col(WIN))
                dve.wait_ge(*ml_act.at(l, "vt"))
                spread_s(UX, tt(0)).then_inc(*ml_dve.did(l, "ux"))
                dve.wait_ge(*ml_dve.at(l, "ux"))
                sample_state(ml_dve, ml_pe, stm, WIN[:, :, ends])
                v.tensor_tensor(stn[:, :, :], stn[:, :, :], WIN[:, :, ends], ALU.mult).then_inc(*ml_dve.did(l, "sn0"))
                dve.wait_ge(*ml_dve.at(l, "sn0"))
                v.tensor_tensor(stn[:, :, :], stn[:, :, :], PJ[:, :, 0:NB], ALU.add).then_inc(*ml_dve.did(l, "ss"))
                dve.wait_ge(*ml_dve.at(l, "ss"))
                v.tensor_copy(tt(9), Q0[:, :, 0:T]).then_inc(*ml_dve.did(l, "o"))
                dve.wait_ge(*ml_dve.at(l, "o"))
                dve.wait_ge(*ml_act.at(l, "dab"))
                v.tensor_tensor(tt(7), tt(7), EMT, ALU.max).then_inc(*ml_dve.did(l, "dmx"))
                dve.wait_ge(*ml_dve.at(l, "dmx"))
                v.reciprocal(tt(7), tt(7)).then_inc(*ml_dve.did(l, "drc"))
                dve.wait_ge(*ml_dve.at(l, "drc"))
                v.tensor_tensor(tt(9), tt(9), tt(7), ALU.mult).then_inc(*ml_dve.did(l, "oo"))
                dve.wait_ge(*ml_dve.at(l, "oo"))
                norm_gate(ml_dve, ml_act, tt(9), tt(8), pr(l, "mnorm"), mlo, 3)
                dve.wait_ge(*ml_dve.at(l, "br"))

                def gated(g0, dst, first):
                    for t in range(KT):
                        dve.wait_ge(gat_act, 16 * g0 + 8 + t + 1)
                        if first:
                            v.tensor_tensor(dst[:, t, :], sgs[:, t % 4, :], prod[:, t, :], ALU.mult).then_inc(gat_dve, 1)
                        else:
                            v.tensor_tensor(sgs[:, t % 4, :], sgs[:, t % 4, :], prod[:, t, :], ALU.mult).then_inc(gat_mul, 1)
                            muls[0] += 1
                            dve.wait_ge(gat_mul, muls[0])
                            v.tensor_tensor(dst[:, t, :], dst[:, t, :], sgs[:, t % 4, :], ALU.add).then_inc(gat_dve, 1)

                for n in range(4):
                    gated(5 * l + n, merged, n == 0)
                for t in range(8):
                    dve.wait_ge(out_pe, 8 * l + t + 1)
                    last = v.tensor_tensor(h[:, t, :], h[:, t, :], PJ[:, t % 2, 0:T], ALU.add).then_inc(out_ev, 1)
                dve.wait_ge(out_ev, 8 * l + 8)
                dve.sem_inc(h_done, 1)
                norm(3 * l + 1)

                def swiglu(f0, e=None):
                    def val(c, per):
                        return c if e is None else e * per + c

                    for f in range(FT):
                        dve.wait_ge(ff_pe, val(f0 * 2 * FT + 2 * f + 2, 2 * FT))
                        dve.wait_ge(ff_act, val(f0 * FT + f + 1, FT))
                        if f == 0 and (f0 or e is not None):
                            dve.wait_ge(dn_pe, val(f0 * len(DOWN), len(DOWN)))
                        v.tensor_tensor(hid[:, f, :], ffs[:, f % 2, :], (Q0, Q1)[f % 2][:, 1, 0:T], ALU.mult).then_inc(ff_dve, 1)
                    for t in range(8):
                        s = t // 2
                        if t % 2 == 0:
                            last_d = max(d for d, x in enumerate(DOWN) if x[0] == s)
                            dve.wait_ge(dn_pe, val(f0 * len(DOWN) + last_d + 1, len(DOWN)))
                        src = (PJ, Q2)[s % 2][:, t % 2, 0:T]
                        if e is None:
                            v.tensor_tensor(h[:, t, :], h[:, t, :], src, ALU.add).then_inc(dn_dve, 1)
                        else:
                            v.tensor_tensor(ytmp[:, t % 2, :], src, crow[:, e, :], ALU.mult).then_inc(dn_mul, 1)
                            dve.wait_ge(dn_mul, val(t + 1, 8))
                            dve.wait_ge(dn_dve, val(8 * f0 + t, 8))
                            v.tensor_tensor(h[:, t, :], h[:, t, :], ytmp[:, t % 2, :], ALU.add).then_inc(dn_dve, 1)

                if l == 0:
                    swiglu(0)
                    dve.wait_ge(dn_dve, 8)
                else:
                    LG, MX, IX = rt[:, :, 0:8], rt[:, :, 8:16], rt[:, :, 16:24]
                    dve.wait_ge(*rt_pe.at(0, "logit"))
                    v.tensor_copy(rt[:, 0:2, 0:8], PJ[:, 0, 0:16].rearrange("p (t e) -> p t e", t=2))
                    v.tensor_copy(rt[0:64, 2, 0:8], PJ[0:64, 0, 16:24])
                    v.memset(rt[64:128, 2, 0:8], 0.0).then_inc(*rt_dve.did(0, "lg"))
                    dve.wait_ge(*rt_dve.at(0, "lg"))
                    for t in range(3):
                        last = v.max(MX[:, t, :], LG[:, t, :])
                    last.then_inc(*rt_dve.did(0, "max"))
                    dve.wait_ge(*rt_dve.at(0, "max"))
                    for t in range(3):
                        last = v.max_index(ridx[:, t, :], MX[:, t, :], LG[:, t, :])
                    last.then_inc(*rt_dve.did(0, "idx"))
                    dve.wait_ge(*rt_dve.at(0, "idx"))
                    v.tensor_copy(IX, ridx[:, :, :]).then_inc(*rt_dve.did(0, "idf"))
                    dve.wait_ge(*rt_dve.at(0, "idf"))
                    v.tensor_tensor(rt[:, :, 24:25], MX[:, :, 1:2], MX[:, :, 0:1], ALU.subtract).then_inc(*rt_dve.did(0, "d"))
                    dve.wait_ge(*rt_dve.at(0, "d"))
                    dve.wait_ge(*rt_act.at(0, "e"))
                    v.tensor_scalar(rt[:, :, 25:26], rt[:, :, 24:25], 1.0, None, ALU.add).then_inc(*rt_dve.did(0, "s"))
                    dve.wait_ge(*rt_dve.at(0, "s"))
                    v.reciprocal(rt[:, :, 26:27], rt[:, :, 25:26]).then_inc(*rt_dve.did(0, "r"))
                    dve.wait_ge(*rt_dve.at(0, "r"))
                    v.tensor_tensor(rt[:, :, 27:28], rt[:, :, 24:25], rt[:, :, 26:27], ALU.mult).then_inc(*rt_dve.did(0, "w2"))
                    dve.wait_ge(*rt_dve.at(0, "w2"))
                    for c in range(2):
                        v.tensor_tensor(rt[:, :, 40 + 8 * c:48 + 8 * c], IOTA.unsqueeze(1).to_broadcast([128, 3, 8]),
                                        IX[:, :, c:c + 1].to_broadcast([128, 3, 8]), ALU.is_equal).then_inc(*rt_dve.did(0, f"oh{c}"))
                        dve.wait_ge(*rt_dve.at(0, f"oh{c}"))
                    v.tensor_tensor(rt[:, :, 40:48], rt[:, :, 40:48], rt[:, :, 26:27].to_broadcast([128, 3, 8]), ALU.mult)
                    v.tensor_tensor(rt[:, :, 48:56], rt[:, :, 48:56], rt[:, :, 27:28].to_broadcast([128, 3, 8]), ALU.mult)\
                     .then_inc(*rt_dve.did(0, "oh2"))
                    dve.wait_ge(*rt_dve.at(0, "oh2"))
                    v.tensor_tensor(rt[:, :, 56:64], rt[:, :, 40:48], rt[:, :, 48:56], ALU.add).then_inc(*rt_dve.did(0, "comb"))
                    dve.wait_ge(*rt_dve.at(0, "comb"))
                    for half in range(2):
                        dve.wait_ge(*rt_pe.at(0, f"crow{half}"))
                        v.tensor_copy(crow[:, 4 * half:4 * half + 2, :], Q0[:, :, 0:T])
                        v.tensor_copy(crow[:, 4 * half + 2:4 * half + 4, :], Q1[:, :, 0:T]).then_inc(*rt_dve.did(0, f"crow{half}"))
                        dve.wait_ge(*rt_dve.at(0, f"crow{half}"))
                    dve.wait_ge(*rt_dve.at(0, "crow1"))
                    with dve.Fori(0, NE) as e:
                        swiglu(1, e)
                    dve.wait_ge(dn_dve, 8 * (1 + NE))
                dve.sem_inc(h_done, 1)
                norm(3 * l + 2)
                gated(5 * l + 4, h, False)
                dve.wait_ge(gat_dve, 8 * (5 * l + 5))
                dve.sem_inc(h_done, 1)
            norm(N_NORM - 1)



_INS = ["xT", "pT", "cst", "par", "slabs", "wsm", "wr", "st_conv", "st_gdn", "st_hg", "st_ssd", "st_mlc", "st_mln", "st_mlm"]
_OUTS = [("y", (KT, 128, T)), ("conv", (DEPTH, 128, 2, 6, 1 + NB, 3)),
         ("gdn_p", (DEPTH, 128, 2, 64)), ("gdn_s", (DEPTH, 128, 2, NB, 64)),
         ("hg_p", (DEPTH, 128, 2, 64)), ("hg_s", (DEPTH, 128, 2, NB, 64)),
         ("ssd_p", (DEPTH, 128, 2, 128)), ("ssd_s", (DEPTH, 128, 2, NB, 128)),
         ("mlc_p", (DEPTH, 128, 2, 64)), ("mlc_s", (DEPTH, 128, 2, NB, 64)),
         ("mln_p", (DEPTH, 128, 2)), ("mln_s", (DEPTH, 128, 2, NB)),
         ("mlm_p", (DEPTH, 128, 2)), ("mlm_s", (DEPTH, 128, 2, NB))]


def constants():
    out = np.zeros((128, N_CST), np.float32)

    def put(name, a):
        o, w = CST[name]
        out[:, o:o + w] = np.broadcast_to(a.reshape(a.shape[0], -1), (128, w))

    s, t = np.arange(64)[:, None], np.arange(64)[None, :]
    E, LM, TRI = np.zeros((2, 8, 64, 64)), np.zeros((2, 7, 64, 64)), np.zeros((2, 64, 64))
    for k in range(2):
        same = np.ones((64, 64), bool) if k == 0 else (s // DS == t // DS)
        TRI[k] = (s <= t) & same
        E[k, 6], E[k, 7] = TRI[k], (s > t) & same
        for j in range(6 if k == 0 else 3):
            w = 2 ** j
            base = t // (2 * w) * (2 * w) + w
            right = t >= base
            E[k, j] = np.where(right, (s >= base) & (s <= t), (s > t) & (s < base))
            LM[k, j] = (s // (2 * w) == t // (2 * w)) & (s % (2 * w) < w) & (t % (2 * w) >= w)
        LM[k, 6] = s == t
    put("E", np.tile(E.transpose(2, 0, 1, 3), (2, 1, 1, 1)))
    put("LM", np.tile(LM.transpose(2, 0, 1, 3), (2, 1, 1, 1)))
    put("TRIM", np.tile(np.concatenate([TRI[0]] * NPB + [TRI[1]], axis=1), (2, 1)))
    put("ID", np.eye(128))
    put("BLK", np.kron(np.eye(2), np.ones((64, 64))))
    put("ONES", np.ones((128, 128)))
    put("BT", np.array([[t[0] // DS == b for b in range(NB)]]).astype(np.float32))
    put("BM", np.tile((s // DS == np.arange(NB)[None, :]), (2, 1)))
    put("RESET", np.where(t % DS == 0, -3.0e38, 0.0))
    put("IOTA", np.arange(8)[None, :])
    put("EPS", np.array([[EPS, 64 * EPS]]))
    return out


def lanes(a):
    a = a.reshape(a.shape[:-1] + (2, 2))
    return np.repeat(np.moveaxis(a, -1, 0), 64, axis=0)


def parameters(w, l):
    out = np.zeros((128, N_PAR), np.float32)

    def put(name, a):
        o, n = PAR[name]
        out[:, o:o + n] = a.reshape(128, n)

    for name, src in (("g_mix", w["g_mix"][l]), ("g_ffn", w["g_ffn"][l]), ("g_ple", w["g_ple"][l]), ("g_final", w["g_final"])):
        put(name, src.reshape(KT, 128).T)
    put("gcw", w["gdn_conv_w"][l].reshape(4, 6, 128).transpose(2, 1, 0))
    put("scw", w["ssd_conv_w"][l].reshape(4, 6, 128).transpose(2, 1, 0))
    put("scb", w["ssd_conv_b"][l].reshape(6, 128).T)
    for name, src in (("gnorm", "gdn_norm"), ("hnorm", "hgrn_norm"), ("mnorm", "ml_norm")):
        put(name, np.tile(w[src][l], 2))
    put("snorm", w["ssd_norm"][l].reshape(2, 128).T)
    put("ssd_d", lanes(w["ssd_d"][l]))
    z = np.zeros(4, np.float32)
    put("gb", lanes(np.stack([z, w["gdn_dt_bias"][l], w["ssd_dt_bias"][l], w["ml_ig_b"][l], w["ml_fg_b"][l]])))
    put("alog", lanes(np.stack([w["gdn_a_log"][l], w["ssd_a_log"][l]])))
    put("lb", w["hgrn_lb"].reshape(DEPTH, 2, 128).transpose(2, 0, 1))
    return out


def cut(slabs, n, w):
    k = w.shape[0] // 128
    for c in range(w.shape[1] // 256):
        slabs[n + c].reshape(128, 8, 256)[:, 0:k] = w[:, c * 256:(c + 1) * 256].reshape(k, 128, 256).transpose(1, 0, 2)
    return n + w.shape[1] // 256


def cut_rows(slabs, n, w):
    slabs[n].reshape(128, 2, 1024)[:] = w.reshape(2, 128, 1024).transpose(1, 0, 2)
    return n + 1


def cut_ff(slabs, n, wg, wu, wd):
    for c in range(FF // 256):
        n = cut(slabs, n, wg[:, c * 256:(c + 1) * 256])
        n = cut(slabs, n, wu[:, c * 256:(c + 1) * 256])
    for s, k0, k1 in DOWN:
        n = cut(slabs, n, wd[k0 * 128:k1 * 128, s * 256:(s + 1) * 256])
    return n


def kernel(**inputs):
    import concourse.bacc as _bacc
    from concourse.bass_utils import run_bass_kernel_spmd as _run

    w = {k: np.asarray(a) for k, a in inputs.items()}
    per = [N_PROJ + N_GATED + N_OUT + n * N_FF + 5 for n in (1, NE)]
    slabs = np.zeros((sum(per), 128, SLAB), np.float32)
    starts = {"gdn_in0": 0, "gdn_in1": 256, "gdn_in2": 512, "gdn_z": 776, "hg_q": 1032, "hg_f": 1288, "hg_v": 1544,
              "hg_g": 1800, "ssd_z": 2056, "ssd_in0": 2312, "ssd_in1": 2568, "ssd_in2": 2824, "ml_qk": 3084,
              "ml_v": 3340, "ml_o": 3604}
    n = 0
    for l in range(DEPTH):
        wi = w["w_in"][l]
        for name in PROJ:
            n = cut(slabs, n, wi[:, starts[name]:starts[name] + 256])
        for b in range(4):
            n = cut_rows(slabs, n, w["w_branch"][l, b])
            n = cut(slabs, n, wi[:, 3860 + b * DM:3860 + (b + 1) * DM])
        n = cut(slabs, n, w["w_out"][l])
        if l % 2 == 0:
            n = cut_ff(slabs, n, w["w_ff_gate"][0], w["w_ff_up"][0], w["w_ff_down"][0])
        else:
            for e in range(NE):
                n = cut_ff(slabs, n, w["w_ex_gate"][0, e], w["w_ex_up"][0, e], w["w_ex_down"][0, e])
        n = cut_rows(slabs, n, w["w_ple"][l])
        n = cut(slabs, n, w["w_ple_gate"][l])
    assert n == len(slabs)

    def tokens(p, s):
        return np.concatenate([p.reshape(SEQ, -1), s.reshape(NB * DS, -1)]).T

    small = np.concatenate([w["w_in"][:, :, 768:776], w["w_in"][:, :, 3080:3084], w["w_in"][:, :, 3596:3604]], axis=2)
    conv = np.stack([w["state_gdn_conv"], w["state_ssd_conv"]], axis=1)

    def heads(a):
        L, B, H, K, V = a.shape
        return a.reshape(L, B, 2, 2, K, V).transpose(0, 3, 4, 2, 1, 5).reshape(L, 2 * K, 2, B, V)

    mlc = np.zeros((DEPTH, NB, 4, 64, 64), np.float32)
    mlc[:, :, :, 0:32] = w["state_mlstm_c"]
    mln = np.zeros((DEPTH, NB, 4, 64, 1), np.float32)
    mln[:, :, :, 0:32, 0] = w["state_mlstm_n"]
    arrays = {
        "xT": tokens(w["x_prompt"], w["x_sample"]).reshape(KT, 128, T),
        "pT": np.stack([tokens(w["p_prompt"][l], w["p_sample"][l]).reshape(2, 128, T).transpose(1, 0, 2) for l in range(DEPTH)]),
        "cst": constants(),
        "par": np.stack([parameters(w, l) for l in range(DEPTH)]),
        "slabs": slabs,
        "wsm": small.reshape(DEPTH, KT, 128, 20).transpose(0, 2, 1, 3),
        "wr": w["w_router"][0].reshape(KT, 128, NE).transpose(1, 0, 2),
        "st_conv": conv.reshape(DEPTH, 2, NB, 3, 6, 128).transpose(0, 5, 1, 4, 2, 3),
        "st_gdn": heads(w["state_gdn"]), "st_hg": heads(w["state_hgrn"]), "st_ssd": heads(w["state_ssd"]),
        "st_mlc": heads(mlc), "st_mln": heads(mln)[..., 0],
        "st_mlm": np.stack([lanes(w["state_mlstm_m"][l]).transpose(0, 2, 1) for l in range(DEPTH)]),
    }
    arrays = {f"in_{k}_dram": np.ascontiguousarray(a) for k, a in arrays.items()}
    nc = _bacc.Bacc("TRN2", target_bir_lowering=False, num_devices=1)
    args = [nc.dram_tensor(f"in_{k}_dram", arrays[f"in_{k}_dram"].shape, F32, kind="ExternalInput").ap() for k in _INS]
    args += [nc.dram_tensor(f"out_{k}_dram", shape, F32, kind="ExternalOutput").ap() for k, shape in _OUTS]
    trunk_kernel(nc, *args)
    r = _run(nc, [arrays], core_ids=[0])
    o = {k: np.asarray(r.results[0][f"out_{k}_dram"]).reshape(shape) for k, shape in _OUTS}

    y = o["y"].reshape(DM, T).T
    cv = o["conv"].transpose(0, 2, 4, 5, 3, 1).reshape(DEPTH, 2, 1 + NB, 3, 768)

    def back(a, k=64):
        L, _, _, B, V = a.shape
        return np.ascontiguousarray(a.reshape(L, 2, 64, 2, B, V).transpose(0, 4, 3, 1, 2, 5).reshape(L, B, 4, 64, V)[:, :, :, 0:k])

    def states(sfx):
        one = (lambda a: a[:, :, :, None]) if sfx == "p" else (lambda a: a)
        c = cv[:, :, 0:1] if sfx == "p" else cv[:, :, 1:]
        m = one(o["mlm_" + sfx])
        return (np.ascontiguousarray(c[:, 0]), back(one(o["gdn_" + sfx])), back(one(o["hg_" + sfx])), np.ascontiguousarray(c[:, 1]),
                back(one(o["ssd_" + sfx])), back(one(o["mlc_" + sfx]), 32), back(one(o["mln_" + sfx])[..., None], 32)[..., 0],
                np.ascontiguousarray(m.reshape(DEPTH, 2, 64, 2, -1)[:, :, 0].transpose(0, 3, 2, 1).reshape(DEPTH, -1, 4)))

    return (np.ascontiguousarray(y[0:SEQ]).reshape(1, SEQ, DM), np.ascontiguousarray(y[SEQ:]).reshape(NB, DS, DM),
            *states("p"), *states("s"))
```

```python
from contextlib import ExitStack

import numpy as np

import concourse.bass as bass
from concourse import mybir

F32 = mybir.dt.float32
U32 = mybir.dt.uint32
ALU = mybir.AluOpType
ACT = mybir.ActivationFunctionType
AX = mybir.AxisListType

DM, SEQ, NB, DS, DEPTH = 1024, 256, 8, 8, 2
T = SEQ + NB * DS
KT = DM // 128
FF = ((8 * DM // 3 + 255) // 256) * 256
FT = FF // 128
NE = 8
BL = 64
NBLK = T // BL
NPB = SEQ // BL
EPS = 1e-6
R = 5
SLAB = 8 * 256
XPW = 3 + SEQ + NB * (3 + DS)

PROJ = ["gdn_in0", "gdn_in1", "gdn_in2", "ml_qk", "hg_q", "hg_v", "ml_v", "gdn_z", "hg_g", "ssd_z",
        "hg_f", "ml_o", "ssd_in0", "ssd_in1", "ssd_in2"]
N_PROJ = len(PROJ)
N_GATED = 4 * 5
N_OUT = 4
DOWN = [(0, 0, 8), (0, 8, 15), (0, 15, 22), (1, 0, 8), (1, 8, 15), (1, 15, 22), (2, 0, 8), (2, 8, 15), (2, 15, 22),
        (3, 0, 6), (3, 6, 12), (3, 12, 17), (3, 17, 22)]
N_FF = 2 * (FF // 256) + len(DOWN)
CH = FF // 256
N_X = 2 * CH + FT // 2
N_SKIP = -N_X % R
N_XV = N_X + N_SKIP
CAP = 128
GROUPS = -(-T // CAP)
TT = [(0, 128), (128, 256), (256, T)]

CST = {}
for _n, _w in (("E", 2 * 8 * 64), ("LM", 2 * 7 * 64), ("TRIM", T), ("ID", 128), ("BLK", 128), ("ONES", 128),
               ("BT", NB * 64), ("BM", NB), ("RESET", 64), ("IOTA", 128), ("EPS", 2), ("STR", 128)):
    CST[_n] = (sum(w for _, w in CST.values()), _w)
N_CST = sum(w for _, w in CST.values())
PAR = {}
for _n, _w in (("g_mix", 8), ("g_ffn", 8), ("g_ple", 8), ("g_final", 8), ("gcw", 24), ("gcb", 6), ("scw", 24),
               ("scb", 6), ("gnorm", 1), ("hnorm", 1), ("mnorm", 1), ("snorm", 2), ("ssd_d", 2), ("gb", 10),
               ("alog", 4), ("lb", 4)):
    PAR[_n] = (sum(w for _, w in PAR.values()), _w)
N_PAR = sum(w for _, w in PAR.values())


class Steps:

    def __init__(self, sem, names):
        self.sem, self.names, self.count = sem, names.split(), 0

    def at(self, rnd, name):
        return self.sem, rnd * len(self.names) + self.names.index(name) + 1

    def did(self, rnd, name):
        self.count += 1
        assert self.at(rnd, name)[1] == self.count, (name, self.count)
        return self.sem, 1


def trunk_kernel(nc, xT, pT, cst_d, par_d, slabs, xslabs, wsm_d, wr_d, st_conv, st_gdn, st_hg, st_ssd, st_mlc, st_mln, st_mlm,
                 y_d, o_conv, o_gdn_p, o_gdn_s, o_hg_p, o_hg_s, o_ssd_p, o_ssd_s, o_mlc_p, o_mlc_s,
                 o_mln_p, o_mln_s, o_mlm_p, o_mlm_s):
    ctx = ExitStack()
    with ctx:
        def sb(name, shape, dt=F32):
            return ctx.enter_context(nc.sbuf_tensor(name, shape, dt))

        def sem(name):
            return ctx.enter_context(nc.semaphore(name))

        PJ, Q0, Q1, Q2 = [ctx.enter_context(nc.psum_tensor(n, [128, 2, 512], F32)) for n in ("PJ", "Q0", "Q1", "Q2")]

        ring = sb("ring", [128, R, SLAB])
        cst = sb("cst", [128, N_CST])
        par = sb("par", [128, DEPTH, N_PAR])
        h = sb("h", [128, KT, T])
        u = sb("u", [128, KT, T])
        BR = sb("BR", [128, 4, 2, T])
        wsm = sb("wsm", [128, KT, 20])
        wr = sb("wr", [128, KT, NE])
        NT = 640
        N_MIX = 11 * NT + 6 * XPW + 12 * T + 4 * NT + 13 * NT
        mix = sb("mix", [128, N_MIX])
        stg = sb("stg", [128, 2, NB, 64])
        sth = sb("sth", [128, 2, NB, 64])
        sts = sb("sts", [128, 2, NB, 128])
        stm = sb("stm", [128, 2, NB, 64])
        stn = sb("stn", [128, 2, NB])
        stmm = sb("stmm", [128, 2, NB])
        sconv = sb("sconv", [128, 2, 6, NB, 3])
        cs = sb("cs", [128, 2, 6, 1 + NB, 3])
        rstd = sb("rstd", [128, T])
        Sp = sb("Sp", [128, 2, 2, 128])
        nst = sb("nst", [128, 2, 2])
        mm = sb("mm", [128, NPB + 1, 2])
        mms = sb("mms", [128, 2, NB])
        smb = sb("smb", [128, 5, 2, NBLK])
        beta = sb("beta", [128, 2, NBLK])
        sp3 = sb("sp3", [128, 6, 3 * 2 * NBLK])
        cf = sb("cf", [128, 3, 2])
        G = sb("G", [128, NBLK, 6])
        gt = sb("gt", [128, 2, NBLK, 6])
        egt = sb("egt", [128, 2, NBLK, 6])
        sm1 = sb("sm1", [128, 2, NBLK])
        xtk = sb("xtk", [128, 2, NBLK])
        wend = sb("wend", [128, 2, NBLK])
        msel = sb("msel", [128, 2, NB])
        egc = sb("egc", [128, 2, NPB + NB])
        lbt = sb("lbt", [128, 8, 2])
        lbv = sb("lbv", [128, DEPTH, 2, 2])
        rt = sb("rt", [128, 3, 64])
        ridx = sb("ridx", [128, 3, 8], U32)

        at = [0]

        def part(n):
            a = mix[:, at[0]:at[0] + n]
            at[0] += n
            return a

        def pairs(a):
            return a.rearrange("p (q t) -> p q t", q=2)

        hgq, hgv, mlq, mlk, mlv, gz, hgg, sz, sf, sfn, mlo = [pairs(part(NT)) for _ in range(11)]
        XP = part(6 * XPW).rearrange("p (c t) -> p c t", c=6)
        C6 = [part(6 * T).rearrange("p (c t) -> p c t", c=6) for _ in range(2)]
        GR = [pairs(part(NT)) for _ in range(3)]
        XROW = pairs(part(NT))
        scr = part(13 * NT)

        def sl(i, n=1):
            return scr[:, i * NT:(i + n) * NT]

        def tt(i):
            return pairs(sl(i))

        def c_(name):
            o, w = CST[name]
            return cst[:, o:o + w]

        E = c_("E").rearrange("p (k j t) -> p k j t", k=2, j=8)
        LM = c_("LM").rearrange("p (k j t) -> p k j t", k=2, j=7)
        TRIM, ID, BLK, ONES = c_("TRIM"), c_("ID"), c_("BLK"), c_("ONES")
        BT = c_("BT").rearrange("p (b t) -> p b t", b=NB)
        BM, RESET, IOTA, EPSC, STR = c_("BM"), c_("RESET"), c_("IOTA"), c_("EPS"), c_("STR")

        def pr(l, name):
            o, w = PAR[name]
            return par[:, l, o:o + w]

        LN = (slice(0, 64), slice(64, 128))

        def kind(blk):
            return 0 if blk < NPB else 1

        def tk(blk):
            return slice(blk * BL, (blk + 1) * BL)

        def units(blks=range(NBLK)):
            return [(b, q, i) for b in blks for q in range(2) for i in range(2)]

        def bt(a):
            return a.rearrange("p q (b t) -> p q b t", t=BL)

        def bcol(a):
            return a.unsqueeze(3).to_broadcast([128, 2, NBLK, BL])

        def gcol(t, w, m):
            return t[:, w, :, 2 * m:2 * m + 2].rearrange("p b q -> p q b")

        slab_in = [sem(f"slab_in{i}") for i in range(R)]
        slab_done = sem("slab_done")
        consts_in, layer_in, ple_in, out_sem = sem("consts_in"), sem("layer_in"), sem("ple_in"), sem("out_sem")
        h_done = sem("h_done")
        N_NORM = 3 * DEPTH + 1
        norm_act = Steps(sem("norm_act"), "sq root")
        norm_pe = Steps(sem("norm_pe"), "ss")
        norm_dve = Steps(sem("norm_dve"), "rstd u")
        setup_dve = Steps(sem("setup_dve"), "max sub sum rcp sm lb one")
        setup_act = Steps(sem("setup_act"), "exp")
        proj_pe, proj_ev = sem("proj_pe"), sem("proj_ev")
        halo, conv_tap, conv_silu, conv_new = sem("halo"), sem("conv_tap"), sem("conv_silu"), sem("conv_new")
        gp_pe = Steps(sem("gp_pe"), "small gam gr0 gr1 gr2 ig")
        gp_act = Steps(sem("gp_act"), "beta ea abs e ln egt gr0 gr1 gr2")
        gp_dve = Steps(sem("gp_dve"), "smb spc spi u1 d z dz lz rd le lp sp cf G gt xrow")
        gd_pe = Steps(sem("gd_pe"), "l2 ktok vtok kk qk " + " ".join(f"w{j} tu{j}" for j in range(6)) + " skt sv "
                      + " ".join(f"p{c} o{c} k{c}" for c in range(NPB)) + " ps os ks nss")
        gd_act = Steps(sem("gd_act"), "sq rootq rootk dexp egrow skt osq root")
        gd_dve = Steps(sem("gd_dve"), "rn qk dsub dmin D bg kb kw vb lt qkd init qe " + " ".join(
            f"al{j} wb{j} t{j} u{j}" for j in range(6)) + " sv zero " + " ".join(f"u{c}_ s{c}" for c in range(NPB))
            + " sx us ux sd ss o rn2 on br")
        hg_pe = Steps(sem("hg_pe"), "lftok vtok " + "x0 " + " ".join(f"x{i + 1} a{i}" for i in range(9)) + " a9 kw "
                      + " ".join(f"o{c} k{c}" for c in range(NPB)) + " os ks nss")
        hg_act = Steps(sem("hg_act"), "lf lft vt " + " ".join(f"x{i} e{i}" for i in range(10)) + " kw osq root")
        hg_dve = Steps(sem("hg_dve"), "pre kin " + "z0 " + " ".join(f"z{i + 1} m{i} r{i}" for i in range(9)) + " m9 r9" + " zero "
                       + " ".join(f"s{c}" for c in range(NPB)) + " ux sd ss o rn2 on br")
        sd_pe = Steps(sem("sd_pe"), "xtok btok cb " + " ".join(f"t{c} y{c} k{c}" for c in range(NPB))
                      + " t_0 y_0 k_0 t_1 y_1 k_1 nss")
        sd_act = Steps(sem("sd_act"), "dexp egrow xt btp bts " + " ".join(f"t{c}" for c in range(NPB)) + " t_0 t_1 osq root")
        sd_dve = Steps(sem("sd_dve"), "dsub dmin D wdt xw att0 att xx zero " + " ".join(f"s{c}" for c in range(NPB))
                       + " sd0 ss0 sd1 ss1 y0 y1 y2 yz rn2 br")
        ml_pe = Steps(sem("ml_pe"), "vtok ktok kq " + " ".join(f"o{c} k{c}" for c in range(NPB)) + " os ks nss")
        ml_act = Steps(sem("ml_act"), "vt wexp win wend emt dab osq root")
        ml_dve = Steps(sem("ml_dve"), "m0 " + " ".join(f"sc{c} mm{c}" for c in range(NPB))
                       + " inj scs mms xtk sub min selm sel we0 wpre mt qw wt0 wt kw kw0 zero "
                       + " ".join(f"s{c}" for c in range(NPB)) + " ux sd sn0 ss o dmx drc oo rn2 on br")
        gat_pe = sem("gat_pe")
        gat_act, gat_dve = sem("gat_act"), sem("gat_dve")
        out_pe = sem("out_pe")
        out_ev = sem("out_ev")
        ff_act, ff_dve = sem("ff_act"), sem("ff_dve")
        gat_mul = sem("gat_mul")
        pads = Steps(sem("pads"), "zero")
        dn_dve = sem("dn_dve")
        rt_pe = Steps(sem("rt_pe"), "utok logit rank")
        rt_dve = Steps(sem("rt_dve"), "lg max idx idf d s r w2 oh0 oh1 M ohw comb rk0 rk1 RK cnt flag")
        rt_act = Steps(sem("rt_act"), "utok0 utok1 utok2 e")

        def xpart(n, _a=[0]):
            a = mix[:, _a[0]:_a[0] + n]
            _a[0] += n
            assert _a[0] <= 11 * NT + 6 * XPW + 12 * T + 4 * NT
            return a

        hidx = xpart(FT * CAP).rearrange("p (f t) -> p f t", f=FT)
        utok = xpart(3 * DM).rearrange("p (t c) -> p t c", t=3)
        xg = xpart(KT * CAP).rearrange("p (k t) -> p k t", k=KT)
        sgx = xpart(4 * CAP).rearrange("p (r t) -> p r t", r=2)
        sel = xpart(3 * CAP).rearrange("p (t c) -> p t c", t=3)
        selw = xpart(3 * CAP).rearrange("p (t c) -> p t c", t=3)
        selt = xpart(T)
        yg = xpart(DM)
        RK = xpart(3 * NE * (GROUPS + 1)).rearrange("p (t c) -> p t c", t=3)
        CB = xpart(3 * NE * (GROUPS + 1)).rearrange("p (t c) -> p t c", t=3)
        flag = sb("flag", [128, 1], mybir.dt.int32)
        X_NAMES = ("selw", "sel", "selt_pe", "selt", "xg_pe", "xg", "silu", "hid", "yg", "scat", "hadd")
        main = {n: sem("x_" + n) for n in X_NAMES}
        over = {n: sem("o_" + n) for n in X_NAMES}
        over["slab_in"] = [sem(f"o_slab_in{i}") for i in range(R)]
        over["slab_done"] = sem("o_slab_done")
        main["slab_in"], main["slab_done"] = slab_in, slab_done

        hid = mix[:, 0:FT * T].rearrange("p (f t) -> p f t", f=FT)
        ffs = mix[:, FT * T:(FT + 4) * T].rearrange("p (r f t) -> p r f t", r=2, f=2)
        merged = scr[:, 0:KT * T].rearrange("p (k t) -> p k t", k=KT)
        prod = scr[:, KT * T:2 * KT * T].rearrange("p (k t) -> p k t", k=KT)
        sgs = scr[:, 2 * KT * T:(2 * KT + 4) * T].rearrange("p (k t) -> p k t", k=4)
        pt = pairs(scr[:, 11 * NT:12 * NT])
        assert (2 * KT + 4) * T <= 11 * NT
        sqh = scr[:, KT * T:2 * KT * T].rearrange("p (k t) -> p k t", k=KT)

        PER_LAYER = [N_PROJ + N_GATED + N_OUT + n + 5 for n in (N_FF, NE * N_XV)]
        BASE = [0, PER_LAYER[0]]
        TOTAL = sum(PER_LAYER)
        dst_sections = [2, 2]
        N_OUTS = [0]

        def slab(n):
            return ring[:, n % R, :].rearrange("p (k c) -> p k c", k=8)

        def slab2(n):
            return ring[:, n % R, :].rearrange("p (k c) -> p k c", k=2)

        slab_x = slab

        block = ctx.enter_context(nc.Block())

        @block.sync
        def _(sp):
            def load(n, src):
                if n >= R:
                    sp.wait_ge(slab_done, n - R + 1)
                sp.dma_start(ring[:, n % R, :], src).then_inc(slab_in[n % R], 16)

            def load_expert(e, n0, loaded, done, i0):
                for i in range(N_X):
                    n = n0 + i
                    if n >= R or i0:
                        sp.wait_ge(done, e * N_XV + (n - R + 1))
                    src = xslabs[bass.ds(e * N_X + i, 1), :, :].rearrange("a p c -> (a p) c")
                    sp.dma_start(ring[:, n % R, :], src).then_inc(loaded[n % R], 16)

            pre = N_PROJ + N_GATED + N_OUT
            for n in range(BASE[1] + pre):
                load(n, slabs[n])
            first = BASE[1] + pre
            with sp.Fori(0, NE) as e:
                load_expert(e, first, slab_in, slab_done, 1)
            last = first + NE * N_XV
            sp.wait_ge(*rt_dve.at(0, "flag"))
            with sp.If(sp.value_load(flag[0:1, 0:1], min_val=0, max_val=1)):
                sp.wait_ge(slab_done, last)
                for g in range(1, GROUPS):
                    with sp.Fori(0, NE) as e:
                        load_expert(e, NE * N_XV * (g - 1) + R, over["slab_in"], over["slab_done"], 1)
                sp.wait_ge(over["slab_done"], (GROUPS - 1) * NE * N_XV + R)
            for n in range(last, TOTAL):
                load(n, slabs[n - NE * N_XV])

        @block.gpsimd
        def _(pool):
            for k in range(KT):
                pool.dma_start(h[:, k, :], xT[k]).then_inc(consts_in, 16)
            pool.dma_start(cst[:], cst_d).then_inc(consts_in, 16)
            pool.dma_start(par[:], par_d.rearrange("l p c -> p l c")).then_inc(consts_in, 16)
            pool.dma_start(wr[:], wr_d).then_inc(consts_in, 16)
            for l in range(DEPTH):
                if l:
                    pool.wait_ge(h_done, 3 * l)
                    pool.wait_ge(out_sem, 16 * N_OUTS[0])
                pool.dma_start(wsm[:], wsm_d[l]).then_inc(layer_in, 16)
                pool.dma_start(sconv[:], st_conv[l]).then_inc(layer_in, 16)
                pool.dma_start(stg[:], st_gdn[l]).then_inc(layer_in, 16)
                pool.dma_start(sth[:], st_hg[l]).then_inc(layer_in, 16)
                pool.dma_start(sts[:], st_ssd[l]).then_inc(layer_in, 16)
                pool.dma_start(stm[:], st_mlc[l]).then_inc(layer_in, 16)
                pool.dma_start(stn[:], st_mln[l]).then_inc(layer_in, 16)
                pool.dma_start(stmm[:], st_mlm[l]).then_inc(layer_in, 16)

                def store(dst, src):
                    N_OUTS[0] += 1
                    pool.dma_start(dst, src).then_inc(out_sem, 16)

                pool.wait_ge(*gd_dve.at(l, f"s{NPB - 1}"))
                store(o_gdn_p[l], Sp[:, NPB % 2, :, 0:64])
                pool.wait_ge(*gd_dve.at(l, "ss"))
                store(o_gdn_s[l], stg[:])
                pool.wait_ge(*hg_dve.at(l, f"s{NPB - 1}"))
                store(o_hg_p[l], Sp[:, NPB % 2, :, 0:64])
                pool.wait_ge(*hg_dve.at(l, "ss"))
                store(o_hg_s[l], sth[:])
                pool.wait_ge(*sd_dve.at(l, f"s{NPB - 1}"))
                store(o_ssd_p[l], Sp[:, NPB % 2, :, :])
                pool.wait_ge(*sd_dve.at(l, "ss1"))
                store(o_ssd_s[l], sts[:])
                pool.wait_ge(*ml_dve.at(l, f"s{NPB - 1}"))
                store(o_mlc_p[l], Sp[:, NPB % 2, :, 0:64])
                store(o_mln_p[l], nst[:, NPB % 2, :])
                store(o_mlm_p[l], mm[:, NPB, :])
                pool.wait_ge(*ml_dve.at(l, "ss"))
                store(o_mlc_s[l], stm[:])
                store(o_mln_s[l], stn[:])
                store(o_mlm_s[l], mms[:])
                pool.wait_ge(conv_new, 4 * (l + 1))
                store(o_conv[l], cs[:])
                pool.wait_ge(*ml_dve.at(l, "br"))
                pool.dma_start(pt, pT[l]).then_inc(ple_in, 16)
            pool.wait_ge(*norm_dve.at(N_NORM - 1, "u"))
            for k in range(KT):
                pool.dma_start(y_d[k], u[:, k, :]).then_inc(out_sem, 16)
                N_OUTS[0] += 1
            pool.wait_ge(out_sem, 16 * N_OUTS[0])

        N_CONSTS = 16 * (KT + 3)
        PER_L_IN = 16 * 8

        @block.tensor
        def _(pe):
            mmul = nc.tensor.matmul

            first_x = BASE[1] + N_PROJ + N_GATED + N_OUT

            def take(n):
                skipped = NE if n > first_x and (n - first_x) % R >= R - N_SKIP else 0
                pe.wait_ge(slab_in[n % R], 16 * (n // R + 1 - skipped))

            def norm(k):
                pe.wait_ge(*norm_act.at(k, "sq"))
                if k == 0:
                    pe.wait_ge(consts_in, N_CONSTS)
                for i in range(KT):
                    last = mmul(Q0[:, 0, 0:T], ONES, sqh[:, i, :], start=(i == 0), stop=(i == KT - 1))
                last.then_inc(*norm_pe.did(k, "ss"))
                pe.wait_ge(*norm_dve.at(k, "u"))

            def linear(n, j, out, rhs, k0=0, k1=KT, start=True, stop=True):
                w = slab(n)
                for k in range(k0, k1):
                    last = mmul(out, w[:, k - k0, j * 128:(j + 1) * 128], rhs[:, k, :],
                                start=(start and k == k0), stop=(stop and k == k1 - 1))
                return last

            def tokens(out, src):
                for b, q, i in units():
                    last = mmul(out[LN[i], q, tk(b)], src[LN[i], q, tk(b)], ID[LN[i], LN[i]], start=True, stop=True)
                return last

            def each(out, lhs, rhs, blks=range(NBLK)):
                for b, q, i in units(blks):
                    last = mmul(out[LN[i], q, tk(b)], lhs[LN[i], q, tk(b)], rhs[LN[i], q, tk(b)], start=True, stop=True)
                return last

            def head_norm(src_done, steps, l, sq):
                pe.wait_ge(*src_done)
                for q in range(2):
                    last = mmul(Q1[:, q, 0:T], BLK, sq[:, q, :], start=True, stop=True)
                last.then_inc(*steps.did(l, "nss"))

            for l in range(DEPTH):
                n0 = BASE[l]
                norm(3 * l)
                for s in range(N_PROJ):
                    take(n0 + s)
                    for j in range(2):
                        m = l * 2 * N_PROJ + 2 * s + j
                        if m >= 2:
                            pe.wait_ge(proj_ev, m - 1)
                        linear(n0 + s, j, PJ[:, j, 0:T], u).then_inc(slab_done if j else proj_pe, 1)
                pe.wait_ge(layer_in, PER_L_IN * (l + 1))
                SMP = Q1[:, 0, 0:50].rearrange("p (b g) -> p b g", b=NBLK)
                for b in range(NBLK):
                    for i in range(2):
                        for k in range(KT):
                            last = mmul(SMP[LN[i], b, :], u[:, k, tk(b)], wsm[:, k, i::2], start=(k == 0), stop=(k == KT - 1))
                last.then_inc(*gp_pe.did(l, "small"))
                pe.wait_ge(*gp_dve.at(l, "G"))
                GT = Q1[:, 1, 0:60].rearrange("p (w b g) -> p w b g", w=2, b=NBLK)
                for w in range(2):
                    for kd, b0, b1 in ((0, 0, NPB), (1, NPB, NBLK)):
                        for i in range(2):
                            last = mmul(GT[LN[i], w, b0:b1, :].rearrange("p b g -> p (b g)"), E[LN[i], kd, 6 + w, :],
                                        G[LN[i], b0:b1, :].rearrange("p b g -> p (b g)"), start=True, stop=True)
                last.then_inc(*gp_pe.did(l, "gam"))
                for m, out in ((0, Q0), (1, Q2), (2, Q0)):
                    if m == 2:
                        pe.wait_ge(*gp_act.at(l, "gr0"))
                    for b, q, i in units():
                        last = mmul(out[LN[i], q, tk(b)], G[LN[i], b, 2 * m + q:2 * m + q + 1].to_broadcast([64, 64]),
                                    E[LN[i], kind(b), 6, :], start=True, stop=True)
                    last.then_inc(*gp_pe.did(l, f"gr{m}"))
                pe.wait_ge(*gp_act.at(l, "gr1"))
                for b, q, i in units():
                    last = mmul(Q2[LN[i], q, tk(b)], smb[LN[i], 3, q, b:b + 1].to_broadcast([64, 64]), ID[LN[i], LN[i]],
                                start=True, stop=True)
                last.then_inc(*gp_pe.did(l, "ig"))

                C = C6[0]
                pe.wait_ge(*gd_act.at(l, "sq"))
                pe.wait_ge(*gp_act.at(l, "gr2"))
                pe.wait_ge(*gp_dve.at(l, "gt"))
                sq4 = sl(0, 2).rearrange("p (c t) -> p c t", c=4)
                for c in range(4):
                    last = mmul((Q0, Q1)[c // 2][:, c % 2, 0:T], BLK, sq4[:, c, :], start=True, stop=True)
                last.then_inc(*gd_pe.did(l, "l2"))
                pe.wait_ge(*gd_dve.at(l, "qk"))
                pe.wait_ge(*gp_dve.at(l, "xrow"))
                qT, kT, vT = C[:, 0:2, :], C[:, 2:4, :], C[:, 4:6, :]
                tokens(Q0, kT).then_inc(*gd_pe.did(l, "ktok"))
                tokens(Q1, vT).then_inc(*gd_pe.did(l, "vtok"))
                each(Q2, kT, kT).then_inc(*gd_pe.did(l, "kk"))
                pe.wait_ge(*gd_dve.at(l, "kw"))
                each(Q0, kT, qT).then_inc(*gd_pe.did(l, "qk"))
                pe.wait_ge(*gd_dve.at(l, "qkd"))
                LT, QKD, VB, KB, KW, Tm, U, W, AL, SV, SKT = [tt(i) for i in (3, 4, 5, 6, 7, 8, 9, 10, 11, 0, 1)]
                QE, UU = tt(2), tt(12)
                for j in range(6):
                    blks = range(NBLK) if j < 3 else range(NPB)
                    pe.wait_ge(*gd_dve.at(l, f"al{j}"))
                    pe.wait_ge(*gd_dve.at(l, f"u{j - 1}" if j else "init"))
                    each(Q0, AL, Tm, blks).then_inc(*gd_pe.did(l, f"w{j}"))
                    pe.wait_ge(*gd_dve.at(l, f"wb{j}"))
                    each(Q1, U, W, blks)
                    each(Q2, W, U, blks).then_inc(*gd_pe.did(l, f"tu{j}"))
                pe.wait_ge(*gd_dve.at(l, "u5"))
                each(Q0, KB, U).then_inc(*gd_pe.did(l, "skt"))
                each(Q1, U, VB).then_inc(*gd_pe.did(l, "sv"))
                pe.wait_ge(*gd_act.at(l, "skt"))
                pe.wait_ge(*gd_dve.at(l, "sv"))
                pe.wait_ge(*gd_dve.at(l, "zero"))
                for c in range(NPB):
                    S = Sp[:, c % 2, :, 0:64]
                    if c:
                        pe.wait_ge(*gd_dve.at(l, f"s{c - 1}"))
                    for q in range(2):
                        for i in range(2):
                            last = mmul(Q2[LN[i], q, 0:64], SKT[LN[i], q, tk(c)], S[LN[i], q, :], start=True, stop=True)
                    last.then_inc(*gd_pe.did(l, f"p{c}"))
                    pe.wait_ge(*gd_dve.at(l, f"u{c}_"))
                    for q in range(2):
                        for i in range(2):
                            mmul(Q0[LN[i], q, tk(c)], UU[LN[i], q, tk(c)], QKD[LN[i], q, tk(c)], start=True, stop=False)
                            last = mmul(Q0[LN[i], q, tk(c)], S[LN[i], q, :], QE[LN[i], q, tk(c)], start=False, stop=True)
                    last.then_inc(*gd_pe.did(l, f"o{c}"))
                    for q in range(2):
                        for i in range(2):
                            last = mmul(Q1[LN[i], q, 0:64], KW[LN[i], q, tk(c)], UU[LN[i], q, tk(c)], start=True, stop=True)
                    last.then_inc(*gd_pe.did(l, f"k{c}"))
                SX = sl(5, 2)[:, 0:1024].rearrange("p (q b t) -> p q b t", q=2, b=NB)
                UX = sl(10, 2)[:, 0:1024].rearrange("p (q b t) -> p q b t", q=2, b=NB)
                pe.wait_ge(*gd_dve.at(l, "sx"))
                pe.wait_ge(layer_in, PER_L_IN * (l + 1))
                for q in range(2):
                    for i in range(2):
                        for b in range(NB):
                            last = mmul(Q2[LN[i], q, 0:64], SX[LN[i], q, b, :], stg[LN[i], q, b, :], start=(b == 0), stop=(b == NB - 1))
                last.then_inc(*gd_pe.did(l, "ps"))
                pe.wait_ge(*gd_dve.at(l, "us"))

                def sample_out(Q, V_, A_, S_, X_):
                    for q in range(2):
                        for i in range(2):
                            mmul(Q[LN[i], q, SEQ:T], V_[LN[i], q, SEQ:T], A_[LN[i], q, SEQ:T], start=True, stop=False)
                            for b in range(NB):
                                cols = slice(SEQ + DS * b, SEQ + DS * (b + 1))
                                last = mmul(Q[LN[i], q, cols], S_[LN[i], q, b, :], X_[LN[i], q, cols], start=False, stop=(b == NB - 1))
                    return last

                def sample_state(Q, K_, X_):
                    for q in range(2):
                        for i in range(2):
                            last = mmul(Q[LN[i], q, :], K_[LN[i], q, SEQ:T], X_[LN[i], q, :, :].rearrange("p b v -> p (b v)"),
                                        start=True, stop=True)
                    return last

                sample_out(Q0, UU, QKD, stg, QE).then_inc(*gd_pe.did(l, "os"))
                pe.wait_ge(*gd_dve.at(l, "ux"))
                sample_state(Q1, KW, UX).then_inc(*gd_pe.did(l, "ks"))
                pe.wait_ge(*gd_dve.at(l, "ss"))
                head_norm(gd_act.at(l, "osq"), gd_pe, l, tt(3))

                LFT, VT, ATT, QEh, KWC, KWh = tt(0), tt(1), tt(2), tt(3), tt(4), tt(5)
                ZQ = sl(8, 2)[:, 0:768].rearrange("p (r j t) -> p r j t", r=2, j=6)
                ZK = sl(10, 2)[:, 0:768].rearrange("p (r j t) -> p r j t", r=2, j=6)
                pe.wait_ge(*hg_act.at(l, "lf"))
                pe.wait_ge(*gd_act.at(l, "root"))
                tokens(Q0, sf).then_inc(*hg_pe.did(l, "lftok"))
                tokens(Q1, hgv).then_inc(*hg_pe.did(l, "vtok"))
                pe.wait_ge(*hg_act.at(l, "vt"))
                for n in range(11):
                    if n < 10:
                        b, q = n // 2, n % 2
                        if n >= 2:
                            pe.wait_ge(*hg_act.at(l, f"e{n - 2}"))
                        for i in range(2):
                            last = mmul(Q2[LN[i], n % 2, :], LFT[LN[i], q, tk(b)], E[LN[i], kind(b), :, :].rearrange("p j t -> p (j t)"),
                                        start=True, stop=True)
                        last.then_inc(*hg_pe.did(l, f"x{n}"))
                    if n:
                        n, b, q = n - 1, (n - 1) // 2, (n - 1) % 2
                        pe.wait_ge(*hg_dve.at(l, f"z{n}"))
                        if n >= 2:
                            pe.wait_ge(*hg_dve.at(l, f"m{n - 2}"))
                        for i in range(2):
                            for j in range(6):
                                mmul(Q1[LN[i], n % 2, j * 64:(j + 1) * 64], ZK[LN[i], n % 2, j, :], ZQ[LN[i], n % 2, j, :], start=True, stop=True)
                            last = mmul(Q1[LN[i], n % 2, 384:448], sfn[LN[i], q, tk(b)], hgq[LN[i], q, tk(b)], start=True, stop=True)
                        last.then_inc(*hg_pe.did(l, f"a{n}"))
                tokens(Q0, KWC).then_inc(*hg_pe.did(l, "kw"))
                pe.wait_ge(*hg_act.at(l, "kw"))
                pe.wait_ge(*hg_dve.at(l, "r9"))
                pe.wait_ge(*hg_dve.at(l, "zero"))

                def chunk(c, steps, dve, V_, A_, X_, K_):
                    S = Sp[:, c % 2, :, 0:64]
                    if c:
                        pe.wait_ge(*dve.at(l, f"s{c - 1}"))
                    for q in range(2):
                        for i in range(2):
                            mmul(Q0[LN[i], q, tk(c)], V_[LN[i], q, tk(c)], A_[LN[i], q, tk(c)], start=True, stop=False)
                            last = mmul(Q0[LN[i], q, tk(c)], S[LN[i], q, :], X_[LN[i], q, tk(c)], start=False, stop=True)
                    if steps is ml_pe:
                        for q in range(2):
                            for i in range(2):
                                mmul(Q2[LN[i], q, tk(c)], ONES[LN[i], 0:64], A_[LN[i], q, tk(c)], start=True, stop=False)
                                last = mmul(Q2[LN[i], q, tk(c)], nst[LN[i], c % 2, q:q + 1].to_broadcast([64, 64]),
                                            X_[LN[i], q, tk(c)], start=False, stop=True)
                    last.then_inc(*steps.did(l, f"o{c}"))
                    for q in range(2):
                        for i in range(2):
                            last = mmul(Q1[LN[i], q, 0:64], K_[LN[i], q, tk(c)], V_[LN[i], q, tk(c)], start=True, stop=True)
                            if steps is ml_pe:
                                last = mmul(Q1[LN[i], q, 64:65], K_[LN[i], q, tk(c)], ONES[LN[i], 0:1], start=True, stop=True)
                    last.then_inc(*steps.did(l, f"k{c}"))

                for c in range(NPB):
                    chunk(c, hg_pe, hg_dve, VT, ATT, QEh, KWh)
                sample_out(Q0, VT, ATT, sth, QEh).then_inc(*hg_pe.did(l, "os"))
                pe.wait_ge(*hg_dve.at(l, "ux"))
                sample_state(Q1, KWh, UX).then_inc(*hg_pe.did(l, "ks"))
                pe.wait_ge(*hg_dve.at(l, "ss"))
                head_norm(hg_act.at(l, "osq"), hg_pe, l, tt(7))

                C = C6[1]
                XT, XW, AT, BTK = tt(0), tt(1), tt(2), sl(4, 2).rearrange("p (q b n) -> p q b n", q=2, b=NBLK)
                XWX = sl(6, 2)[:, 0:1024].rearrange("p (q b t) -> p q b t", q=2, b=NB)
                HT = sl(8)[:, 0:256].rearrange("p (q t) -> p q t", q=2)
                HTS = sl(9, 2)[:, 0:1024].rearrange("p (b t) -> p b t", b=NB)
                pe.wait_ge(conv_silu, 12 * (l + 1))
                pe.wait_ge(*hg_act.at(l, "root"))
                pe.wait_ge(*hg_dve.at(l, "o"))
                tokens(Q0, C[:, 0:2, :]).then_inc(*sd_pe.did(l, "xtok"))
                for b, q, i in units():
                    out = Q1[LN[i], q, b * 128:(b + 1) * 128] if b < NPB else Q2[LN[i], q, 0:128]
                    last = mmul(out, C[:, 2 + q, tk(b)], ID[:, :], start=True, stop=True)
                last.then_inc(*sd_pe.did(l, "btok"))
                pe.wait_ge(*sd_dve.at(l, "xw"))
                pe.wait_ge(*sd_act.at(l, "bts"))
                for b, q, i in units():
                    last = mmul(Q0[LN[i], q, tk(b)], C[:, 2 + q, tk(b)], C[:, 4 + q, tk(b)], start=True, stop=True)
                last.then_inc(*sd_pe.did(l, "cb"))
                pe.wait_ge(*sd_dve.at(l, "xx"))
                pe.wait_ge(*sd_dve.at(l, "zero"))
                for c in range(NPB):
                    S = Sp[:, c % 2, :, :]
                    if c:
                        pe.wait_ge(*sd_dve.at(l, f"s{c - 1}"))
                    for q in range(2):
                        last = nc.tensor.transpose(Q2[:, q, 0:128], S[:, q, :], ID[:, :])
                    last.then_inc(*sd_pe.did(l, f"t{c}"))
                    pe.wait_ge(*sd_act.at(l, f"t{c}"))
                    for q in range(2):
                        mmul(Q1[:, q, tk(c)], HT[:, q, :], C[:, 4 + q, tk(c)], start=True, stop=True)
                        for i in range(2):
                            last = mmul(Q0[LN[i], q, tk(c)], XT[LN[i], q, tk(c)], AT[LN[i], q, tk(c)], start=True, stop=True)
                    last.then_inc(*sd_pe.did(l, f"y{c}"))
                    for q in range(2):
                        for i in range(2):
                            last = mmul(Q2[LN[i], q, 128:256], XW[LN[i], q, tk(c)], BTK[LN[i], q, c, :], start=True, stop=True)
                    last.then_inc(*sd_pe.did(l, f"k{c}"))
                Q2f = Q2[:, :, :].rearrange("p a (b n) -> p (a b) n", n=128)
                for q in range(2):
                    pe.wait_ge(*sd_dve.at(l, "ss0" if q else f"s{NPB - 1}"))
                    for b in range(NB):
                        last = nc.tensor.transpose(Q2f[:, b, :], sts[:, q, b, :], ID[:, :])
                    last.then_inc(*sd_pe.did(l, f"t_{q}"))
                    pe.wait_ge(*sd_act.at(l, f"t_{q}"))
                    for b in range(NB):
                        cols = slice(SEQ + DS * b, SEQ + DS * (b + 1))
                        last = mmul(Q1[:, q, cols], HTS[:, b, :], C[:, 4 + q, cols], start=True, stop=True)
                    for i in range(2):
                        last = mmul(Q0[LN[i], q, SEQ:T], XT[LN[i], q, SEQ:T], AT[LN[i], q, SEQ:T], start=True, stop=True)
                    last.then_inc(*sd_pe.did(l, f"y_{q}"))
                    for b in range(NB):
                        for i in range(2):
                            last = mmul(Q2f[LN[i], b, :], XWX[LN[i], q, b, :], BTK[LN[i], q, NPB, :], start=True, stop=True)
                    last.then_inc(*sd_pe.did(l, f"k_{q}"))
                pe.wait_ge(*sd_act.at(l, "osq"))
                pe.wait_ge(*sd_dve.at(l, "yz"))
                for q in range(2):
                    last = mmul(Q1[:, 0, 0:T], ONES, tt(10)[:, q, :], start=(q == 0), stop=(q == 1))
                last.then_inc(*sd_pe.did(l, "nss"))

                VTm, WT, QW, KWm = tt(0), tt(2), tt(3), tt(4)
                pe.wait_ge(*sd_act.at(l, "root"))
                pe.wait_ge(*sd_dve.at(l, "y1"))
                pe.wait_ge(*sd_dve.at(l, "ss1"))
                tokens(Q0, mlv).then_inc(*ml_pe.did(l, "vtok"))
                tokens(Q1, mlk).then_inc(*ml_pe.did(l, "ktok"))
                each(Q2, mlk, mlq).then_inc(*ml_pe.did(l, "kq"))
                pe.wait_ge(*ml_dve.at(l, "kw0"))
                pe.wait_ge(*ml_act.at(l, "vt"))
                pe.wait_ge(*ml_dve.at(l, "zero"))
                for c in range(NPB):
                    chunk(c, ml_pe, ml_dve, VTm, WT, QW, KWm)
                sample_out(Q0, VTm, WT, stm, QW)
                for q in range(2):
                    for i in range(2):
                        mmul(Q2[LN[i], q, SEQ:T], ONES[LN[i], 0:64], WT[LN[i], q, SEQ:T], start=True, stop=False)
                        for b in range(NB):
                            cols = slice(SEQ + DS * b, SEQ + DS * (b + 1))
                            last = mmul(Q2[LN[i], q, cols], stn[LN[i], q, b:b + 1].to_broadcast([64, 64]), QW[LN[i], q, cols],
                                        start=False, stop=(b == NB - 1))
                last.then_inc(*ml_pe.did(l, "os"))
                pe.wait_ge(*ml_dve.at(l, "ux"))
                sample_state(Q1, KWm, UX)
                for q in range(2):
                    for i in range(2):
                        last = mmul(PJ[LN[i], q, 0:NB], KWm[LN[i], q, SEQ:T], BM[LN[i], :], start=True, stop=True)
                last.then_inc(*ml_pe.did(l, "ks"))
                pe.wait_ge(*ml_dve.at(l, "ss"))
                head_norm(ml_act.at(l, "osq"), ml_pe, l, tt(7))

                def gated(n1, g0, src, wait):
                    pe.wait_ge(*wait)
                    take(n1)
                    w = slab2(n1)
                    for t in range(KT):
                        m = 16 * g0 + t
                        if t >= 2:
                            pe.wait_ge(gat_act, m - 1)
                        for k in range(2):
                            last = mmul(PJ[:, t % 2, 0:T], w[:, k, t * 128:(t + 1) * 128], src[:, k, :], start=(k == 0), stop=(k == 1))
                        last.then_inc(gat_pe, 1)
                    pe.wait_ge(gat_pe, 16 * g0 + 8)
                    pe.sem_inc(slab_done, 1)
                    for s in range(4):
                        take(n1 + 1 + s)
                        for j in range(2):
                            m = 16 * g0 + 8 + 2 * s + j
                            if s:
                                pe.wait_ge(gat_act, m - 1)
                            linear(n1 + 1 + s, j, Q2[:, j, 0:T], u).then_inc(gat_pe, 1)
                        pe.wait_ge(gat_pe, 16 * g0 + 8 + 2 * s + 2)
                        pe.sem_inc(slab_done, 1)

                n1 = n0 + N_PROJ
                for n in range(4):
                    gated(n1 + 5 * n, 5 * l + n, BR[:, n], ml_dve.at(l, "br") if n == 0 else (gat_act, 16 * (5 * l + n)))
                n2 = n1 + N_GATED
                pe.wait_ge(gat_dve, 8 * (5 * l + 4))
                for s in range(N_OUT):
                    take(n2 + s)
                    for j in range(2):
                        m = 8 * l + 2 * s + j
                        if s:
                            pe.wait_ge(out_ev, m - 1)
                        linear(n2 + s, j, PJ[:, j, 0:T], merged).then_inc(slab_done if j else out_pe, 1)
                norm(3 * l + 1)
                n3 = n2 + N_OUT

                def swiglu(n3):
                    for c in range(CH):
                        for up in range(2):
                            n = n3 + 2 * c + up
                            take(n)
                            Q = ((Q0, Q1), (PJ, Q2))[c % 2][up]
                            if c >= 2 and not up:
                                pe.wait_ge(ff_dve, c - 1)
                            for j in range(2):
                                last = linear(n, j, Q[:, j, 0:T], u)
                            last.then_inc(slab_done, 1)
                    pe.wait_ge(ff_dve, CH)
                    for d, (s, k0, k1) in enumerate(DOWN):
                        n = n3 + FT + d
                        take(n)
                        Q = (PJ, Q2)[s % 2]
                        if k0 == 0 and s >= 2:
                            pe.wait_ge(dn_dve, 2 * s - 2)
                        for j in range(2):
                            last = linear(n, j, Q[:, j, 0:T], hid, k0, k1, start=(k0 == 0), stop=(k1 == FT))
                        last.then_inc(slab_done, 1)

                def gather(x):
                    for k in range(KT):
                        for t, (t0, t1) in enumerate(TT):
                            last = mmul(PJ[:, k // 4, (k % 4) * CAP:(k % 4 + 1) * CAP], utok[0:t1 - t0, t, k * 128:(k + 1) * 128],
                                        sel[0:t1 - t0, t, :], start=(t == 0), stop=(t == 2))
                    last.then_inc(x["xg_pe"], 1)

                def expert(e, x, n0, c0):
                    si, sd = x["slab_in"], x["slab_done"]

                    def ready(i):
                        n = n0 + i
                        per = loads(n, 0, N_X)
                        before = loads(n, -n0, 0) if x is main else (c0 - 1) * per
                        pe.wait_ge(si[n % R], e * (16 * per) + 16 * (before + loads(n, 0, i) + 1))

                    def loads(n, i0, i1):
                        return sum((n0 + i) % R == n % R for i in range(i0, i1))

                    for c in range(CH):
                        if c == 0:
                            pe.wait_ge(x["xg"], e + c0)
                        for up in range(2):
                            n = n0 + 2 * c + up
                            ready(2 * c + up)
                            Q = (Q0, Q1)[c % 2]
                            if up == 0:
                                pe.wait_ge(x["hid"], e * CH + (c0 * CH + c - 1))
                            w = slab_x(n)
                            for j in range(2):
                                for k in range(KT):
                                    last = mmul(Q[:, up, j * CAP:(j + 1) * CAP], w[:, k, j * 128:(j + 1) * 128], xg[:, k, :],
                                                start=(k == 0), stop=(k == KT - 1))
                            last.then_inc(sd, 1)
                        if c == 2:
                            pe.wait_ge(x["selw"], e + (c0 + 1))
                            pe.wait_ge(x["hadd"], e * KT + c0 * KT)
                            for t, (t0, t1) in enumerate(TT):
                                last = nc.tensor.transpose(PJ[0:CAP, 0, t0:t1], selw[0:t1 - t0, t, :], ID[0:t1 - t0, 0:t1 - t0])
                            last.then_inc(x["selt_pe"], 1)
                    pe.wait_ge(x["sel"], e + (c0 + 1))
                    pe.wait_ge(x["selt"], e + (c0 + 1))
                    gather(x)
                    pe.wait_ge(x["hid"], e * CH + (c0 * CH + CH))
                    pe.wait_ge(x["yg"], e + c0)
                    for d in range(FT // 2):
                        n = n0 + 2 * CH + d
                        ready(2 * CH + d)
                        w = slab2(n)
                        for r in range(2):
                            for c in range(2):
                                last = mmul(Q2[0:CAP, c, :], hidx[:, 2 * d + r, :], w[:, r, c * 512:(c + 1) * 512],
                                            start=(d == 0 and r == 0), stop=(d == FT // 2 - 1 and r == 1))
                        last.then_inc(sd, 1 + N_SKIP if d == FT // 2 - 1 else 1)
                    pe.wait_ge(x["yg"], e + (c0 + 1))
                    pe.wait_ge(x["xg"], e + (c0 + 1))
                    for t in range(KT):
                        if t >= 2:
                            pe.wait_ge(x["hadd"], e * KT + (c0 * KT + t - 1))
                        mmul(PJ[:, t % 2, 0:T], yg[0:CAP, t * 128:(t + 1) * 128], selt[0:CAP, :], start=True, stop=True).then_inc(x["scat"], 1)

                if l == 0:
                    swiglu(n3)
                    n4 = n3 + N_FF
                else:
                    for t, (t0, t1) in enumerate(TT):
                        for k in range(KT):
                            last = nc.tensor.transpose((Q0, Q1, Q2)[t][0:t1 - t0, k // 4, (k % 4) * 128:(k % 4 + 1) * 128], u[:, k, t0:t1], ID[:, :])
                    last.then_inc(*rt_pe.did(0, "utok"))
                    for t, (t0, t1) in enumerate(TT):
                        for k in range(KT):
                            last = mmul(PJ[0:t1 - t0, 0, t * 8:(t + 1) * 8], u[:, k, t0:t1], wr[:, k, :], start=(k == 0), stop=(k == KT - 1))
                    last.then_inc(*rt_pe.did(0, "logit"))
                    pe.wait_ge(*rt_dve.at(0, "M"))
                    M = rt[:, :, 28:36]
                    for t, (t0, t1) in enumerate(TT):
                        w = t1 - t0
                        for j in range(t):
                            mmul(PJ[0:w, 1, t * 8:(t + 1) * 8], ONES[:, 0:w], M[:, j, :], start=(j == 0), stop=False)
                        mmul(PJ[0:w, 1, t * 8:(t + 1) * 8], STR[0:w, 0:w], M[0:w, t, :], start=(t == 0), stop=True)
                    for t, (t0, t1) in enumerate(TT):
                        last = mmul(PJ[:, 1, 24:32], ONES[0:t1 - t0, :], M[0:t1 - t0, t, :], start=(t == 0), stop=(t == 2))
                    last.then_inc(*rt_pe.did(0, "rank"))
                    pe.wait_ge(*rt_act.at(0, "utok2"))
                    pe.wait_ge(*rt_dve.at(0, "flag"))

                    def start(x):
                        pe.sem_inc(x["scat"], KT)
                        pe.sem_inc(x["selt_pe"], 1)
                        pe.wait_ge(x["sel"], 1)
                        gather(x)

                    start(main)
                    with pe.Fori(0, NE) as e:
                        expert(e, main, n3, 1)
                    with pe.If(pe.value_load(flag[0:1, 0:1], min_val=0, max_val=1)):
                        pe.wait_ge(main["hadd"], (NE + 1) * KT)
                        pe.sem_inc(over["slab_done"], R)
                        start(over)
                        for g in range(1, GROUPS):
                            with pe.Fori(0, NE) as e:
                                expert(e, over, NE * N_XV * (g - 1) + R, NE * (g - 1) + 1)
                    n4 = n3 + NE * N_XV
                norm(3 * l + 2)
                pe.wait_ge(ple_in, 16 * (l + 1))
                gated(n4, 5 * l + 4, pt, norm_dve.at(3 * l + 2, "u"))
            norm(N_NORM - 1)

        @block.scalar
        def _(act):
            av = nc.scalar.activation

            def norm(k):
                if k == 0:
                    act.wait_ge(consts_in, N_CONSTS)
                else:
                    act.wait_ge(h_done, k)
                av(sqh[:, :, :], h[:, :, :], ACT.Square).then_inc(*norm_act.did(k, "sq"))
                act.wait_ge(*norm_act.at(k, "sq"))
                act.wait_ge(*norm_pe.at(k, "ss"))
                av(rstd[:, :], Q0[:, 0, 0:T], ACT.Sqrt, bias=EPSC[:, 0:1], scale=1.0 / DM).then_inc(*norm_act.did(k, "root"))
                act.wait_ge(*norm_act.at(k, "root"))

            tiles = []
            for i in range(6):
                tiles.append(("xp", i))
            tiles += [("mlq", 0), ("mlk", 0)]
            for name in ("hgq", "hgv", "mlv", "gz", "hgg", "sz", "f", "o"):
                tiles += [(name, 0), (name, 1)]
            for i in range(6):
                tiles.append(("xps", i))
            dst = {"hgq": hgq, "hgv": hgv, "mlv": mlv, "gz": gz, "hgg": hgg, "sz": sz, "o": mlo}

            def conv_act(l, g, c):
                m = (2 * l + g) * 6 + c
                act.wait_ge(conv_tap, 8 * (m + 1))
                av(C6[g][:, c, :], cacc[:, m % 2, :], ACT.Silu).then_inc(conv_silu, 1)

            cacc = XROW

            def head_norm(l, steps, dve, pe_, o, sq, rn, src):
                act.wait_ge(*dve.at(l, src))
                av(sq, o, ACT.Square).then_inc(*steps.did(l, "osq"))
                act.wait_ge(*steps.at(l, "osq"))
                act.wait_ge(*pe_.at(l, "nss"))
                av(rn, Q1[:, :, 0:T], ACT.Sqrt, bias=EPSC[:, 0:1], scale=1.0 / 64).then_inc(*steps.did(l, "root"))
                act.wait_ge(*steps.at(l, "root"))

            for l in range(DEPTH):
                if l == 0:
                    act.wait_ge(*setup_dve.at(0, "sub"))
                    av(lbt[:, 3:5, :], lbt[:, 1:3, :], ACT.Exp).then_inc(*setup_act.did(0, "exp"))
                    act.wait_ge(*setup_act.at(0, "exp"))
                norm(3 * l)
                for i, (name, j) in enumerate(tiles):
                    m = l * 30 + i
                    if m % 2 == 0:
                        act.wait_ge(proj_pe, m // 2 + 1)
                    else:
                        act.wait_ge(slab_done, BASE[l] + i // 2 + 1)
                    P = PJ[:, m % 2, 0:T]
                    if name in ("xp", "xps"):
                        g = name == "xps"
                        if i == 0:
                            act.wait_ge(*pads.at(l, "zero"))
                            if l:
                                act.wait_ge(conv_new, 4 * l)
                        if g and j == 0:
                            act.wait_ge(conv_new, 4 * l + 2)
                            act.wait_ge(conv_tap, 96 * l + 48)
                        av(XP[:, j, 3:3 + SEQ], P[:, 0:SEQ], ACT.Copy)
                        last = av(XP[:, j, 3 + SEQ:XPW].rearrange("p (b t) -> p b t", b=NB)[:, :, 3:3 + DS],
                                  P[:, SEQ:T].rearrange("p (b t) -> p b t", b=NB), ACT.Copy)
                    elif name in ("mlq", "mlk"):
                        for hd in range(4):
                            d = (mlq if name == "mlq" else mlk)[64 * (hd % 2):64 * (hd % 2) + 32, hd // 2, :]
                            last = av(d, PJ[32 * hd:32 * hd + 32, m % 2, 0:T], ACT.Copy, scale=1.0 if name == "mlq" else 32 ** -0.5)
                    elif name == "f":
                        av(sf[:, j, :], P, ACT.Sigmoid)
                        last = av(sfn[:, j, :], P, ACT.Sigmoid, scale=-1.0)
                    else:
                        fn = {"gz": ACT.Silu, "hgg": ACT.Silu, "sz": ACT.Silu, "o": ACT.Sigmoid}.get(name, ACT.Copy)
                        last = av(dst[name][:, j, :], P, fn)
                    last.then_inc(proj_ev, 1)
                    if 12 <= i < 18:
                        conv_act(l, 0, i - 12)
                for c in range(6):
                    conv_act(l, 1, c)
                act.wait_ge(*gp_dve.at(l, "smb"))
                av(beta[:, :, :], smb[:, 0, :, :], ACT.Sigmoid).then_inc(*gp_act.did(l, "beta"))
                act.wait_ge(*gp_act.at(l, "beta"))
                av(sm1[:, :, 0:2], pr(l, "alog").rearrange("p (a q) -> p a q", a=2), ACT.Exp).then_inc(*gp_act.did(l, "ea"))
                act.wait_ge(*gp_act.at(l, "ea"))
                act.wait_ge(*gp_dve.at(l, "spi"))
                av(sp3[:, 1, :], sp3[:, 0, :], ACT.Abs).then_inc(*gp_act.did(l, "abs"))
                act.wait_ge(*gp_act.at(l, "abs"))
                av(sp3[:, 2, :], sp3[:, 1, :], ACT.Exp, scale=-1.0).then_inc(*gp_act.did(l, "e"))
                act.wait_ge(*gp_act.at(l, "e"))
                act.wait_ge(*gp_dve.at(l, "u1"))
                av(sp3[:, 4, :], sp3[:, 3, :], ACT.Ln).then_inc(*gp_act.did(l, "ln"))
                act.wait_ge(*gp_act.at(l, "ln"))
                act.wait_ge(*gp_dve.at(l, "gt"))
                av(egt[:, :, :, :], gt[:, :, :, :], ACT.Exp).then_inc(*gp_act.did(l, "egt"))
                act.wait_ge(*gp_act.at(l, "egt"))
                for m, Q in ((0, Q0), (1, Q2), (2, Q0)):
                    act.wait_ge(*gp_pe.at(l, f"gr{m}"))
                    av(GR[m], Q[:, :, 0:T], ACT.Copy).then_inc(*gp_act.did(l, f"gr{m}"))
                    act.wait_ge(*gp_act.at(l, f"gr{m}"))

                C = C6[0]
                act.wait_ge(conv_silu, 12 * l + 6)
                sq4 = sl(0, 2).rearrange("p (c t) -> p c t", c=4)
                av(sq4, C[:, 0:4, :], ACT.Square).then_inc(*gd_act.did(l, "sq"))
                act.wait_ge(*gd_act.at(l, "sq"))
                act.wait_ge(*gd_pe.at(l, "l2"))
                av(sq4[:, 0:2, :], Q0[:, :, 0:T], ACT.Sqrt, bias=EPSC[:, 1:2], scale=64.0).then_inc(*gd_act.did(l, "rootq"))
                act.wait_ge(*gd_act.at(l, "rootq"))
                av(sq4[:, 2:4, :], Q1[:, :, 0:T], ACT.Sqrt, bias=EPSC[:, 0:1], scale=1.0).then_inc(*gd_act.did(l, "rootk"))
                act.wait_ge(*gd_act.at(l, "rootk"))
                act.wait_ge(*gd_dve.at(l, "dmin"))
                av(tt(2), tt(2), ACT.Exp).then_inc(*gd_act.did(l, "dexp"))
                act.wait_ge(*gd_act.at(l, "dexp"))
                act.wait_ge(*gp_act.at(l, "gr2"))
                av(GR[0], GR[0], ACT.Exp).then_inc(*gd_act.did(l, "egrow"))
                act.wait_ge(*gd_act.at(l, "egrow"))
                act.wait_ge(*gd_pe.at(l, "skt"))
                av(tt(1), Q0[:, :, 0:T], ACT.Copy).then_inc(*gd_act.did(l, "skt"))
                act.wait_ge(*gd_act.at(l, "skt"))
                head_norm(l, gd_act, gd_dve, gd_pe, tt(9), tt(3), tt(8), "o")

                act.wait_ge(*hg_dve.at(l, "pre"))
                av(sf, sf, ACT.Ln).then_inc(*hg_act.did(l, "lf"))
                act.wait_ge(*hg_act.at(l, "lf"))
                act.wait_ge(*hg_pe.at(l, "lftok"))
                av(tt(0), Q0[:, :, 0:T], ACT.Copy).then_inc(*hg_act.did(l, "lft"))
                act.wait_ge(*hg_act.at(l, "lft"))
                act.wait_ge(*hg_pe.at(l, "vtok"))
                av(tt(1), Q1[:, :, 0:T], ACT.Copy).then_inc(*hg_act.did(l, "vt"))
                act.wait_ge(*hg_act.at(l, "vt"))
                X = sl(6, 2)[:, 0:1024].rearrange("p (r j t) -> p r j t", r=2, j=8)
                for n in range(10):
                    b, q = n // 2, n % 2
                    act.wait_ge(*hg_pe.at(l, f"x{n}"))
                    if n >= 2:
                        act.wait_ge(*hg_dve.at(l, f"z{n - 2}"))
                    av(X[:, n % 2], Q2[:, n % 2, :].rearrange("p (j t) -> p j t", j=8), ACT.Exp).then_inc(*hg_act.did(l, f"x{n}"))
                    act.wait_ge(*hg_act.at(l, f"x{n}"))
                    o, i_ = (egc[:, q, b:b + 1], X[:, n % 2, 6, BL - 1:BL]) if b < NPB else (egc[:, q, NPB:], X[:, n % 2, 6, DS - 1::DS])
                    av(o, i_, ACT.Copy).then_inc(*hg_act.did(l, f"e{n}"))
                    act.wait_ge(*hg_act.at(l, f"e{n}"))
                act.wait_ge(*hg_pe.at(l, "kw"))
                av(tt(5), Q0[:, :, 0:T], ACT.Copy).then_inc(*hg_act.did(l, "kw"))
                act.wait_ge(*hg_act.at(l, "kw"))
                head_norm(l, hg_act, hg_dve, hg_pe, tt(6), tt(7), tt(8), "o")

                act.wait_ge(*sd_dve.at(l, "dmin"))
                av(tt(3), tt(3), ACT.Exp).then_inc(*sd_act.did(l, "dexp"))
                act.wait_ge(*sd_act.at(l, "dexp"))
                av(GR[1], GR[1], ACT.Exp).then_inc(*sd_act.did(l, "egrow"))
                act.wait_ge(*sd_act.at(l, "egrow"))
                act.wait_ge(*sd_pe.at(l, "xtok"))
                act.wait_ge(*sd_dve.at(l, "xw"))
                av(tt(0), Q0[:, :, 0:T], ACT.Copy).then_inc(*sd_act.did(l, "xt"))
                act.wait_ge(*sd_act.at(l, "xt"))
                BTK = sl(4, 2).rearrange("p (q b n) -> p q b n", q=2, b=NBLK)
                act.wait_ge(*sd_pe.at(l, "btok"))
                av(BTK[:, :, 0:NPB, :], Q1[:, :, :].rearrange("p q (b n) -> p q b n", n=128), ACT.Copy).then_inc(*sd_act.did(l, "btp"))
                act.wait_ge(*sd_act.at(l, "btp"))
                av(BTK[:, :, NPB, :], Q2[:, :, 0:128], ACT.Copy).then_inc(*sd_act.did(l, "bts"))
                act.wait_ge(*sd_act.at(l, "bts"))
                HT = sl(8)[:, 0:256].rearrange("p (q t) -> p q t", q=2)
                HTS = sl(9, 2)[:, 0:1024].rearrange("p (b t) -> p b t", b=NB)
                for c in range(NPB):
                    act.wait_ge(*sd_pe.at(l, f"t{c}"))
                    av(HT, Q2[:, :, 0:128], ACT.Copy).then_inc(*sd_act.did(l, f"t{c}"))
                    act.wait_ge(*sd_act.at(l, f"t{c}"))
                for q in range(2):
                    act.wait_ge(*sd_pe.at(l, f"t_{q}"))
                    av(HTS, Q2[:, :, :].rearrange("p a (b n) -> p (a b) n", n=128), ACT.Copy).then_inc(*sd_act.did(l, f"t_{q}"))
                    act.wait_ge(*sd_act.at(l, f"t_{q}"))
                act.wait_ge(*sd_dve.at(l, "yz"))
                av(tt(10), tt(9), ACT.Square).then_inc(*sd_act.did(l, "osq"))
                act.wait_ge(*sd_act.at(l, "osq"))
                act.wait_ge(*sd_pe.at(l, "nss"))
                av(tt(8)[:, 0, :], Q1[:, 0, 0:T], ACT.Sqrt, bias=EPSC[:, 0:1], scale=1.0 / 256).then_inc(*sd_act.did(l, "root"))
                act.wait_ge(*sd_act.at(l, "root"))

                act.wait_ge(*ml_pe.at(l, "vtok"))
                act.wait_ge(*sd_dve.at(l, "br"))
                av(tt(0), Q0[:, :, 0:T], ACT.Copy).then_inc(*ml_act.did(l, "vt"))
                act.wait_ge(*ml_act.at(l, "vt"))
                act.wait_ge(*ml_dve.at(l, "min"))
                av(tt(2), tt(2), ACT.Exp).then_inc(*ml_act.did(l, "wexp"))
                act.wait_ge(*ml_act.at(l, "wexp"))
                act.wait_ge(*ml_dve.at(l, "wpre"))
                av(tt(5), tt(5), ACT.Exp).then_inc(*ml_act.did(l, "win"))
                act.wait_ge(*ml_act.at(l, "win"))
                av(wend[:, :, :], wend[:, :, :], ACT.Exp).then_inc(*ml_act.did(l, "wend"))
                act.wait_ge(*ml_act.at(l, "wend"))
                act.wait_ge(*ml_dve.at(l, "mt"))
                av(tt(6), tt(6), ACT.Exp, scale=-1.0).then_inc(*ml_act.did(l, "emt"))
                act.wait_ge(*ml_act.at(l, "emt"))
                act.wait_ge(*ml_pe.at(l, "os"))
                av(tt(7), Q2[:, :, 0:T], ACT.Abs).then_inc(*ml_act.did(l, "dab"))
                act.wait_ge(*ml_act.at(l, "dab"))
                head_norm(l, ml_act, ml_dve, ml_pe, tt(9), tt(7), tt(8), "oo")

                def gated(g0):
                    for t in range(16):
                        m = 16 * g0 + t
                        act.wait_ge(gat_pe, m + 1)
                        if t < 8:
                            if t == 0 and g0:
                                act.wait_ge(gat_dve, 8 * g0)
                            av(prod[:, t, :], PJ[:, t % 2, 0:T], ACT.Copy).then_inc(gat_act, 1)
                        else:
                            if t >= 12:
                                act.wait_ge(gat_dve, 8 * g0 + t - 11)
                            av(sgs[:, t % 4, :], Q2[:, t % 2, 0:T], ACT.Sigmoid).then_inc(gat_act, 1)

                act.wait_ge(*ml_dve.at(l, "br"))
                for n in range(4):
                    gated(5 * l + n)
                norm(3 * l + 1)

                n3 = BASE[l] + N_PROJ + N_GATED + N_OUT

                def expert(e, x, n0, c0):
                    for c in range(CH):
                        act.wait_ge(x["slab_done"], e * N_XV + (n0 + 2 * c + 1))
                        act.wait_ge(x["hid"], e * CH + (c0 * CH + c - 1))
                        av(sgx[:, c % 2, :], (Q0, Q1)[c % 2][:, 0, 0:2 * CAP], ACT.Silu).then_inc(x["silu"], 1)
                        if c == 4:
                            act.wait_ge(x["selt_pe"], e + (c0 + 1))
                            av(selt[0:CAP, :], PJ[0:CAP, 0, 0:T], ACT.Copy).then_inc(x["selt"], 1)
                    act.wait_ge(x["xg_pe"], e + (c0 + 1))
                    av(xg.rearrange("p (a k) t -> p a (k t)", a=2), PJ[:, :, 0:4 * CAP], ACT.Copy).then_inc(x["xg"], 1)
                    act.wait_ge(x["slab_done"], e * N_XV + (n0 + N_XV))
                    av(yg[0:CAP, :].rearrange("p (a c) -> p a c", a=2), Q2[0:CAP, :, :], ACT.Copy).then_inc(x["yg"], 1)

                if l == 0:
                    for c in range(CH):
                        act.wait_ge(slab_done, n3 + 2 * c + 1)
                        if c >= 2:
                            act.wait_ge(ff_dve, c - 1)
                        av(ffs[:, c % 2], (Q0, PJ)[c % 2][:, :, 0:T], ACT.Silu).then_inc(ff_act, 1)
                else:
                    act.wait_ge(*rt_pe.at(0, "utok"))
                    for t, (t0, t1) in enumerate(TT):
                        av(utok[0:t1 - t0, t, :].rearrange("p (a c) -> p a c", a=2), (Q0, Q1, Q2)[t][0:t1 - t0, :, :], ACT.Copy)\
                            .then_inc(*rt_act.did(0, f"utok{t}"))
                    act.wait_ge(*rt_dve.at(0, "d"))
                    av(rt[:, :, 24:25], rt[:, :, 24:25], ACT.Exp).then_inc(*rt_act.did(0, "e"))

                    def start(x):
                        act.sem_inc(x["silu"], CH)
                        act.sem_inc(x["yg"], 1)
                        act.sem_inc(x["selt"], 1)
                        act.wait_ge(x["xg_pe"], 1)
                        av(xg.rearrange("p (a k) t -> p a (k t)", a=2), PJ[:, :, 0:4 * CAP], ACT.Copy).then_inc(x["xg"], 1)

                    start(main)
                    with act.Fori(0, NE) as e:
                        expert(e, main, n3, 1)
                    act.wait_ge(*rt_dve.at(0, "flag"))
                    with act.If(act.value_load(flag[0:1, 0:1], min_val=0, max_val=1)):
                        start(over)
                        for g in range(1, GROUPS):
                            with act.Fori(0, NE) as e:
                                expert(e, over, NE * N_XV * (g - 1) + R, NE * (g - 1) + 1)
                norm(3 * l + 2)
                gated(5 * l + 4)
            norm(N_NORM - 1)

        @block.vector
        def _(dve):
            v = nc.vector

            def norm(k):
                dve.wait_ge(*norm_act.at(k, "root"))
                v.reciprocal(rstd[:, :], rstd[:, :]).then_inc(*norm_dve.did(k, "rstd"))
                dve.wait_ge(*norm_dve.at(k, "rstd"))
                l = min(k // 3, DEPTH - 1)
                g = pr(l, "g_final" if k == N_NORM - 1 else ("g_mix", "g_ffn", "g_ple")[k % 3])
                for i in range(KT):
                    last = v.scalar_tensor_tensor(out=u[:, i, :], in0=h[:, i, :], scalar=g[:, i:i + 1], in1=rstd[:, :],
                                                  op0=ALU.mult, op1=ALU.mult)
                last.then_inc(*norm_dve.did(k, "u"))
                dve.wait_ge(*norm_dve.at(k, "u"))

            dve.wait_ge(consts_in, N_CONSTS)
            lb = pr(0, "lb").rearrange("p (d q) -> p d q", d=2)
            v.tensor_tensor(lbt[:, 0, :], lb[:, 0, :], lb[:, 1, :], ALU.max).then_inc(*setup_dve.did(0, "max"))
            dve.wait_ge(*setup_dve.at(0, "max"))
            v.tensor_tensor(lbt[:, 1:3, :], lb, lbt[:, 0:1, :].to_broadcast([128, 2, 2]), ALU.subtract).then_inc(*setup_dve.did(0, "sub"))
            dve.wait_ge(*setup_dve.at(0, "sub"))
            dve.wait_ge(*setup_act.at(0, "exp"))
            v.tensor_tensor(lbt[:, 5, :], lbt[:, 3, :], lbt[:, 4, :], ALU.add).then_inc(*setup_dve.did(0, "sum"))
            dve.wait_ge(*setup_dve.at(0, "sum"))
            v.reciprocal(lbt[:, 6, :], lbt[:, 5, :]).then_inc(*setup_dve.did(0, "rcp"))
            dve.wait_ge(*setup_dve.at(0, "rcp"))
            v.memset(lbv[:, 0, 0, :], 0.0)
            v.tensor_tensor(lbv[:, 1, 0, :], lbt[:, 4, :], lbt[:, 6, :], ALU.mult).then_inc(*setup_dve.did(0, "sm"))
            dve.wait_ge(*setup_dve.at(0, "sm"))
            v.tensor_scalar(lbv[:, :, 1, :], lbv[:, :, 0, :], -1.0, 1.0, ALU.mult, ALU.add).then_inc(*setup_dve.did(0, "lb"))
            dve.wait_ge(*setup_dve.at(0, "lb"))
            v.memset(cf[:, 2, :], -1.0).then_inc(*setup_dve.did(0, "one"))
            dve.wait_ge(*setup_dve.at(0, "one"))

            cacc = XROW
            muls = [0]

            for l in range(DEPTH):
                norm(3 * l)
                v.memset(XP[:, :, 0:3], 0.0)
                for i in range(2):
                    v.memset(mlq[64 * i + 32:64 * i + 64, :, :], 0.0)
                    last = v.memset(mlk[64 * i + 32:64 * i + 64, :, :], 0.0)
                last.then_inc(*pads.did(l, "zero"))
                dve.wait_ge(*pads.at(l, "zero"))
                dve.wait_ge(layer_in, PER_L_IN * (l + 1))

                def conv(g):
                    cw = pr(l, "scw" if g else "gcw").rearrange("p (c j) -> p c j", c=6)
                    cb = pr(l, "scb" if g else "gcb")
                    if g:
                        dve.wait_ge(conv_tap, 96 * l + 48)
                        dve.wait_ge(conv_new, 4 * l + 2)
                    samp = XP[:, :, 3 + SEQ:XPW].rearrange("p c (b t) -> p c b t", b=NB)
                    for c in range(6):
                        last = v.tensor_copy(samp[:, c, :, 0:3], sconv[:, g, c, :, :])
                    last.then_inc(halo, 1)
                    dve.wait_ge(halo, 2 * l + g + 1)
                    for c in range(6):
                        m = (2 * l + g) * 6 + c
                        dve.wait_ge(proj_ev, 30 * l + (24 if g else 0) + c + 1)
                        if m >= 2:
                            dve.wait_ge(conv_silu, m - 1)
                        if c == 0 and g == 0 and l:
                            dve.wait_ge(*ml_dve.at(l - 1, "br"))
                        ap_, as_ = cacc[:, m % 2, 0:SEQ], cacc[:, m % 2, SEQ:T].rearrange("p (b t) -> p b t", b=NB)
                        for j in range(4):
                            if j:
                                dve.wait_ge(conv_tap, 8 * m + 2 * j - 1)
                            if j == 0:
                                v.tensor_scalar(ap_, XP[:, c, 0:SEQ], cw[:, c, 0:1], cb[:, c:c + 1], ALU.mult, ALU.add).then_inc(conv_tap, 1)
                                v.tensor_scalar(as_, samp[:, c, :, 0:DS], cw[:, c, 0:1], cb[:, c:c + 1], ALU.mult, ALU.add).then_inc(conv_tap, 1)
                            else:
                                v.scalar_tensor_tensor(out=ap_, in0=XP[:, c, j:j + SEQ], scalar=cw[:, c, j:j + 1], in1=ap_,
                                                       op0=ALU.mult, op1=ALU.add).then_inc(conv_tap, 1)
                                dve.wait_ge(conv_tap, 8 * m + 2 * j)
                                v.scalar_tensor_tensor(out=as_, in0=samp[:, c, :, j:j + DS], scalar=cw[:, c, j:j + 1], in1=as_,
                                                       op0=ALU.mult, op1=ALU.add).then_inc(conv_tap, 1)
                    v.tensor_copy(cs[:, g, :, 0, :], XP[:, :, SEQ:SEQ + 3]).then_inc(conv_new, 1)
                    for c in range(6):
                        last = v.tensor_copy(cs[:, g, c, 1:, :], samp[:, c, :, DS:DS + 3])
                    last.then_inc(conv_new, 1)

                conv(0)
                conv(1)

                dve.wait_ge(*gp_pe.at(l, "small"))
                SMP = Q1[:, 0, 0:50].rearrange("p (b g q) -> p g q b", b=NBLK, g=5)
                gb = pr(l, "gb").rearrange("p (g q) -> p g q", g=5)
                v.tensor_tensor(smb[:, :, :, :], SMP, gb.unsqueeze(3).to_broadcast([128, 5, 2, NBLK]), ALU.add).then_inc(*gp_dve.did(l, "smb"))
                dve.wait_ge(*gp_dve.at(l, "smb"))
                smf = smb[:, :, :, :].rearrange("p g q b -> p (g q b)")
                w = 2 * NBLK
                spi, e_, u1, ln, d = sp3[:, 0, :], sp3[:, 2, :], sp3[:, 3, :], sp3[:, 4, :], sp3[:, 5, :]
                v.tensor_copy(spi[:, 0:2 * w], smf[:, w:3 * w]).then_inc(*gp_dve.did(l, "spc"))
                dve.wait_ge(*gp_dve.at(l, "spc"))
                v.tensor_scalar(spi[:, 2 * w:3 * w], smf[:, 4 * w:5 * w], -1.0, None, ALU.mult).then_inc(*gp_dve.did(l, "spi"))
                dve.wait_ge(*gp_dve.at(l, "spi"))
                dve.wait_ge(*gp_act.at(l, "e"))
                v.tensor_scalar(u1, e_, 1.0, None, ALU.add).then_inc(*gp_dve.did(l, "u1"))
                dve.wait_ge(*gp_dve.at(l, "u1"))
                v.tensor_scalar(d, u1, -1.0, None, ALU.add).then_inc(*gp_dve.did(l, "d"))
                dve.wait_ge(*gp_dve.at(l, "d"))
                z = sp3[:, 1, :]
                v.tensor_scalar(z, d, 0.0, None, ALU.is_equal).then_inc(*gp_dve.did(l, "z"))
                dve.wait_ge(*gp_dve.at(l, "z"))
                dve.wait_ge(*gp_act.at(l, "ln"))
                v.tensor_tensor(d, d, z, ALU.add).then_inc(*gp_dve.did(l, "dz"))
                dve.wait_ge(*gp_dve.at(l, "dz"))
                v.tensor_tensor(ln, ln, z, ALU.add).then_inc(*gp_dve.did(l, "lz"))
                dve.wait_ge(*gp_dve.at(l, "lz"))
                v.reciprocal(d, d).then_inc(*gp_dve.did(l, "rd"))
                dve.wait_ge(*gp_dve.at(l, "rd"))
                v.tensor_tensor(ln, ln, e_, ALU.mult).then_inc(*gp_dve.did(l, "le"))
                dve.wait_ge(*gp_dve.at(l, "le"))
                v.tensor_tensor(ln, ln, d, ALU.mult).then_inc(*gp_dve.did(l, "lp"))
                dve.wait_ge(*gp_dve.at(l, "lp"))
                v.scalar_tensor_tensor(out=spi, in0=spi, scalar=0.0, in1=ln, op0=ALU.max, op1=ALU.add).then_inc(*gp_dve.did(l, "sp"))
                dve.wait_ge(*gp_dve.at(l, "sp"))
                dve.wait_ge(*gp_act.at(l, "ea"))
                v.tensor_scalar(cf[:, 0:2, :], sm1[:, :, 0:2], -1.0, None, ALU.mult).then_inc(*gp_dve.did(l, "cf"))
                dve.wait_ge(*gp_dve.at(l, "cf"))
                v.tensor_tensor(G[:, :, :].rearrange("p b g -> p g b"), spi.rearrange("p (g b) -> p g b", b=NBLK),
                                cf[:, :, :].rearrange("p m q -> p (m q)").unsqueeze(2).to_broadcast([128, 6, NBLK]),
                                ALU.mult).then_inc(*gp_dve.did(l, "G"))
                dve.wait_ge(*gp_dve.at(l, "G"))
                dt = spi[:, w:2 * w].rearrange("p (q b) -> p q b", q=2)
                dve.wait_ge(*gp_pe.at(l, "gam"))
                v.tensor_copy(gt[:, :, :, :], Q1[:, 1, 0:60].rearrange("p (w b g) -> p w b g", w=2, b=NBLK)).then_inc(*gp_dve.did(l, "gt"))
                dve.wait_ge(*gp_dve.at(l, "gt"))
                dve.wait_ge(*gp_pe.at(l, "ig"))
                dve.wait_ge(*gp_act.at(l, "gr2"))
                dve.wait_ge(conv_silu, 12 * (l + 1))
                v.tensor_tensor(XROW, Q2[:, :, 0:T], GR[2], ALU.subtract).then_inc(*gp_dve.did(l, "xrow"))
                dve.wait_ge(*gp_dve.at(l, "xrow"))

                def decay(steps, act_, D, m):
                    v.tensor_tensor(bt(D), bt(GR[m]), bcol(gcol(gt, 0, m)), ALU.subtract).then_inc(*steps.did(l, "dsub"))
                    dve.wait_ge(*steps.at(l, "dsub"))
                    v.tensor_scalar(D, D, 0.0, None, ALU.min).then_inc(*steps.did(l, "dmin"))
                    dve.wait_ge(*steps.at(l, "dmin"))
                    dve.wait_ge(*act_.at(l, "dexp"))
                    v.tensor_tensor(D, D, TRIM.unsqueeze(1).to_broadcast([128, 2, T]), ALU.mult).then_inc(*steps.did(l, "D"))
                    dve.wait_ge(*steps.at(l, "D"))

                def norm_gate(steps, act_, o, rn, w_, z_, br):
                    dve.wait_ge(*act_.at(l, "root"))
                    v.reciprocal(rn, rn).then_inc(*steps.did(l, "rn2"))
                    dve.wait_ge(*steps.at(l, "rn2"))
                    v.tensor_tensor(o, o, rn, ALU.mult).then_inc(*steps.did(l, "on"))
                    dve.wait_ge(*steps.at(l, "on"))
                    v.scalar_tensor_tensor(out=BR[:, br], in0=o, scalar=w_, in1=z_, op0=ALU.mult, op1=ALU.mult)\
                     .then_inc(*steps.did(l, "br"))
                    dve.wait_ge(*steps.at(l, "br"))

                C = C6[0]
                LT, QKD, VB, KB, KW, Tm, U, W, AL, SV, SKT = [tt(i) for i in (3, 4, 5, 6, 7, 8, 9, 10, 11, 0, 1)]
                QE, UU, D = tt(2), tt(12), tt(2)
                sq4 = sl(0, 2).rearrange("p (c t) -> p c t", c=4)
                dve.wait_ge(*gd_act.at(l, "rootk"))
                v.reciprocal(sq4, sq4).then_inc(*gd_dve.did(l, "rn"))
                dve.wait_ge(*gd_dve.at(l, "rn"))
                v.tensor_tensor(C[:, 0:4, :], C[:, 0:4, :], sq4, ALU.mult).then_inc(*gd_dve.did(l, "qk"))
                dve.wait_ge(*gd_dve.at(l, "qk"))
                decay(gd_dve, gd_act, D, 0)
                dve.wait_ge(*gp_act.at(l, "egt"))
                v.tensor_tensor(sm1[:, :, :], beta[:, :, :], gcol(egt, 0, 0), ALU.mult).then_inc(*gd_dve.did(l, "bg"))
                dve.wait_ge(*gd_dve.at(l, "bg"))
                dve.wait_ge(*gd_pe.at(l, "ktok"))
                v.tensor_tensor(bt(KB), bt(Q0[:, :, 0:T]), bcol(sm1[:, :, :]), ALU.mult).then_inc(*gd_dve.did(l, "kb"))
                dve.wait_ge(*gd_dve.at(l, "kb"))
                v.tensor_tensor(bt(KW), bt(Q0[:, :, 0:T]), bcol(gcol(egt, 1, 0)), ALU.mult).then_inc(*gd_dve.did(l, "kw"))
                dve.wait_ge(*gd_dve.at(l, "kw"))
                dve.wait_ge(*gd_pe.at(l, "vtok"))
                v.tensor_tensor(bt(VB), bt(Q1[:, :, 0:T]), bcol(beta[:, :, :]), ALU.mult).then_inc(*gd_dve.did(l, "vb"))
                dve.wait_ge(*gd_dve.at(l, "vb"))
                dve.wait_ge(*gd_pe.at(l, "kk"))
                v.tensor_tensor(LT, Q2[:, :, 0:T], D, ALU.mult).then_inc(*gd_dve.did(l, "lt"))
                dve.wait_ge(*gd_dve.at(l, "lt"))
                dve.wait_ge(*gd_pe.at(l, "qk"))
                v.tensor_tensor(QKD, Q0[:, :, 0:T], D, ALU.mult).then_inc(*gd_dve.did(l, "qkd"))
                dve.wait_ge(*gd_dve.at(l, "qkd"))
                for i in range(2):
                    idl = ID[LN[i], LN[i]].unsqueeze(1).unsqueeze(1).to_broadcast([64, 2, NBLK, 64])
                    v.tensor_copy(bt(Tm)[LN[i]], idl)
                    last = v.tensor_copy(bt(U)[LN[i]], idl)
                last.then_inc(*gd_dve.did(l, "init"))
                dve.wait_ge(*gd_dve.at(l, "init"))
                dve.wait_ge(*gd_act.at(l, "egrow"))
                v.tensor_tensor(QE, C[:, 0:2, :], GR[0], ALU.mult).then_inc(*gd_dve.did(l, "qe"))
                dve.wait_ge(*gd_dve.at(l, "qe"))
                for j in range(6):
                    nb = NBLK if j < 3 else NPB
                    n = nb * BL
                    dve.wait_ge(*gd_dve.at(l, "qe"))
                    v.tensor_tensor(bt(AL)[:, :, 0:NPB, :], bt(LT)[:, :, 0:NPB, :],
                                    LM[:, 0, j, :].unsqueeze(1).unsqueeze(1).to_broadcast([128, 2, NPB, BL]), ALU.mult)
                    last = v.tensor_tensor(AL[:, :, SEQ:T], LT[:, :, SEQ:T], LM[:, 1, j, :].unsqueeze(1).to_broadcast([128, 2, BL]), ALU.mult)
                    last.then_inc(*gd_dve.did(l, f"al{j}"))
                    dve.wait_ge(*gd_dve.at(l, f"al{j}"))
                    dve.wait_ge(*gd_pe.at(l, f"w{j}"))
                    v.tensor_tensor(bt(W)[:, :, 0:nb], bt(Q0[:, :, 0:T])[:, :, 0:nb], bcol(beta[:, :, :])[:, :, 0:nb], ALU.mult)\
                     .then_inc(*gd_dve.did(l, f"wb{j}"))
                    dve.wait_ge(*gd_dve.at(l, f"wb{j}"))
                    dve.wait_ge(*gd_pe.at(l, f"tu{j}"))
                    v.tensor_tensor(Tm[:, :, 0:n], Tm[:, :, 0:n], Q1[:, :, 0:n], ALU.subtract).then_inc(*gd_dve.did(l, f"t{j}"))
                    dve.wait_ge(*gd_dve.at(l, f"t{j}"))
                    v.tensor_tensor(U[:, :, 0:n], U[:, :, 0:n], Q2[:, :, 0:n], ALU.subtract).then_inc(*gd_dve.did(l, f"u{j}"))
                    dve.wait_ge(*gd_dve.at(l, f"u{j}"))
                dve.wait_ge(*gd_pe.at(l, "sv"))
                v.tensor_copy(SV, Q1[:, :, 0:T]).then_inc(*gd_dve.did(l, "sv"))
                dve.wait_ge(*gd_dve.at(l, "sv"))
                v.memset(Sp[:, 0, :, 0:64], 0.0).then_inc(*gd_dve.did(l, "zero"))
                dve.wait_ge(*gd_dve.at(l, "zero"))
                EG = GR[0]

                def state(c, steps, pe_, dcol, q1=Q1, w=64, o=0):
                    dve.wait_ge(*pe_.at(l, f"k{c}"))
                    for q in range(2):
                        last = v.scalar_tensor_tensor(out=Sp[:, (c + 1) % 2, q, 0:w], in0=Sp[:, c % 2, q, 0:w], scalar=dcol(q, c),
                                                      in1=q1[:, q, o:o + w], op0=ALU.mult, op1=ALU.add)
                        if steps is ml_dve:
                            last = v.scalar_tensor_tensor(out=nst[:, (c + 1) % 2, q:q + 1], in0=nst[:, c % 2, q:q + 1],
                                                          scalar=dcol(q, c), in1=q1[:, q, 64:65], op0=ALU.mult, op1=ALU.add)
                    last.then_inc(*steps.did(l, f"s{c}"))
                    dve.wait_ge(*steps.at(l, f"s{c}"))

                def end_col(EG):
                    return lambda q, c: EG[:, q, (c + 1) * BL - 1:(c + 1) * BL]

                for c in range(NPB):
                    dve.wait_ge(*gd_pe.at(l, f"p{c}"))
                    v.tensor_tensor(UU[:, :, tk(c)], SV[:, :, tk(c)], Q2[:, :, 0:64], ALU.subtract).then_inc(*gd_dve.did(l, f"u{c}_"))
                    dve.wait_ge(*gd_dve.at(l, f"u{c}_"))
                    state(c, gd_dve, gd_pe, end_col(EG))
                SX = sl(5, 2)[:, 0:1024].rearrange("p (q b t) -> p q b t", q=2, b=NB)
                UX = sl(10, 2)[:, 0:1024].rearrange("p (q b t) -> p q b t", q=2, b=NB)
                dve.wait_ge(*gd_act.at(l, "skt"))

                def spread_t(out, src):
                    return v.tensor_tensor(out, src[:, :, SEQ:T].unsqueeze(2).to_broadcast([128, 2, NB, 64]),
                                           BT.unsqueeze(1).to_broadcast([128, 2, NB, 64]), ALU.mult)

                def spread_s(out, src):
                    return v.tensor_tensor(out, src[:, :, SEQ:T].unsqueeze(2).to_broadcast([128, 2, NB, 64]),
                                           BM.unsqueeze(1).unsqueeze(3).to_broadcast([128, 2, NB, 64]), ALU.mult)

                spread_t(SX, SKT).then_inc(*gd_dve.did(l, "sx"))
                dve.wait_ge(*gd_dve.at(l, "sx"))
                dve.wait_ge(*gd_pe.at(l, "ps"))
                v.tensor_tensor(UU[:, :, SEQ:T], SV[:, :, SEQ:T], Q2[:, :, 0:64], ALU.subtract).then_inc(*gd_dve.did(l, "us"))
                dve.wait_ge(*gd_dve.at(l, "us"))
                spread_s(UX, UU).then_inc(*gd_dve.did(l, "ux"))
                dve.wait_ge(*gd_dve.at(l, "ux"))

                def sample_state(steps, pe_, S, dec, q1=Q1):
                    dve.wait_ge(*pe_.at(l, "ks"))
                    v.tensor_tensor(S[:, :, :, :], S[:, :, :, :], dec.unsqueeze(3).to_broadcast([128, 2, NB, 64]), ALU.mult)\
                     .then_inc(*steps.did(l, "sd"))
                    dve.wait_ge(*steps.at(l, "sd"))
                    return v.tensor_tensor(S[:, :, :, :], S[:, :, :, :], q1[:, :, :].rearrange("p q (b v) -> p q b v", b=NB), ALU.add)

                sample_state(gd_dve, gd_pe, stg, EG[:, :, SEQ + DS - 1::DS]).then_inc(*gd_dve.did(l, "ss"))
                dve.wait_ge(*gd_dve.at(l, "ss"))
                v.tensor_copy(tt(9), Q0[:, :, 0:T]).then_inc(*gd_dve.did(l, "o"))
                dve.wait_ge(*gd_dve.at(l, "o"))
                norm_gate(gd_dve, gd_act, tt(9), tt(8), pr(l, "gnorm"), gz, 0)
                dve.wait_ge(*gd_dve.at(l, "br"))

                for q in range(2):
                    last = v.tensor_scalar(sf[:, q, :], sf[:, q, :], lbv[:, l, 1, q:q + 1], lbv[:, l, 0, q:q + 1], ALU.mult, ALU.add)
                last.then_inc(*hg_dve.did(l, "pre"))
                dve.wait_ge(*hg_dve.at(l, "pre"))
                for q in range(2):
                    last = v.tensor_scalar(sfn[:, q, :], sfn[:, q, :], lbv[:, l, 1, q:q + 1], None, ALU.mult)
                last.then_inc(*hg_dve.did(l, "kin"))
                dve.wait_ge(*hg_dve.at(l, "kin"))
                ATT, QEh, KWC = tt(2), tt(3), tt(4)
                X = sl(6, 2)[:, 0:1024].rearrange("p (r j t) -> p r j t", r=2, j=8)
                ZQ = sl(8, 2)[:, 0:768].rearrange("p (r j t) -> p r j t", r=2, j=6)
                ZK = sl(10, 2)[:, 0:768].rearrange("p (r j t) -> p r j t", r=2, j=6)
                MA = sl(12)[:, 0:448].rearrange("p (j t) -> p j t", j=7)
                for n in range(11):
                    if n < 10:
                        b, q = n // 2, n % 2
                        dve.wait_ge(*hg_act.at(l, f"x{n}"))
                        if n >= 2:
                            dve.wait_ge(*hg_pe.at(l, f"a{n - 2}"))
                        kb_, qb_ = sfn[:, q, tk(b)].unsqueeze(1), hgq[:, q, tk(b)].unsqueeze(1)
                        v.tensor_tensor(ZK[:, n % 2], X[:, n % 2, 0:6, :], kb_.to_broadcast([128, 6, BL]), ALU.mult)
                        v.tensor_tensor(ZQ[:, n % 2], X[:, n % 2, 0:6, :], qb_.to_broadcast([128, 6, BL]), ALU.mult)
                        v.tensor_tensor(QEh[:, q, tk(b)], X[:, n % 2, 6, :], hgq[:, q, tk(b)], ALU.mult)
                        v.tensor_tensor(KWC[:, q, tk(b)], X[:, n % 2, 7, :], sfn[:, q, tk(b)], ALU.mult).then_inc(*hg_dve.did(l, f"z{n}"))
                        dve.wait_ge(*hg_dve.at(l, f"z{n}"))
                    if n:
                        n, b, q = n - 1, (n - 1) // 2, (n - 1) % 2
                        dve.wait_ge(*hg_pe.at(l, f"a{n}"))
                        v.tensor_tensor(MA, Q1[:, n % 2, 0:448].rearrange("p (j t) -> p j t", j=7), LM[:, kind(b), :, :], ALU.mult)\
                         .then_inc(*hg_dve.did(l, f"m{n}"))
                        dve.wait_ge(*hg_dve.at(l, f"m{n}"))
                        v.tensor_reduce(ATT[:, q, tk(b)], MA.rearrange("p j t -> p t j"), AX.X, ALU.add).then_inc(*hg_dve.did(l, f"r{n}"))
                        dve.wait_ge(*hg_dve.at(l, f"r{n}"))
                dve.wait_ge(out_sem, 16 * (13 * l + 2))
                v.memset(Sp[:, 0, :, 0:64], 0.0).then_inc(*hg_dve.did(l, "zero"))
                dve.wait_ge(*hg_dve.at(l, "zero"))
                dve.wait_ge(*hg_act.at(l, "e9"))
                for c in range(NPB):
                    state(c, hg_dve, hg_pe, lambda q, c: egc[:, q, c:c + 1])
                spread_s(UX, tt(1)).then_inc(*hg_dve.did(l, "ux"))
                dve.wait_ge(*hg_dve.at(l, "ux"))
                sample_state(hg_dve, hg_pe, sth, egc[:, :, NPB:]).then_inc(*hg_dve.did(l, "ss"))
                dve.wait_ge(*hg_dve.at(l, "ss"))
                v.tensor_copy(tt(6), Q0[:, :, 0:T]).then_inc(*hg_dve.did(l, "o"))
                dve.wait_ge(*hg_dve.at(l, "o"))
                norm_gate(hg_dve, hg_act, tt(6), tt(8), pr(l, "hnorm"), hgg, 1)
                dve.wait_ge(*hg_dve.at(l, "br"))

                C = C6[1]
                XT, XW, AT, D = tt(0), tt(1), tt(2), tt(3)
                XWX = sl(6, 2)[:, 0:1024].rearrange("p (q b t) -> p q b t", q=2, b=NB)
                decay(sd_dve, sd_act, D, 1)
                v.tensor_tensor(sm1[:, :, :], dt, gcol(egt, 1, 1), ALU.mult).then_inc(*sd_dve.did(l, "wdt"))
                dve.wait_ge(*sd_dve.at(l, "wdt"))
                dve.wait_ge(*sd_pe.at(l, "xtok"))
                v.tensor_tensor(bt(XW), bt(Q0[:, :, 0:T]), bcol(sm1[:, :, :]), ALU.mult).then_inc(*sd_dve.did(l, "xw"))
                dve.wait_ge(*sd_dve.at(l, "xw"))
                dve.wait_ge(*sd_pe.at(l, "cb"))
                v.tensor_tensor(AT, Q0[:, :, 0:T], D, ALU.mult).then_inc(*sd_dve.did(l, "att0"))
                dve.wait_ge(*sd_dve.at(l, "att0"))
                v.tensor_tensor(bt(AT), bt(AT), bcol(dt), ALU.mult).then_inc(*sd_dve.did(l, "att"))
                dve.wait_ge(*sd_dve.at(l, "att"))
                spread_s(XWX, XW).then_inc(*sd_dve.did(l, "xx"))
                dve.wait_ge(*sd_dve.at(l, "xx"))
                dve.wait_ge(out_sem, 16 * (13 * l + 4))
                v.memset(Sp[:, 0, :, :], 0.0).then_inc(*sd_dve.did(l, "zero"))
                dve.wait_ge(*sd_dve.at(l, "zero"))
                dve.wait_ge(*sd_act.at(l, "egrow"))
                EG = GR[1]
                for c in range(NPB):
                    state(c, sd_dve, sd_pe, end_col(EG), Q2, 128, 128)
                for q in range(2):
                    dve.wait_ge(*sd_pe.at(l, f"k_{q}"))
                    v.tensor_tensor(sts[:, q], sts[:, q], EG[:, q, SEQ + DS - 1::DS].unsqueeze(2).to_broadcast([128, NB, 128]), ALU.mult)\
                     .then_inc(*sd_dve.did(l, f"sd{q}"))
                    dve.wait_ge(*sd_dve.at(l, f"sd{q}"))
                    v.tensor_tensor(sts[:, q], sts[:, q], Q2[:, :, :].rearrange("p a (b n) -> p (a b) n", n=128), ALU.add)\
                     .then_inc(*sd_dve.did(l, f"ss{q}"))
                    dve.wait_ge(*sd_dve.at(l, f"ss{q}"))
                Y = tt(9)
                v.tensor_tensor(Y, Q1[:, :, 0:T], EG, ALU.mult).then_inc(*sd_dve.did(l, "y0"))
                dve.wait_ge(*sd_dve.at(l, "y0"))
                v.tensor_tensor(Y, Y, Q0[:, :, 0:T], ALU.add).then_inc(*sd_dve.did(l, "y1"))
                dve.wait_ge(*sd_dve.at(l, "y1"))
                for q in range(2):
                    last = v.scalar_tensor_tensor(out=Y[:, q, :], in0=C[:, q, :], scalar=pr(l, "ssd_d")[:, q:q + 1], in1=Y[:, q, :],
                                                  op0=ALU.mult, op1=ALU.add)
                last.then_inc(*sd_dve.did(l, "y2"))
                dve.wait_ge(*sd_dve.at(l, "y2"))
                v.tensor_tensor(Y, Y, sz, ALU.mult).then_inc(*sd_dve.did(l, "yz"))
                dve.wait_ge(*sd_dve.at(l, "yz"))
                dve.wait_ge(*sd_act.at(l, "root"))
                v.reciprocal(tt(8)[:, 0, :], tt(8)[:, 0, :]).then_inc(*sd_dve.did(l, "rn2"))
                dve.wait_ge(*sd_dve.at(l, "rn2"))
                for q in range(2):
                    last = v.scalar_tensor_tensor(out=BR[:, 2, q, :], in0=Y[:, q, :], scalar=pr(l, "snorm")[:, q:q + 1],
                                                  in1=tt(8)[:, 0, :], op0=ALU.mult, op1=ALU.mult)
                last.then_inc(*sd_dve.did(l, "br"))
                dve.wait_ge(*sd_dve.at(l, "br"))

                MR = tt(1)
                v.memset(mm[:, 0, :], 0.0).then_inc(*ml_dve.did(l, "m0"))
                dve.wait_ge(*ml_dve.at(l, "m0"))
                for c in range(NPB):
                    dve.wait_ge(*ml_dve.at(l, f"mm{c - 1}" if c else "m0"))
                    for q in range(2):
                        last = v.tensor_tensor_scan(MR[:, q, tk(c)], ONES[:, 0:BL], XROW[:, q, tk(c)], mm[:, c, q:q + 1], ALU.mult, ALU.max)
                    last.then_inc(*ml_dve.did(l, f"sc{c}"))
                    dve.wait_ge(*ml_dve.at(l, f"sc{c}"))
                    e0 = (c + 1) * BL - 1
                    v.tensor_tensor(mm[:, c + 1, :], MR[:, :, e0], GR[2][:, :, e0], ALU.add).then_inc(*ml_dve.did(l, f"mm{c}"))
                    dve.wait_ge(*ml_dve.at(l, f"mm{c}"))
                first = XROW[:, :, SEQ::DS]
                v.tensor_tensor(first, first, stmm[:, :, :], ALU.max).then_inc(*ml_dve.did(l, "inj"))
                dve.wait_ge(*ml_dve.at(l, "inj"))
                for q in range(2):
                    last = v.tensor_tensor_scan(MR[:, q, SEQ:T], RESET[:, :], XROW[:, q, SEQ:T], -3.0e38, ALU.add, ALU.max)
                last.then_inc(*ml_dve.did(l, "scs"))
                dve.wait_ge(*ml_dve.at(l, "scs"))
                ends = slice(SEQ + DS - 1, T, DS)
                v.tensor_tensor(mms[:, :, :], MR[:, :, ends], GR[2][:, :, ends], ALU.add).then_inc(*ml_dve.did(l, "mms"))
                dve.wait_ge(*ml_dve.at(l, "mms"))
                WT, QW, KWm, WIN, EMT = tt(2), tt(3), tt(4), tt(5), tt(6)
                v.tensor_tensor(xtk[:, :, :], smb[:, 3, :, :], gcol(gt, 0, 2), ALU.subtract).then_inc(*ml_dve.did(l, "xtk"))
                dve.wait_ge(*ml_dve.at(l, "xtk"))
                v.tensor_tensor(bt(WT), bcol(xtk[:, :, :]), bt(MR), ALU.subtract).then_inc(*ml_dve.did(l, "sub"))
                dve.wait_ge(*ml_dve.at(l, "sub"))
                v.tensor_scalar(WT, WT, 0.0, None, ALU.min).then_inc(*ml_dve.did(l, "min"))
                dve.wait_ge(*ml_dve.at(l, "min"))
                v.tensor_tensor(msel[:, :, :], MR[:, :, ends], BM.unsqueeze(1).to_broadcast([128, 2, NB]), ALU.mult).then_inc(*ml_dve.did(l, "selm"))
                dve.wait_ge(*ml_dve.at(l, "selm"))
                v.tensor_reduce(wend[:, :, NPB:NBLK], msel[:, :, :], AX.X, ALU.add).then_inc(*ml_dve.did(l, "sel"))
                dve.wait_ge(*ml_dve.at(l, "sel"))
                v.tensor_tensor(wend[:, :, 0:NPB], xtk[:, :, 0:NPB], MR[:, :, BL - 1:SEQ:BL], ALU.subtract)
                v.tensor_tensor(wend[:, :, NPB:], xtk[:, :, NPB:], wend[:, :, NPB:], ALU.subtract).then_inc(*ml_dve.did(l, "we0"))
                dve.wait_ge(*ml_dve.at(l, "we0"))
                v.tensor_tensor(bt(WIN)[:, :, 0:NPB, :], mm[:, 0:NPB, :].rearrange("p c q -> p q c").unsqueeze(3).to_broadcast([128, 2, NPB, BL]),
                                bt(MR)[:, :, 0:NPB, :], ALU.subtract)
                v.tensor_tensor(WIN[:, :, SEQ:T].rearrange("p q (b t) -> p q b t", b=NB), stmm[:, :, :].unsqueeze(3).to_broadcast([128, 2, NB, DS]),
                                MR[:, :, SEQ:T].rearrange("p q (b t) -> p q b t", b=NB), ALU.subtract).then_inc(*ml_dve.did(l, "wpre"))
                dve.wait_ge(*ml_dve.at(l, "wpre"))
                v.tensor_tensor(EMT, MR, GR[2], ALU.add).then_inc(*ml_dve.did(l, "mt"))
                dve.wait_ge(*ml_dve.at(l, "mt"))
                dve.wait_ge(*ml_act.at(l, "win"))
                v.tensor_tensor(QW, mlq, WIN, ALU.mult).then_inc(*ml_dve.did(l, "qw"))
                dve.wait_ge(*ml_dve.at(l, "qw"))
                dve.wait_ge(*ml_act.at(l, "wexp"))
                v.tensor_tensor(WT, WT, TRIM.unsqueeze(1).to_broadcast([128, 2, T]), ALU.mult).then_inc(*ml_dve.did(l, "wt0"))
                dve.wait_ge(*ml_dve.at(l, "wt0"))
                dve.wait_ge(*ml_pe.at(l, "kq"))
                v.tensor_tensor(WT, WT, Q2[:, :, 0:T], ALU.mult).then_inc(*ml_dve.did(l, "wt"))
                dve.wait_ge(*ml_dve.at(l, "wt"))
                dve.wait_ge(*ml_act.at(l, "wend"))
                v.tensor_tensor(bt(KWm), bt(Q1[:, :, 0:T]), bcol(wend[:, :, :]), ALU.mult).then_inc(*ml_dve.did(l, "kw"))
                dve.wait_ge(*ml_dve.at(l, "kw"))
                v.memset(nst[:, 0, :], 0.0).then_inc(*ml_dve.did(l, "kw0"))
                dve.wait_ge(*ml_dve.at(l, "kw0"))
                dve.wait_ge(out_sem, 16 * (13 * l + 6))
                v.memset(Sp[:, 0, :, 0:64], 0.0).then_inc(*ml_dve.did(l, "zero"))
                dve.wait_ge(*ml_dve.at(l, "zero"))
                for c in range(NPB):
                    state(c, ml_dve, ml_pe, end_col(WIN))
                dve.wait_ge(*ml_act.at(l, "vt"))
                spread_s(UX, tt(0)).then_inc(*ml_dve.did(l, "ux"))
                dve.wait_ge(*ml_dve.at(l, "ux"))
                sample_state(ml_dve, ml_pe, stm, WIN[:, :, ends])
                v.tensor_tensor(stn[:, :, :], stn[:, :, :], WIN[:, :, ends], ALU.mult).then_inc(*ml_dve.did(l, "sn0"))
                dve.wait_ge(*ml_dve.at(l, "sn0"))
                v.tensor_tensor(stn[:, :, :], stn[:, :, :], PJ[:, :, 0:NB], ALU.add).then_inc(*ml_dve.did(l, "ss"))
                dve.wait_ge(*ml_dve.at(l, "ss"))
                v.tensor_copy(tt(9), Q0[:, :, 0:T]).then_inc(*ml_dve.did(l, "o"))
                dve.wait_ge(*ml_dve.at(l, "o"))
                dve.wait_ge(*ml_act.at(l, "dab"))
                v.tensor_tensor(tt(7), tt(7), EMT, ALU.max).then_inc(*ml_dve.did(l, "dmx"))
                dve.wait_ge(*ml_dve.at(l, "dmx"))
                v.reciprocal(tt(7), tt(7)).then_inc(*ml_dve.did(l, "drc"))
                dve.wait_ge(*ml_dve.at(l, "drc"))
                v.tensor_tensor(tt(9), tt(9), tt(7), ALU.mult).then_inc(*ml_dve.did(l, "oo"))
                dve.wait_ge(*ml_dve.at(l, "oo"))
                norm_gate(ml_dve, ml_act, tt(9), tt(8), pr(l, "mnorm"), mlo, 3)
                dve.wait_ge(*ml_dve.at(l, "br"))

                def gated(g0, dst, first):
                    for t in range(KT):
                        dve.wait_ge(gat_act, 16 * g0 + 8 + t + 1)
                        if first:
                            v.tensor_tensor(dst[:, t, :], sgs[:, t % 4, :], prod[:, t, :], ALU.mult).then_inc(gat_dve, 1)
                        else:
                            v.tensor_tensor(sgs[:, t % 4, :], sgs[:, t % 4, :], prod[:, t, :], ALU.mult).then_inc(gat_mul, 1)
                            muls[0] += 1
                            dve.wait_ge(gat_mul, muls[0])
                            v.tensor_tensor(dst[:, t, :], dst[:, t, :], sgs[:, t % 4, :], ALU.add).then_inc(gat_dve, 1)

                for n in range(4):
                    gated(5 * l + n, merged, n == 0)
                for t in range(8):
                    if t % 2 == 0:
                        dve.wait_ge(out_pe, 4 * l + t // 2 + 1)
                    else:
                        dve.wait_ge(slab_done, BASE[l] + N_PROJ + N_GATED + t // 2 + 1)
                    last = v.tensor_tensor(h[:, t, :], h[:, t, :], PJ[:, t % 2, 0:T], ALU.add).then_inc(out_ev, 1)
                dve.wait_ge(out_ev, 8 * l + 8)
                dve.sem_inc(h_done, 1)
                norm(3 * l + 1)

                n3 = BASE[l] + N_PROJ + N_GATED + N_OUT

                def choose(out, i, x, name, weighted):
                    for t, (t0, t1) in enumerate(TT):
                        w = t1 - t0
                        last = v.tensor_scalar(out[0:w, t, :], IOTA[0:w, 0:CAP], RK[0:w, t, bass.ds(i, 1)],
                                               CB[0:w, t, bass.ds(i, 1)] if weighted else None, ALU.is_equal,
                                               *([ALU.mult] if weighted else []))
                    last.then_inc(x[name], 1)

                def expert(e, x, n0, c0, turn0):
                    dve.wait_ge(x["selt_pe"], e + c0)
                    choose(selw, e + turn0, x, "selw", True)
                    dve.wait_ge(x["xg_pe"], e + c0)
                    choose(sel, e + (turn0 + 1), x, "sel", False)
                    for c in range(CH):
                        dve.wait_ge(x["silu"], e * CH + (c0 * CH + c + 1))
                        dve.wait_ge(x["slab_done"], e * N_XV + (n0 + 2 * c + 2))
                        v.tensor_tensor(hidx[:, 2 * c:2 * c + 2, :], sgx[:, c % 2, :].rearrange("p (f t) -> p f t", f=2),
                                        (Q0, Q1)[c % 2][:, 1, 0:2 * CAP].rearrange("p (f t) -> p f t", f=2), ALU.mult).then_inc(x["hid"], 1)
                    for t in range(KT):
                        dve.wait_ge(x["scat"], e * KT + (c0 * KT + t + 1))
                        v.tensor_tensor(h[:, t, :], h[:, t, :], PJ[:, t % 2, 0:T], ALU.add).then_inc(x["hadd"], 1)
                    dve.wait_ge(x["hadd"], e * KT + (c0 * KT + KT))

                if l == 0:
                    for c in range(CH):
                        dve.wait_ge(ff_act, c + 1)
                        dve.wait_ge(slab_done, n3 + 2 * c + 2)
                        v.tensor_tensor(hid[:, 2 * c:2 * c + 2, :], ffs[:, c % 2], (Q1, Q2)[c % 2][:, :, 0:T], ALU.mult).then_inc(ff_dve, 1)
                    for t in range(8):
                        if t % 2 == 0:
                            last_d = max(d for d, x in enumerate(DOWN) if x[0] == t // 2)
                            dve.wait_ge(slab_done, n3 + FT + last_d + 1)
                        v.tensor_tensor(h[:, t, :], h[:, t, :], (PJ, Q2)[t // 2 % 2][:, t % 2, 0:T], ALU.add).then_inc(dn_dve, 1)
                    dve.wait_ge(dn_dve, 8)
                else:
                    LG, MX, IX = rt[:, :, 0:8], rt[:, :, 8:16], rt[:, :, 16:24]
                    OH = [rt[:, :, 40:48], rt[:, :, 48:56]]
                    M, CM = rt[:, :, 28:36], rt[:, :, 56:64]

                    def did(name, ins):
                        ins.then_inc(*rt_dve.did(0, name))
                        dve.wait_ge(*rt_dve.at(0, name))

                    dve.wait_ge(*rt_pe.at(0, "logit"))
                    v.tensor_copy(rt[:, 0:2, 0:8], PJ[:, 0, 0:16].rearrange("p (t e) -> p t e", t=2))
                    v.tensor_copy(rt[0:64, 2, 0:8], PJ[0:64, 0, 16:24])
                    did("lg", v.memset(rt[64:128, 2, 0:8], 0.0))
                    for t in range(3):
                        last = v.max(MX[:, t, :], LG[:, t, :])
                    did("max", last)
                    for t in range(3):
                        last = v.max_index(ridx[:, t, :], MX[:, t, :], LG[:, t, :])
                    did("idx", last)
                    did("idf", v.tensor_copy(IX, ridx[:, :, :]))
                    did("d", v.tensor_tensor(rt[:, :, 24:25], MX[:, :, 1:2], MX[:, :, 0:1], ALU.subtract))
                    dve.wait_ge(*rt_act.at(0, "e"))
                    did("s", v.tensor_scalar(rt[:, :, 25:26], rt[:, :, 24:25], 1.0, None, ALU.add))
                    did("r", v.reciprocal(rt[:, :, 26:27], rt[:, :, 25:26]))
                    did("w2", v.tensor_tensor(rt[:, :, 27:28], rt[:, :, 24:25], rt[:, :, 26:27], ALU.mult))
                    for c in range(2):
                        did(f"oh{c}", v.tensor_tensor(OH[c], IOTA[:, 0:8].unsqueeze(1).to_broadcast([128, 3, 8]),
                                                      IX[:, :, c:c + 1].to_broadcast([128, 3, 8]), ALU.is_equal))
                    did("M", v.tensor_tensor(M, OH[0], OH[1], ALU.add))
                    v.tensor_tensor(OH[0], OH[0], rt[:, :, 26:27].to_broadcast([128, 3, 8]), ALU.mult)
                    did("ohw", v.tensor_tensor(OH[1], OH[1], rt[:, :, 27:28].to_broadcast([128, 3, 8]), ALU.mult))
                    for g in range(GROUPS + 1):
                        last = v.tensor_tensor(CB[:, :, 8 * g:8 * g + 8], OH[0], OH[1], ALU.add)
                    did("comb", last)
                    dve.wait_ge(*rt_pe.at(0, "rank"))
                    v.memset(RK[64:128, 2, 0:NE * GROUPS], -1000.0)
                    v.memset(RK[:, :, NE * GROUPS:], -1000.0)
                    v.scalar_tensor_tensor(out=CM[:, 0:2, :], in0=PJ[:, 1, 0:16].rearrange("p (t e) -> p t e", t=2), scalar=1.0,
                                           in1=M[:, 0:2, :], op0=ALU.add, op1=ALU.mult)
                    did("rk0", v.scalar_tensor_tensor(out=CM[0:64, 2, :], in0=PJ[0:64, 1, 16:24], scalar=1.0, in1=M[0:64, 2, :],
                                                      op0=ALU.add, op1=ALU.mult))
                    did("rk1", v.tensor_reduce(rt[:, 1, 36:37], PJ[:, 1, 24:32], AX.X, ALU.max))
                    for g in range(GROUPS):
                        v.tensor_scalar(RK[:, 0:2, 8 * g:8 * g + 8], CM[:, 0:2, :], -1.0 - CAP * g, None, ALU.add)
                        last = v.tensor_scalar(RK[0:64, 2, 8 * g:8 * g + 8], CM[0:64, 2, :], -1.0 - CAP * g, None, ALU.add)
                    did("RK", last)
                    did("cnt", v.tensor_scalar(rt[:, 2, 36:37], rt[:, 1, 36:37], float(CAP), None, ALU.is_gt))
                    did("flag", v.tensor_copy(flag[:, :], rt[:, 2, 36:37]))


                    def start(x):
                        dve.sem_inc(x["hid"], CH)
                        dve.sem_inc(x["hadd"], KT)
                        dve.sem_inc(x["selw"], 1)

                    start(main)
                    choose(sel, 0, main, "sel", False)
                    with dve.Fori(0, NE) as e:
                        expert(e, main, n3, 1, 0)
                    with dve.If(dve.value_load(flag[0:1, 0:1], min_val=0, max_val=1)):
                        dve.wait_ge(main["selt_pe"], NE + 1)
                        dve.wait_ge(main["xg_pe"], NE + 1)
                        start(over)
                        choose(sel, NE, over, "sel", False)
                        for g in range(1, GROUPS):
                            with dve.Fori(0, NE) as e:
                                expert(e, over, NE * N_XV * (g - 1) + R, NE * (g - 1) + 1, NE * g)
                dve.sem_inc(h_done, 1)
                norm(3 * l + 2)
                gated(5 * l + 4, h, False)
                dve.wait_ge(gat_dve, 8 * (5 * l + 5))
                dve.sem_inc(h_done, 1)
            norm(N_NORM - 1)



_INS = ["xT", "pT", "cst", "par", "slabs", "xslabs", "wsm", "wr", "st_conv", "st_gdn", "st_hg", "st_ssd", "st_mlc", "st_mln", "st_mlm"]
_OUTS = [("y", (KT, 128, T)), ("conv", (DEPTH, 128, 2, 6, 1 + NB, 3)),
         ("gdn_p", (DEPTH, 128, 2, 64)), ("gdn_s", (DEPTH, 128, 2, NB, 64)),
         ("hg_p", (DEPTH, 128, 2, 64)), ("hg_s", (DEPTH, 128, 2, NB, 64)),
         ("ssd_p", (DEPTH, 128, 2, 128)), ("ssd_s", (DEPTH, 128, 2, NB, 128)),
         ("mlc_p", (DEPTH, 128, 2, 64)), ("mlc_s", (DEPTH, 128, 2, NB, 64)),
         ("mln_p", (DEPTH, 128, 2)), ("mln_s", (DEPTH, 128, 2, NB)),
         ("mlm_p", (DEPTH, 128, 2)), ("mlm_s", (DEPTH, 128, 2, NB))]


def constants():
    out = np.zeros((128, N_CST), np.float32)

    def put(name, a):
        o, w = CST[name]
        out[:, o:o + w] = np.broadcast_to(a.reshape(a.shape[0], -1), (128, w))

    s, t = np.arange(64)[:, None], np.arange(64)[None, :]
    E, LM, TRI = np.zeros((2, 8, 64, 64)), np.zeros((2, 7, 64, 64)), np.zeros((2, 64, 64))
    for k in range(2):
        same = np.ones((64, 64), bool) if k == 0 else (s // DS == t // DS)
        TRI[k] = (s <= t) & same
        E[k, 6], E[k, 7] = TRI[k], (s > t) & same
        for j in range(6 if k == 0 else 3):
            w = 2 ** j
            base = t // (2 * w) * (2 * w) + w
            right = t >= base
            E[k, j] = np.where(right, (s >= base) & (s <= t), (s > t) & (s < base))
            LM[k, j] = (s // (2 * w) == t // (2 * w)) & (s % (2 * w) < w) & (t % (2 * w) >= w)
        LM[k, 6] = s == t
    put("E", np.tile(E.transpose(2, 0, 1, 3), (2, 1, 1, 1)))
    put("LM", np.tile(LM.transpose(2, 0, 1, 3), (2, 1, 1, 1)))
    put("TRIM", np.tile(np.concatenate([TRI[0]] * NPB + [TRI[1]], axis=1), (2, 1)))
    put("ID", np.eye(128))
    put("BLK", np.kron(np.eye(2), np.ones((64, 64))))
    put("ONES", np.ones((128, 128)))
    put("BT", np.array([[t[0] // DS == b for b in range(NB)]]).astype(np.float32))
    put("BM", np.tile((s // DS == np.arange(NB)[None, :]), (2, 1)))
    put("RESET", np.where(t % DS == 0, -3.0e38, 0.0))
    put("IOTA", np.arange(128)[None, :])
    put("STR", np.arange(128)[:, None] < np.arange(128)[None, :])
    put("EPS", np.array([[EPS, 64 * EPS]]))
    return out


def lanes(a):
    a = a.reshape(a.shape[:-1] + (2, 2))
    return np.repeat(np.moveaxis(a, -1, 0), 64, axis=0)


def parameters(w, l):
    out = np.zeros((128, N_PAR), np.float32)

    def put(name, a):
        o, n = PAR[name]
        out[:, o:o + n] = a.reshape(128, n)

    for name, src in (("g_mix", w["g_mix"][l]), ("g_ffn", w["g_ffn"][l]), ("g_ple", w["g_ple"][l]), ("g_final", w["g_final"])):
        put(name, src.reshape(KT, 128).T)
    put("gcw", w["gdn_conv_w"][l].reshape(4, 6, 128).transpose(2, 1, 0))
    put("scw", w["ssd_conv_w"][l].reshape(4, 6, 128).transpose(2, 1, 0))
    put("scb", w["ssd_conv_b"][l].reshape(6, 128).T)
    for name, src in (("gnorm", "gdn_norm"), ("hnorm", "hgrn_norm"), ("mnorm", "ml_norm")):
        put(name, np.tile(w[src][l], 2))
    put("snorm", w["ssd_norm"][l].reshape(2, 128).T)
    put("ssd_d", lanes(w["ssd_d"][l]))
    z = np.zeros(4, np.float32)
    put("gb", lanes(np.stack([z, w["gdn_dt_bias"][l], w["ssd_dt_bias"][l], w["ml_ig_b"][l], w["ml_fg_b"][l]])))
    put("alog", lanes(np.stack([w["gdn_a_log"][l], w["ssd_a_log"][l]])))
    put("lb", w["hgrn_lb"].reshape(DEPTH, 2, 128).transpose(2, 0, 1))
    return out


def cut(slabs, n, w):
    k = w.shape[0] // 128
    for c in range(w.shape[1] // 256):
        slabs[n + c].reshape(128, 8, 256)[:, 0:k] = w[:, c * 256:(c + 1) * 256].reshape(k, 128, 256).transpose(1, 0, 2)
    return n + w.shape[1] // 256


def cut_rows(slabs, n, w):
    slabs[n].reshape(128, 2, 1024)[:] = w.reshape(2, 128, 1024).transpose(1, 0, 2)
    return n + 1


def cut_ff(slabs, n, wg, wu, wd):
    for c in range(FF // 256):
        n = cut(slabs, n, wg[:, c * 256:(c + 1) * 256])
        n = cut(slabs, n, wu[:, c * 256:(c + 1) * 256])
    for s, k0, k1 in DOWN:
        n = cut(slabs, n, wd[k0 * 128:k1 * 128, s * 256:(s + 1) * 256])
    return n


def kernel(**inputs):
    import concourse.bacc as _bacc
    from concourse.bass_utils import run_bass_kernel_spmd as _run

    w = {k: np.asarray(a) for k, a in inputs.items()}
    slabs = np.zeros((DEPTH * (N_PROJ + N_GATED + N_OUT + 5) + N_FF, 128, SLAB), np.float32)
    xslabs = np.zeros((NE * N_X, 128, SLAB), np.float32)
    starts = {"gdn_in0": 0, "gdn_in1": 256, "gdn_in2": 512, "gdn_z": 776, "hg_q": 1032, "hg_f": 1288, "hg_v": 1544,
              "hg_g": 1800, "ssd_z": 2056, "ssd_in0": 2312, "ssd_in1": 2568, "ssd_in2": 2824, "ml_qk": 3084,
              "ml_v": 3340, "ml_o": 3604}
    n = 0
    for l in range(DEPTH):
        wi = w["w_in"][l]
        for name in PROJ:
            n = cut(slabs, n, wi[:, starts[name]:starts[name] + 256])
        for b in range(4):
            n = cut_rows(slabs, n, w["w_branch"][l, b])
            n = cut(slabs, n, wi[:, 3860 + b * DM:3860 + (b + 1) * DM])
        n = cut(slabs, n, w["w_out"][l])
        if l % 2 == 0:
            n = cut_ff(slabs, n, w["w_ff_gate"][0], w["w_ff_up"][0], w["w_ff_down"][0])
        else:
            m = 0
            for e in range(NE):
                for c in range(CH):
                    for part in ("w_ex_gate", "w_ex_up"):
                        m = cut(xslabs, m, w[part][0, e][:, c * 256:(c + 1) * 256])
                for c in range(FT // 2):
                    m = cut_rows(xslabs, m, w["w_ex_down"][0, e][c * 256:(c + 1) * 256])
        n = cut_rows(slabs, n, w["w_ple"][l])
        n = cut(slabs, n, w["w_ple_gate"][l])
    assert n == len(slabs)

    def tokens(p, s):
        return np.concatenate([p.reshape(SEQ, -1), s.reshape(NB * DS, -1)]).T

    small = np.concatenate([w["w_in"][:, :, 768:776], w["w_in"][:, :, 3080:3084], w["w_in"][:, :, 3596:3604]], axis=2)
    conv = np.stack([w["state_gdn_conv"], w["state_ssd_conv"]], axis=1)

    def heads(a):
        L, B, H, K, V = a.shape
        return a.reshape(L, B, 2, 2, K, V).transpose(0, 3, 4, 2, 1, 5).reshape(L, 2 * K, 2, B, V)

    mlc = np.zeros((DEPTH, NB, 4, 64, 64), np.float32)
    mlc[:, :, :, 0:32] = w["state_mlstm_c"]
    mln = np.zeros((DEPTH, NB, 4, 64, 1), np.float32)
    mln[:, :, :, 0:32, 0] = w["state_mlstm_n"]
    arrays = {
        "xT": tokens(w["x_prompt"], w["x_sample"]).reshape(KT, 128, T),
        "pT": np.stack([tokens(w["p_prompt"][l], w["p_sample"][l]).reshape(2, 128, T).transpose(1, 0, 2) for l in range(DEPTH)]),
        "cst": constants(),
        "par": np.stack([parameters(w, l) for l in range(DEPTH)]),
        "slabs": slabs, "xslabs": xslabs,
        "wsm": small.reshape(DEPTH, KT, 128, 20).transpose(0, 2, 1, 3),
        "wr": w["w_router"][0].reshape(KT, 128, NE).transpose(1, 0, 2),
        "st_conv": conv.reshape(DEPTH, 2, NB, 3, 6, 128).transpose(0, 5, 1, 4, 2, 3),
        "st_gdn": heads(w["state_gdn"]), "st_hg": heads(w["state_hgrn"]), "st_ssd": heads(w["state_ssd"]),
        "st_mlc": heads(mlc), "st_mln": heads(mln)[..., 0],
        "st_mlm": np.stack([lanes(w["state_mlstm_m"][l]).transpose(0, 2, 1) for l in range(DEPTH)]),
    }
    arrays = {f"in_{k}_dram": np.ascontiguousarray(a) for k, a in arrays.items()}
    nc = _bacc.Bacc("TRN2", target_bir_lowering=False, num_devices=1)
    args = [nc.dram_tensor(f"in_{k}_dram", arrays[f"in_{k}_dram"].shape, F32, kind="ExternalInput").ap() for k in _INS]
    args += [nc.dram_tensor(f"out_{k}_dram", shape, F32, kind="ExternalOutput").ap() for k, shape in _OUTS]
    trunk_kernel(nc, *args)
    r = _run(nc, [arrays], core_ids=[0])
    o = {k: np.asarray(r.results[0][f"out_{k}_dram"]).reshape(shape) for k, shape in _OUTS}

    y = o["y"].reshape(DM, T).T
    cv = o["conv"].transpose(0, 2, 4, 5, 3, 1).reshape(DEPTH, 2, 1 + NB, 3, 768)

    def back(a, k=64):
        L, _, _, B, V = a.shape
        return np.ascontiguousarray(a.reshape(L, 2, 64, 2, B, V).transpose(0, 4, 3, 1, 2, 5).reshape(L, B, 4, 64, V)[:, :, :, 0:k])

    def states(sfx):
        one = (lambda a: a[:, :, :, None]) if sfx == "p" else (lambda a: a)
        c = cv[:, :, 0:1] if sfx == "p" else cv[:, :, 1:]
        m = one(o["mlm_" + sfx])
        return (np.ascontiguousarray(c[:, 0]), back(one(o["gdn_" + sfx])), back(one(o["hg_" + sfx])), np.ascontiguousarray(c[:, 1]),
                back(one(o["ssd_" + sfx])), back(one(o["mlc_" + sfx]), 32), back(one(o["mln_" + sfx])[..., None], 32)[..., 0],
                np.ascontiguousarray(m.reshape(DEPTH, 2, 64, 2, -1)[:, :, 0].transpose(0, 3, 2, 1).reshape(DEPTH, -1, 4)))

    return (np.ascontiguousarray(y[0:SEQ]).reshape(1, SEQ, DM), np.ascontiguousarray(y[SEQ:]).reshape(NB, DS, DM),
            *states("p"), *states("s"))
```

```python
from contextlib import ExitStack

import numpy as np

import concourse.bass as bass
from concourse import mybir

F32 = mybir.dt.float32
U32 = mybir.dt.uint32
ALU = mybir.AluOpType
ACT = mybir.ActivationFunctionType
AX = mybir.AxisListType

DM, SEQ, NB, DS, DEPTH = 1024, 256, 8, 8, 2
T = SEQ + NB * DS
KT = DM // 128
FF = ((8 * DM // 3 + 255) // 256) * 256
FT = FF // 128
NE = 8
BL = 64
NBLK = T // BL
NPB = SEQ // BL
EPS = 1e-6
R = 5
SLAB = 8 * 256
XPW = 3 + SEQ + NB * (3 + DS)

PROJ = ["gdn_in0", "gdn_in1", "gdn_in2", "ml_qk", "hg_q", "ssd_in0", "ssd_in1", "ssd_in2", "hg_v", "ml_v",
        "gdn_z", "hg_g", "ssd_z", "hg_f", "ml_o"]
N_PROJ = len(PROJ)
N_GATED = 4 * 5
N_OUT = 4
DOWN = [(0, 0, 8), (0, 8, 15), (0, 15, 22), (1, 0, 8), (1, 8, 15), (1, 15, 22), (2, 0, 8), (2, 8, 15), (2, 15, 22),
        (3, 0, 6), (3, 6, 12), (3, 12, 17), (3, 17, 22)]
N_FF = 2 * (FF // 256) + len(DOWN)
CH = FF // 256
N_X = 2 * CH + FT // 2
N_SKIP = -N_X % R
N_XV = N_X + N_SKIP
CAP = 128
GROUPS = -(-T // CAP)
TT = [(0, 128), (128, 256), (256, T)]

CST = {}
for _n, _w in (("E", 2 * 8 * 64), ("LM", 2 * 7 * 64), ("TRIM", T), ("ID", 128), ("BLK", 128), ("ONES", 128),
               ("BT", NB * 64), ("BM", NB), ("RESET", 64), ("IOTA", 128), ("EPS", 2), ("STR", 128)):
    CST[_n] = (sum(w for _, w in CST.values()), _w)
N_CST = sum(w for _, w in CST.values())
PAR = {}
for _n, _w in (("g_mix", 8), ("g_ffn", 8), ("g_ple", 8), ("g_final", 8), ("gcw", 24), ("gcb", 6), ("scw", 24),
               ("scb", 6), ("gnorm", 1), ("hnorm", 1), ("mnorm", 1), ("snorm", 2), ("ssd_d", 2), ("gb", 10),
               ("alog", 4), ("lb", 4)):
    PAR[_n] = (sum(w for _, w in PAR.values()), _w)
N_PAR = sum(w for _, w in PAR.values())


class Steps:

    def __init__(self, sem, names):
        self.sem, self.names, self.count = sem, names.split(), 0

    def at(self, rnd, name):
        return self.sem, rnd * len(self.names) + self.names.index(name) + 1

    def did(self, rnd, name):
        self.count += 1
        assert self.at(rnd, name)[1] == self.count, (name, self.count)
        return self.sem, 1


def trunk_kernel(nc, xT, pT, cst_d, par_d, slabs, xslabs, wsm_d, wr_d, st_conv, st_gdn, st_hg, st_ssd, st_mlc, st_mln, st_mlm,
                 y_d, o_conv, o_gdn_p, o_gdn_s, o_hg_p, o_hg_s, o_ssd_p, o_ssd_s, o_mlc_p, o_mlc_s,
                 o_mln_p, o_mln_s, o_mlm_p, o_mlm_s):
    ctx = ExitStack()
    with ctx:
        def sb(name, shape, dt=F32):
            return ctx.enter_context(nc.sbuf_tensor(name, shape, dt))

        def sem(name):
            return ctx.enter_context(nc.semaphore(name))

        PJ, Q0, Q1, Q2 = [ctx.enter_context(nc.psum_tensor(n, [128, 2, 512], F32)) for n in ("PJ", "Q0", "Q1", "Q2")]

        ring = sb("ring", [128, R, SLAB])
        cst = sb("cst", [128, N_CST])
        par = sb("par", [128, DEPTH, N_PAR])
        h = sb("h", [128, KT, T])
        u = sb("u", [128, KT, T])
        BR = sb("BR", [128, 4, 2, T])
        wsm = sb("wsm", [128, KT, 20])
        wr = sb("wr", [128, KT, NE])
        NT = 640
        mix = sb("mix", [128, 28 * NT + 6 * XPW + 12 * T])
        stg = sb("stg", [128, 2, NB, 64])
        sth = sb("sth", [128, 2, NB, 64])
        sts = sb("sts", [128, 2, NB, 128])
        stm = sb("stm", [128, 2, NB, 64])
        stn = sb("stn", [128, 2, NB])
        stmm = sb("stmm", [128, 2, NB])
        sconv = sb("sconv", [128, 2, 6, NB, 3])
        cs = sb("cs", [128, 2, 6, 1 + NB, 3])
        rstd = sb("rstd", [128, T])
        Sp = sb("Sp", [128, 2, 2, 128])
        nst = sb("nst", [128, 2, 2])
        mm = sb("mm", [128, NPB + 1, 2])
        mms = sb("mms", [128, 2, NB])
        smb = sb("smb", [128, 5, 2, NBLK])
        beta = sb("beta", [128, 2, NBLK])
        sp3 = sb("sp3", [128, 6, 3 * 2 * NBLK])
        cf = sb("cf", [128, 3, 2])
        G = sb("G", [128, NBLK, 6])
        gt = sb("gt", [128, 2, NBLK, 6])
        egt = sb("egt", [128, 2, NBLK, 6])
        sm1 = sb("sm1", [128, 2, NBLK])
        xtk = sb("xtk", [128, 2, NBLK])
        wend = sb("wend", [128, 2, NBLK])
        msel = sb("msel", [128, 2, NB])
        egc = sb("egc", [128, 2, NPB + NB])
        lbt = sb("lbt", [128, 8, 2])
        lbv = sb("lbv", [128, DEPTH, 2, 2])
        rt = sb("rt", [128, 3, 64])
        ridx = sb("ridx", [128, 3, 8], U32)

        at = [0]

        def part(n):
            a = mix[:, at[0]:at[0] + n]
            at[0] += n
            return a

        def pairs(a):
            return a.rearrange("p (q t) -> p q t", q=2)

        hgq, hgv, mlq, mlk, mlv, gz, hgg, sz, sf, sfn, mlo = [pairs(part(NT)) for _ in range(11)]
        XP = part(6 * XPW).rearrange("p (c t) -> p c t", c=6)
        C6 = [part(6 * T).rearrange("p (c t) -> p c t", c=6) for _ in range(2)]
        GR = [pairs(part(NT)) for _ in range(3)]
        XROW = pairs(part(NT))
        scr = part(13 * NT)

        def sl(i, n=1):
            return scr[:, i * NT:(i + n) * NT]

        def tt(i):
            return pairs(sl(i))

        def c_(name):
            o, w = CST[name]
            return cst[:, o:o + w]

        E = c_("E").rearrange("p (k j t) -> p k j t", k=2, j=8)
        LM = c_("LM").rearrange("p (k j t) -> p k j t", k=2, j=7)
        TRIM, ID, BLK, ONES = c_("TRIM"), c_("ID"), c_("BLK"), c_("ONES")
        BT = c_("BT").rearrange("p (b t) -> p b t", b=NB)
        BM, RESET, IOTA, EPSC, STR = c_("BM"), c_("RESET"), c_("IOTA"), c_("EPS"), c_("STR")

        def pr(l, name):
            o, w = PAR[name]
            return par[:, l, o:o + w]

        LN = (slice(0, 64), slice(64, 128))

        def kind(blk):
            return 0 if blk < NPB else 1

        def tk(blk):
            return slice(blk * BL, (blk + 1) * BL)

        def units(blks=range(NBLK)):
            return [(b, q, i) for b in blks for q in range(2) for i in range(2)]

        def bt(a):
            return a.rearrange("p q (b t) -> p q b t", t=BL)

        def bcol(a):
            return a.unsqueeze(3).to_broadcast([128, 2, NBLK, BL])

        def gcol(t, w, m):
            return t[:, w, :, 2 * m:2 * m + 2].rearrange("p b q -> p q b")

        slab_in = [sem(f"slab_in{i}") for i in range(R)]
        slab_done = sem("slab_done")
        consts_in, layer_in, ple_in, out_sem = sem("consts_in"), sem("layer_in"), sem("ple_in"), sem("out_sem")
        h_done, h_in, y_out = sem("h_done"), sem("h_in"), sem("y_out")
        N_NORM = 3 * DEPTH + 1
        norm_act = Steps(sem("norm_act"), " ".join(f"sq{i}" for i in range(KT)) + " root")
        norm_pe = Steps(sem("norm_pe"), "ss")
        norm_dve = Steps(sem("norm_dve"), "rstd " + " ".join(f"u{i}" for i in range(KT // 2)))
        setup_dve = Steps(sem("setup_dve"), "max sub sum rcp sm lb one")
        setup_act = Steps(sem("setup_act"), "exp")
        proj_pe, proj_ev = sem("proj_pe"), sem("proj_ev")
        halo, conv_tap, conv_silu, conv_new = sem("halo"), sem("conv_tap"), sem("conv_silu"), sem("conv_new")
        gp_pe = Steps(sem("gp_pe"), "small gam gr0 gr1 gr2 ig")
        gp_act = Steps(sem("gp_act"), "beta ea abs e ln egt gr0 gr1 gr2")
        gp_dve = Steps(sem("gp_dve"), "smb spc spi u1 d z dz lz rd le lp sp cf G gt xrow")
        gd_pe = Steps(sem("gd_pe"), "l2 ktok vtok kk qk " + " ".join(f"w{j} tu{j}" for j in range(6)) + " skt sv "
                      + " ".join(f"p{c} o{c} k{c}" for c in range(NPB)) + " ps os ks nss")
        gd_act = Steps(sem("gd_act"), "sq rootq rootk dexp egrow skt osq root")
        gd_dve = Steps(sem("gd_dve"), "rn qk dsub dmin D bg kb kw vb lt qkd init qe " + " ".join(
            f"al{j} wb{j} t{j} u{j}" for j in range(6)) + " sv zero " + " ".join(f"u{c}_ s{c}" for c in range(NPB))
            + " sx us ux o sd ss on rn2 br")
        hg_pe = Steps(sem("hg_pe"), "lftok vtok " + "x0 " + " ".join(f"x{i + 1} a{i}" for i in range(9)) + " a9 kw "
                      + " ".join(f"o{c} k{c}" for c in range(NPB)) + " os ks nss")
        hg_act = Steps(sem("hg_act"), "lf lft vt " + " ".join(f"x{i} e{i}" for i in range(10)) + " kw osq root")
        hg_dve = Steps(sem("hg_dve"), "pre kin " + "z0 " + " ".join(f"z{i + 1} m{i} r{i}" for i in range(9)) + " m9 r9" + " zero "
                       + " ".join(f"s{c}" for c in range(NPB)) + " ux o sd ss on rn2 br")
        sd_pe = Steps(sem("sd_pe"), "xtok btok cb " + " ".join(f"t{c} y{c} k{c}" for c in range(NPB))
                      + " t_0 y_0 k_0 t_1 y_1 k_1 nss")
        sd_act = Steps(sem("sd_act"), "dexp egrow xt btp bts " + " ".join(f"t{c}" for c in range(NPB)) + " t_0 t_1 osq root")
        sd_dve = Steps(sem("sd_dve"), "dsub dmin D wdt xw att0 att xx zero " + " ".join(f"s{c}" for c in range(NPB))
                       + " sd0 ss0 sd1 ss1 y0 y1 y2 yz rn2 br")
        ml_pe = Steps(sem("ml_pe"), "vtok ktok kq " + " ".join(f"o{c} k{c}" for c in range(NPB)) + " os ks nss")
        ml_act = Steps(sem("ml_act"), "vt wexp win wend emt dab osq root")
        ml_dve = Steps(sem("ml_dve"), "m0 " + " ".join(f"sc{c} mm{c}" for c in range(NPB))
                       + " inj scs mms xtk sub min selm sel we0 wpre mt qw wt0 wt kw kw0 zero "
                       + " ".join(f"s{c}" for c in range(NPB)) + " ux dmx drc oo sd sn0 ss on rn2 br")
        gat_pe, prod_pe, gat_act, gat_dve = sem("gat_pe"), sem("prod_pe"), sem("gat_act"), sem("gat_dve")
        out_pe = sem("out_pe")
        out_ev = sem("out_ev")
        ff_act, ff_dve = sem("ff_act"), sem("ff_dve")
        gat_mul = sem("gat_mul")
        pads = Steps(sem("pads"), "zero")
        dn_dve = sem("dn_dve")
        rt_pe = Steps(sem("rt_pe"), "utok logit rank")
        rt_dve = Steps(sem("rt_dve"), "lg max idx idf d s r w2 oh0 oh1 M ohw comb rk0 rk1 RK cnt flag")
        rt_act = Steps(sem("rt_act"), "utok0 utok1 utok2 e")

        def xpart(n, _a=[0]):
            a = mix[:, _a[0]:_a[0] + n]
            _a[0] += n
            assert _a[0] <= 11 * NT + 6 * XPW + 12 * T + 4 * NT
            return a

        hidx = xpart(FT * CAP).rearrange("p (f t) -> p f t", f=FT)
        utok = xpart(3 * DM).rearrange("p (t c) -> p t c", t=3)
        xg = xpart(KT * CAP).rearrange("p (k t) -> p k t", k=KT)
        sgx = xpart(4 * CAP).rearrange("p (r t) -> p r t", r=2)
        sel = xpart(3 * CAP).rearrange("p (t c) -> p t c", t=3)
        selw = xpart(3 * CAP).rearrange("p (t c) -> p t c", t=3)
        selt = xpart(T)
        yg = xpart(DM)
        RK = xpart(3 * NE * (GROUPS + 1)).rearrange("p (t c) -> p t c", t=3)
        CB = xpart(3 * NE * (GROUPS + 1)).rearrange("p (t c) -> p t c", t=3)
        flag = sb("flag", [128, 1], mybir.dt.int32)
        X_NAMES = ("selw", "sel", "selt_pe", "selt", "xg_pe", "xg", "silu", "hid", "yg", "scat", "hadd")
        main = {n: sem("x_" + n) for n in X_NAMES}
        over = {n: sem("o_" + n) for n in X_NAMES}
        over["slab_in"] = [sem(f"o_slab_in{i}") for i in range(R)]
        over["slab_done"] = sem("o_slab_done")
        main["slab_in"], main["slab_done"] = slab_in, slab_done

        hid = mix[:, 0:FT * T].rearrange("p (f t) -> p f t", f=FT)
        ffs = mix[:, FT * T:(FT + 4) * T].rearrange("p (r f t) -> p r f t", r=2, f=2)
        gat0 = 11 * NT
        merged = mix[:, gat0:gat0 + KT * T].rearrange("p (k t) -> p k t", k=KT)
        sgs = mix[:, gat0 + KT * T:gat0 + (KT + 4) * T].rearrange("p (k t) -> p k t", k=4)

        def sg(m):
            return sgs[:, m % 8, :] if m % 8 < 4 else (gz, hgv)[m % 8 // 2 - 2][:, m % 2, :]

        assert (KT + 4) * T <= 6 * XPW + 6 * T
        pt = pairs(scr[:, 11 * NT:12 * NT])
        sqh = scr[:, KT * T:2 * KT * T].rearrange("p (k t) -> p k t", k=KT)

        PER_LAYER = [N_PROJ + N_GATED + N_OUT + n + 5 for n in (N_FF, NE * N_XV)]
        BASE = [0, PER_LAYER[0]]
        TOTAL = sum(PER_LAYER)
        N_OUTS = [0]

        def adds(m):
            return (m + 1) // 40 * 32 + max(0, (m + 1) % 40 - 8)

        def h_tile(k, i):
            if k == 0:
                return h_in, 16
            if k == 5:
                return h_done, k
            return ((gat_dve, 32 * (k // 3) - 8 + i + 1), (out_ev, 8 * (k // 3) + i + 1), (dn_dve, i + 1))[k % 3]

        def prod_bank(i):
            return 1 - i % 2 if i // 8 == 3 else 1

        def slab(n):
            return ring[:, n % R, :].rearrange("p (k c) -> p k c", k=8)

        def slab2(n):
            return ring[:, n % R, :].rearrange("p (k c) -> p k c", k=2)

        block = ctx.enter_context(nc.Block())

        @block.sync
        def _(sp):
            def load(n, src):
                if n >= R:
                    sp.wait_ge(slab_done, n - R + 1)
                sp.dma_start(ring[:, n % R, :], src).then_inc(slab_in[n % R], 16)

            def load_expert(e, n0, loaded, done, i0):
                for i in range(N_X):
                    n = n0 + i
                    if n >= R or i0:
                        sp.wait_ge(done, e * N_XV + (n - R + 1))
                    src = xslabs[bass.ds(e * N_X + i, 1), :, :].rearrange("a p c -> (a p) c")
                    sp.dma_start(ring[:, n % R, :], src).then_inc(loaded[n % R], 16)

            sp.dma_start(cst[:], cst_d).then_inc(consts_in, 16)
            sp.dma_start(par[:], par_d.rearrange("l p c -> p l c")).then_inc(consts_in, 16)
            sp.dma_start(wr[:], wr_d).then_inc(consts_in, 16)
            sp.wait_ge(h_in, 16)
            pre = N_PROJ + N_GATED + N_OUT
            for n in range(BASE[1] + pre):
                load(n, slabs[n])
            first = BASE[1] + pre
            with sp.Fori(0, NE) as e:
                load_expert(e, first, slab_in, slab_done, 1)
            last = first + NE * N_XV
            sp.wait_ge(*rt_dve.at(0, "flag"))
            with sp.If(sp.value_load(flag[0:1, 0:1], min_val=0, max_val=1)):
                sp.wait_ge(slab_done, last)
                for g in range(1, GROUPS):
                    with sp.Fori(0, NE) as e:
                        load_expert(e, NE * N_XV * (g - 1) + R, over["slab_in"], over["slab_done"], 1)
                sp.wait_ge(over["slab_done"], (GROUPS - 1) * NE * N_XV + R)
            for n in range(last, TOTAL):
                load(n, slabs[n - NE * N_XV])
            for k in range(KT // 2):
                sp.wait_ge(*norm_dve.at(N_NORM - 1, f"u{k}"))
                sp.dma_start(y_d[2 * k:2 * k + 2].rearrange("k p t -> p k t"), u[:, 2 * k:2 * k + 2, :]).then_inc(y_out, 16)
            sp.wait_ge(y_out, 16 * (KT // 2))

        @block.gpsimd
        def _(pool):
            for l in range(DEPTH):
                if l:
                    pool.wait_ge(h_done, 3 * l)
                    pool.wait_ge(out_sem, 16 * N_OUTS[0])
                pool.dma_start(wsm[:], wsm_d[l]).then_inc(layer_in, 16)
                pool.dma_start(sconv[:], st_conv[l]).then_inc(layer_in, 16)
                pool.dma_start(stg[:], st_gdn[l]).then_inc(layer_in, 16)
                pool.dma_start(sth[:], st_hg[l]).then_inc(layer_in, 16)
                pool.dma_start(sts[:], st_ssd[l]).then_inc(layer_in, 16)
                pool.dma_start(stm[:], st_mlc[l]).then_inc(layer_in, 16)
                pool.dma_start(stn[:], st_mln[l]).then_inc(layer_in, 16)
                pool.dma_start(stmm[:], st_mlm[l]).then_inc(layer_in, 16)

                def store(dst, src):
                    N_OUTS[0] += 1
                    pool.dma_start(dst, src).then_inc(out_sem, 16)

                pool.wait_ge(*gd_dve.at(l, f"s{NPB - 1}"))
                store(o_gdn_p[l], Sp[:, NPB % 2, :, 0:64])
                pool.wait_ge(*gd_dve.at(l, "ss"))
                store(o_gdn_s[l], stg[:])
                pool.wait_ge(*hg_dve.at(l, f"s{NPB - 1}"))
                store(o_hg_p[l], Sp[:, NPB % 2, :, 0:64])
                pool.wait_ge(*hg_dve.at(l, "ss"))
                store(o_hg_s[l], sth[:])
                pool.wait_ge(*sd_dve.at(l, f"s{NPB - 1}"))
                store(o_ssd_p[l], Sp[:, NPB % 2, :, :])
                pool.wait_ge(*sd_dve.at(l, "ss1"))
                store(o_ssd_s[l], sts[:])
                pool.wait_ge(*ml_dve.at(l, f"s{NPB - 1}"))
                store(o_mlc_p[l], Sp[:, NPB % 2, :, 0:64])
                store(o_mln_p[l], nst[:, NPB % 2, :])
                store(o_mlm_p[l], mm[:, NPB, :])
                pool.wait_ge(*ml_dve.at(l, "ss"))
                store(o_mlc_s[l], stm[:])
                store(o_mln_s[l], stn[:])
                store(o_mlm_s[l], mms[:])
                pool.wait_ge(conv_new, 4 * (l + 1))
                store(o_conv[l], cs[:])
                pool.wait_ge(*ml_dve.at(l, "br"))
                pool.dma_start(pt, pT[l]).then_inc(ple_in, 16)
            pool.wait_ge(out_sem, 16 * N_OUTS[0])

        N_CONSTS = 16 * 3
        PER_L_IN = 16 * 8

        @block.tensor
        def _(pe):
            mmul = nc.tensor.matmul

            first_x = BASE[1] + N_PROJ + N_GATED + N_OUT

            def take(n):
                skipped = NE if n > first_x and (n - first_x) % R >= R - N_SKIP else 0
                pe.wait_ge(slab_in[n % R], 16 * (n // R + 1 - skipped))

            def norm_tile(k, i):
                pe.wait_ge(*norm_act.at(k, f"sq{i}"))
                if k == 0 and i == 0:
                    pe.wait_ge(consts_in, N_CONSTS)
                last = mmul(Q0[:, 0, 0:T], ONES, sqh[:, i, :], start=(i == 0), stop=(i == KT - 1))
                if i == KT - 1:
                    last.then_inc(*norm_pe.did(k, "ss"))

            def u_ready(norm, k):
                if norm is not None and k % 2 == 0:
                    pe.wait_ge(*norm_dve.at(norm, f"u{k // 2}"))

            def linear(n, j, out, rhs, k0=0, k1=KT, start=True, stop=True, norm=None):
                w = slab(n)
                for k in range(k0, k1):
                    u_ready(norm, k)
                    last = mmul(out, w[:, k - k0, j * 128:(j + 1) * 128], rhs[:, k, :],
                                start=(start and k == k0), stop=(stop and k == k1 - 1))
                return last

            def tokens(out, src):
                for b, q, i in units():
                    last = mmul(out[LN[i], q, tk(b)], src[LN[i], q, tk(b)], ID[LN[i], LN[i]], start=True, stop=True)
                return last

            def each(out, lhs, rhs, blks=range(NBLK)):
                for b, q, i in units(blks):
                    last = mmul(out[LN[i], q, tk(b)], lhs[LN[i], q, tk(b)], rhs[LN[i], q, tk(b)], start=True, stop=True)
                return last

            def head_norm(src_done, steps, l, sq):
                pe.wait_ge(*src_done)
                for q in range(2):
                    last = mmul(Q1[:, q, 0:T], BLK, sq[:, q, :], start=True, stop=True)
                last.then_inc(*steps.did(l, "nss"))

            for l in range(DEPTH):
                n0 = BASE[l]
                if l == 0:
                    for i in range(KT):
                        norm_tile(0, i)
                tile = [0]

                def proj(k):
                    for i in range(tile[0], tile[0] + k):
                        m = 2 * N_PROJ * l + i
                        if i % 2 == 0:
                            take(n0 + i // 2)
                        if m >= 2:
                            pe.wait_ge(proj_ev, m - 1)
                        linear(n0 + i // 2, i % 2, PJ[:, i % 2, 0:T], u, norm=None if i else 3 * l)\
                            .then_inc(slab_done if i % 2 else proj_pe, 1)
                    tile[0] += k

                ltile, ptile = [0], [0]
                first_slab = [n0 + N_PROJ + 5 * n for n in range(4)]

                def logits(k):
                    for i in range(ltile[0], ltile[0] + k):
                        n, t = i // 8, i % 8
                        m = 40 * l + i
                        if i == 0:
                            pe.wait_ge(proj_ev, 2 * N_PROJ * (l + 1))
                        if t % 2 == 0:
                            take(first_slab[n] + t // 2)
                        if m:
                            pe.wait_ge(gat_act, m)
                        linear(first_slab[n] + t // 2, t % 2, PJ[:, 0, 0:T], u, norm=3 * l + 2 if i == 32 else None).then_inc(gat_pe, 1)
                    ltile[0] += k

                def products(k):
                    for i in range(ptile[0], ptile[0] + k):
                        n, t = i // 8, i % 8
                        m = 40 * l + i
                        n1 = first_slab[n] + 4
                        if t == 0:
                            take(n1)
                            if n < 4:
                                pe.wait_ge(*(gd_dve, hg_dve, sd_dve, ml_dve)[n].at(l, "br"))
                        if n == 3 and t == 1:
                            pe.wait_ge(gat_act, 40 * l + 32)
                        if m:
                            pe.wait_ge(gat_mul, m - 1 if n == 3 and t else m)
                        x, w = (BR[:, n] if n < 4 else pt), slab2(n1)
                        for k_ in range(2):
                            last = mmul(PJ[:, prod_bank(i), 0:T], w[:, k_, t * 128:(t + 1) * 128], x[:, k_, :],
                                        start=(k_ == 0), stop=(k_ == 1))
                        last.then_inc(slab_done if t % 2 else prod_pe, 2 if t == 7 else 1)
                    ptile[0] += k

                proj(6)
                pe.wait_ge(layer_in, PER_L_IN * (l + 1))
                SMP = Q1[:, 0, 0:50].rearrange("p (b g) -> p b g", b=NBLK)
                for b in range(NBLK):
                    for i in range(2):
                        for k in range(KT):
                            last = mmul(SMP[LN[i], b, :], u[:, k, tk(b)], wsm[:, k, i::2], start=(k == 0), stop=(k == KT - 1))
                last.then_inc(*gp_pe.did(l, "small"))
                proj(4)
                pe.wait_ge(*gp_dve.at(l, "G"))
                GT = Q1[:, 1, 0:60].rearrange("p (w b g) -> p w b g", w=2, b=NBLK)
                for w in range(2):
                    for kd, b0, b1 in ((0, 0, NPB), (1, NPB, NBLK)):
                        for i in range(2):
                            last = mmul(GT[LN[i], w, b0:b1, :].rearrange("p b g -> p (b g)"), E[LN[i], kd, 6 + w, :],
                                        G[LN[i], b0:b1, :].rearrange("p b g -> p (b g)"), start=True, stop=True)
                last.then_inc(*gp_pe.did(l, "gam"))
                for m, out in ((0, Q0), (1, Q2), (2, Q0)):
                    if m == 2:
                        proj(1)
                        pe.wait_ge(*gp_act.at(l, "gr0"))
                    for b, q, i in units():
                        last = mmul(out[LN[i], q, tk(b)], G[LN[i], b, 2 * m + q:2 * m + q + 1].to_broadcast([64, 64]),
                                    E[LN[i], kind(b), 6, :], start=True, stop=True)
                    last.then_inc(*gp_pe.did(l, f"gr{m}"))
                pe.wait_ge(*gp_act.at(l, "gr1"))
                for b, q, i in units():
                    last = mmul(Q2[LN[i], q, tk(b)], smb[LN[i], 3, q, b:b + 1].to_broadcast([64, 64]), ID[LN[i], LN[i]],
                                start=True, stop=True)
                last.then_inc(*gp_pe.did(l, "ig"))
                proj(1)

                C = C6[0]
                pe.wait_ge(*gd_act.at(l, "sq"))
                pe.wait_ge(*gp_act.at(l, "gr2"))
                pe.wait_ge(*gp_dve.at(l, "gt"))
                sq4 = sl(0, 2).rearrange("p (c t) -> p c t", c=4)
                for c in range(4):
                    last = mmul((Q0, Q1)[c // 2][:, c % 2, 0:T], BLK, sq4[:, c, :], start=True, stop=True)
                last.then_inc(*gd_pe.did(l, "l2"))
                proj(3)
                pe.wait_ge(*gd_dve.at(l, "qk"))
                pe.wait_ge(*gp_dve.at(l, "xrow"))
                qT, kT, vT = C[:, 0:2, :], C[:, 2:4, :], C[:, 4:6, :]
                tokens(Q0, kT).then_inc(*gd_pe.did(l, "ktok"))
                tokens(Q1, vT).then_inc(*gd_pe.did(l, "vtok"))
                each(Q2, kT, kT).then_inc(*gd_pe.did(l, "kk"))
                proj(1)
                pe.wait_ge(*gd_dve.at(l, "kw"))
                each(Q0, kT, qT).then_inc(*gd_pe.did(l, "qk"))
                proj(1)
                pe.wait_ge(*gd_dve.at(l, "qkd"))
                LT, QKD, VB, KB, KW, Tm, U, W, AL, SV, SKT = [tt(i) for i in (3, 4, 5, 6, 7, 8, 9, 10, 11, 0, 1)]
                QE, UU = tt(2), tt(12)
                for j in range(6):
                    blks = range(NBLK) if j < 3 else range(NPB)
                    pe.wait_ge(*gd_dve.at(l, f"al{j}"))
                    pe.wait_ge(*gd_dve.at(l, f"u{j - 1}" if j else "init"))
                    each(Q0, AL, Tm, blks).then_inc(*gd_pe.did(l, f"w{j}"))
                    if j > 1:
                        proj(1)
                    pe.wait_ge(*gd_dve.at(l, f"wb{j}"))
                    each(Q1, U, W, blks)
                    each(Q2, W, U, blks).then_inc(*gd_pe.did(l, f"tu{j}"))
                    proj(1)
                pe.wait_ge(*gd_dve.at(l, "u5"))
                each(Q0, KB, U).then_inc(*gd_pe.did(l, "skt"))
                each(Q1, U, VB).then_inc(*gd_pe.did(l, "sv"))
                pe.wait_ge(*gd_act.at(l, "skt"))
                pe.wait_ge(*gd_dve.at(l, "sv"))
                pe.wait_ge(*gd_dve.at(l, "zero"))
                for c in range(NPB):
                    S = Sp[:, c % 2, :, 0:64]
                    if c:
                        pe.wait_ge(*gd_dve.at(l, f"s{c - 1}"))
                    for q in range(2):
                        for i in range(2):
                            last = mmul(Q2[LN[i], q, 0:64], SKT[LN[i], q, tk(c)], S[LN[i], q, :], start=True, stop=True)
                    last.then_inc(*gd_pe.did(l, f"p{c}"))
                    if c < 3:
                        proj(1)
                    pe.wait_ge(*gd_dve.at(l, f"u{c}_"))
                    for q in range(2):
                        for i in range(2):
                            mmul(Q0[LN[i], q, tk(c)], UU[LN[i], q, tk(c)], QKD[LN[i], q, tk(c)], start=True, stop=False)
                            last = mmul(Q0[LN[i], q, tk(c)], S[LN[i], q, :], QE[LN[i], q, tk(c)], start=False, stop=True)
                    last.then_inc(*gd_pe.did(l, f"o{c}"))
                    for q in range(2):
                        for i in range(2):
                            last = mmul(Q1[LN[i], q, 0:64], KW[LN[i], q, tk(c)], UU[LN[i], q, tk(c)], start=True, stop=True)
                    last.then_inc(*gd_pe.did(l, f"k{c}"))
                SX = sl(5, 2)[:, 0:1024].rearrange("p (q b t) -> p q b t", q=2, b=NB)
                UX = sl(10, 2)[:, 0:1024].rearrange("p (q b t) -> p q b t", q=2, b=NB)
                pe.wait_ge(*gd_dve.at(l, "sx"))
                pe.wait_ge(layer_in, PER_L_IN * (l + 1))
                for q in range(2):
                    for i in range(2):
                        for b in range(NB):
                            last = mmul(Q2[LN[i], q, 0:64], SX[LN[i], q, b, :], stg[LN[i], q, b, :], start=(b == 0), stop=(b == NB - 1))
                last.then_inc(*gd_pe.did(l, "ps"))
                pe.wait_ge(*gd_dve.at(l, "us"))

                def sample_out(Q, V_, A_, S_, X_):
                    for q in range(2):
                        for i in range(2):
                            mmul(Q[LN[i], q, SEQ:T], V_[LN[i], q, SEQ:T], A_[LN[i], q, SEQ:T], start=True, stop=False)
                            for b in range(NB):
                                cols = slice(SEQ + DS * b, SEQ + DS * (b + 1))
                                last = mmul(Q[LN[i], q, cols], S_[LN[i], q, b, :], X_[LN[i], q, cols], start=False, stop=(b == NB - 1))
                    return last

                def sample_state(Q, K_, X_):
                    for q in range(2):
                        for i in range(2):
                            last = mmul(Q[LN[i], q, :], K_[LN[i], q, SEQ:T], X_[LN[i], q, :, :].rearrange("p b v -> p (b v)"),
                                        start=True, stop=True)
                    return last

                sample_out(Q0, UU, QKD, stg, QE).then_inc(*gd_pe.did(l, "os"))
                logits(1)
                pe.wait_ge(*gd_dve.at(l, "ux"))
                sample_state(Q1, KW, UX).then_inc(*gd_pe.did(l, "ks"))
                logits(1)
                pe.wait_ge(*gd_dve.at(l, "ss"))
                head_norm(gd_act.at(l, "osq"), gd_pe, l, tt(3))
                logits(1)

                LFT, VT, ATT, QEh, KWC, KWh = tt(0), tt(1), tt(2), tt(3), tt(4), tt(5)
                ZQ = sl(8, 2)[:, 0:768].rearrange("p (r j t) -> p r j t", r=2, j=6)
                ZK = sl(10, 2)[:, 0:768].rearrange("p (r j t) -> p r j t", r=2, j=6)
                pe.wait_ge(*hg_act.at(l, "lf"))
                pe.wait_ge(*gd_act.at(l, "root"))
                tokens(Q0, sf).then_inc(*hg_pe.did(l, "lftok"))
                tokens(Q1, hgv).then_inc(*hg_pe.did(l, "vtok"))
                logits(1)
                pe.wait_ge(*hg_act.at(l, "vt"))
                for n in range(11):
                    if n < 10:
                        b, q = n // 2, n % 2
                        if n >= 2:
                            pe.wait_ge(*hg_act.at(l, f"e{n - 2}"))
                        for i in range(2):
                            last = mmul(Q2[LN[i], n % 2, :], LFT[LN[i], q, tk(b)], E[LN[i], kind(b), :, :].rearrange("p j t -> p (j t)"),
                                        start=True, stop=True)
                        last.then_inc(*hg_pe.did(l, f"x{n}"))
                    if 1 <= n <= 8:
                        products(1)
                        logits(1)
                    if n:
                        n, b, q = n - 1, (n - 1) // 2, (n - 1) % 2
                        pe.wait_ge(*hg_dve.at(l, f"z{n}"))
                        if n >= 2:
                            pe.wait_ge(*hg_dve.at(l, f"m{n - 2}"))
                        for i in range(2):
                            for j in range(6):
                                mmul(Q1[LN[i], n % 2, j * 64:(j + 1) * 64], ZK[LN[i], n % 2, j, :], ZQ[LN[i], n % 2, j, :], start=True, stop=True)
                            last = mmul(Q1[LN[i], n % 2, 384:448], sfn[LN[i], q, tk(b)], hgq[LN[i], q, tk(b)], start=True, stop=True)
                        last.then_inc(*hg_pe.did(l, f"a{n}"))
                tokens(Q0, KWC).then_inc(*hg_pe.did(l, "kw"))
                pe.wait_ge(*hg_act.at(l, "kw"))
                pe.wait_ge(*hg_dve.at(l, "r9"))
                pe.wait_ge(*hg_dve.at(l, "zero"))

                def chunk(c, steps, dve, V_, A_, X_, K_):
                    S = Sp[:, c % 2, :, 0:64]
                    if c:
                        pe.wait_ge(*dve.at(l, f"s{c - 1}"))
                    for q in range(2):
                        for i in range(2):
                            mmul(Q0[LN[i], q, tk(c)], V_[LN[i], q, tk(c)], A_[LN[i], q, tk(c)], start=True, stop=False)
                            last = mmul(Q0[LN[i], q, tk(c)], S[LN[i], q, :], X_[LN[i], q, tk(c)], start=False, stop=True)
                    if steps is ml_pe:
                        for q in range(2):
                            for i in range(2):
                                mmul(Q2[LN[i], q, tk(c)], ONES[LN[i], 0:64], A_[LN[i], q, tk(c)], start=True, stop=False)
                                last = mmul(Q2[LN[i], q, tk(c)], nst[LN[i], c % 2, q:q + 1].to_broadcast([64, 64]),
                                            X_[LN[i], q, tk(c)], start=False, stop=True)
                    last.then_inc(*steps.did(l, f"o{c}"))
                    for q in range(2):
                        for i in range(2):
                            last = mmul(Q1[LN[i], q, 0:64], K_[LN[i], q, tk(c)], V_[LN[i], q, tk(c)], start=True, stop=True)
                            if steps is ml_pe:
                                last = mmul(Q1[LN[i], q, 64:65], K_[LN[i], q, tk(c)], ONES[LN[i], 0:1], start=True, stop=True)
                    last.then_inc(*steps.did(l, f"k{c}"))

                for c in range(NPB):
                    chunk(c, hg_pe, hg_dve, VT, ATT, QEh, KWh)
                sample_out(Q0, VT, ATT, sth, QEh).then_inc(*hg_pe.did(l, "os"))
                pe.wait_ge(*hg_dve.at(l, "ux"))
                sample_state(Q1, KWh, UX).then_inc(*hg_pe.did(l, "ks"))
                logits(1)
                pe.wait_ge(*hg_dve.at(l, "ss"))
                head_norm(hg_act.at(l, "osq"), hg_pe, l, tt(7))
                logits(1)

                C = C6[1]
                XT, XW, AT, BTK = tt(0), tt(1), tt(2), sl(4, 2).rearrange("p (q b n) -> p q b n", q=2, b=NBLK)
                XWX = sl(6, 2)[:, 0:1024].rearrange("p (q b t) -> p q b t", q=2, b=NB)
                HT = sl(8)[:, 0:256].rearrange("p (q t) -> p q t", q=2)
                HTS = sl(9, 2)[:, 0:1024].rearrange("p (b t) -> p b t", b=NB)
                pe.wait_ge(conv_silu, 12 * (l + 1))
                pe.wait_ge(*hg_act.at(l, "root"))
                pe.wait_ge(*hg_dve.at(l, "o"))
                tokens(Q0, C[:, 0:2, :]).then_inc(*sd_pe.did(l, "xtok"))
                for b, q, i in units():
                    out = Q1[LN[i], q, b * 128:(b + 1) * 128] if b < NPB else Q2[LN[i], q, 0:128]
                    last = mmul(out, C[:, 2 + q, tk(b)], ID[:, :], start=True, stop=True)
                last.then_inc(*sd_pe.did(l, "btok"))
                products(1)
                logits(1)
                products(1)
                pe.wait_ge(*sd_dve.at(l, "xw"))
                pe.wait_ge(*sd_act.at(l, "bts"))
                for b, q, i in units():
                    last = mmul(Q0[LN[i], q, tk(b)], C[:, 2 + q, tk(b)], C[:, 4 + q, tk(b)], start=True, stop=True)
                last.then_inc(*sd_pe.did(l, "cb"))
                products(1)
                logits(1)
                products(1)
                pe.wait_ge(*sd_dve.at(l, "xx"))
                pe.wait_ge(*sd_dve.at(l, "zero"))
                for c in range(NPB):
                    S = Sp[:, c % 2, :, :]
                    if c:
                        pe.wait_ge(*sd_dve.at(l, f"s{c - 1}"))
                    for q in range(2):
                        last = nc.tensor.transpose(Q2[:, q, 0:128], S[:, q, :], ID[:, :])
                    last.then_inc(*sd_pe.did(l, f"t{c}"))
                    pe.wait_ge(*sd_act.at(l, f"t{c}"))
                    for q in range(2):
                        mmul(Q1[:, q, tk(c)], HT[:, q, :], C[:, 4 + q, tk(c)], start=True, stop=True)
                        for i in range(2):
                            last = mmul(Q0[LN[i], q, tk(c)], XT[LN[i], q, tk(c)], AT[LN[i], q, tk(c)], start=True, stop=True)
                    last.then_inc(*sd_pe.did(l, f"y{c}"))
                    products(1)
                    logits(1)
                    for q in range(2):
                        for i in range(2):
                            last = mmul(Q2[LN[i], q, 128:256], XW[LN[i], q, tk(c)], BTK[LN[i], q, c, :], start=True, stop=True)
                    last.then_inc(*sd_pe.did(l, f"k{c}"))
                Q2f = Q2[:, :, :].rearrange("p a (b n) -> p (a b) n", n=128)
                for q in range(2):
                    pe.wait_ge(*sd_dve.at(l, "ss0" if q else f"s{NPB - 1}"))
                    for b in range(NB):
                        last = nc.tensor.transpose(Q2f[:, b, :], sts[:, q, b, :], ID[:, :])
                    last.then_inc(*sd_pe.did(l, f"t_{q}"))
                    pe.wait_ge(*sd_act.at(l, f"t_{q}"))
                    for b in range(NB):
                        cols = slice(SEQ + DS * b, SEQ + DS * (b + 1))
                        last = mmul(Q1[:, q, cols], HTS[:, b, :], C[:, 4 + q, cols], start=True, stop=True)
                    for i in range(2):
                        last = mmul(Q0[LN[i], q, SEQ:T], XT[LN[i], q, SEQ:T], AT[LN[i], q, SEQ:T], start=True, stop=True)
                    last.then_inc(*sd_pe.did(l, f"y_{q}"))
                    logits(1)
                    for b in range(NB):
                        for i in range(2):
                            last = mmul(Q2f[LN[i], b, :], XWX[LN[i], q, b, :], BTK[LN[i], q, NPB, :], start=True, stop=True)
                    last.then_inc(*sd_pe.did(l, f"k_{q}"))
                logits(1)
                pe.wait_ge(*sd_act.at(l, "osq"))
                pe.wait_ge(*sd_dve.at(l, "yz"))
                for q in range(2):
                    last = mmul(Q1[:, 0, 0:T], ONES, tt(10)[:, q, :], start=(q == 0), stop=(q == 1))
                last.then_inc(*sd_pe.did(l, "nss"))
                logits(1)

                VTm, WT, QW, KWm = tt(0), tt(2), tt(3), tt(4)
                pe.wait_ge(*sd_act.at(l, "root"))
                pe.wait_ge(*sd_dve.at(l, "y1"))
                pe.wait_ge(*sd_dve.at(l, "ss1"))
                tokens(Q0, mlv).then_inc(*ml_pe.did(l, "vtok"))
                tokens(Q1, mlk).then_inc(*ml_pe.did(l, "ktok"))
                each(Q2, mlk, mlq).then_inc(*ml_pe.did(l, "kq"))
                products(2)
                pe.wait_ge(*ml_dve.at(l, "kw0"))
                pe.wait_ge(*ml_act.at(l, "vt"))
                pe.wait_ge(*ml_dve.at(l, "zero"))
                for c in range(NPB):
                    chunk(c, ml_pe, ml_dve, VTm, WT, QW, KWm)
                    products(1 if c else 2)
                    logits(1)
                sample_out(Q0, VTm, WT, stm, QW)
                for q in range(2):
                    for i in range(2):
                        mmul(Q2[LN[i], q, SEQ:T], ONES[LN[i], 0:64], WT[LN[i], q, SEQ:T], start=True, stop=False)
                        for b in range(NB):
                            cols = slice(SEQ + DS * b, SEQ + DS * (b + 1))
                            last = mmul(Q2[LN[i], q, cols], stn[LN[i], q, b:b + 1].to_broadcast([64, 64]), QW[LN[i], q, cols],
                                        start=False, stop=(b == NB - 1))
                last.then_inc(*ml_pe.did(l, "os"))
                products(1)
                logits(1)
                pe.wait_ge(*ml_dve.at(l, "ux"))
                pe.wait_ge(*ml_act.at(l, "dab"))
                sample_state(Q1, KWm, UX)
                for q in range(2):
                    for i in range(2):
                        last = mmul(Q2[LN[i], q, 400:400 + NB], KWm[LN[i], q, SEQ:T], BM[LN[i], :], start=True, stop=True)
                last.then_inc(*ml_pe.did(l, "ks"))
                logits(1)
                pe.wait_ge(*ml_dve.at(l, "ss"))
                head_norm(ml_act.at(l, "osq"), ml_pe, l, tt(7))
                logits(2)

                products(8)
                n2 = n0 + N_PROJ + N_GATED
                pe.wait_ge(gat_dve, 32 * l + 24)
                for s in range(N_OUT):
                    take(n2 + s)
                    for j in range(2):
                        m = 8 * l + 2 * s + j
                        if s:
                            pe.wait_ge(out_ev, m - 1)
                        linear(n2 + s, j, PJ[:, j, 0:T], merged).then_inc(slab_done if j else out_pe, 1)
                        if s or j:
                            norm_tile(3 * l + 1, 2 * s + j - 1)
                norm_tile(3 * l + 1, KT - 1)
                n3 = n2 + N_OUT

                def swiglu(n3):
                    for c in range(CH):
                        for up in range(2):
                            n = n3 + 2 * c + up
                            take(n)
                            Q = ((Q0, Q1), (PJ, Q2))[c % 2][up]
                            if c >= 2 and not up:
                                pe.wait_ge(ff_dve, c - 1)
                            for j in range(2):
                                last = linear(n, j, Q[:, j, 0:T], u, norm=None if c or up or j else 3 * l + 1)
                            last.then_inc(slab_done, 1)
                    pe.wait_ge(ff_dve, CH)
                    for d, (s, k0, k1) in enumerate(DOWN):
                        n = n3 + FT + d
                        take(n)
                        Q = (PJ, Q2)[s % 2]
                        if k0 == 0 and s >= 2:
                            pe.wait_ge(dn_dve, 2 * s - 2)
                        for j in range(2):
                            last = linear(n, j, Q[:, j, 0:T], hid, k0, k1, start=(k0 == 0), stop=(k1 == FT))
                        last.then_inc(slab_done, 1)
                        if s and k0 == 0:
                            norm_tile(3 * l + 2, 2 * s - 2)
                            norm_tile(3 * l + 2, 2 * s - 1)
                    norm_tile(3 * l + 2, KT - 2)
                    norm_tile(3 * l + 2, KT - 1)

                def gather(x):
                    for k in range(KT):
                        for t, (t0, t1) in enumerate(TT):
                            last = mmul(PJ[:, k // 4, (k % 4) * CAP:(k % 4 + 1) * CAP], utok[0:t1 - t0, t, k * 128:(k + 1) * 128],
                                        sel[0:t1 - t0, t, :], start=(t == 0), stop=(t == 2))
                    last.then_inc(x["xg_pe"], 1)

                def expert(e, x, n0, c0):
                    si, sd = x["slab_in"], x["slab_done"]

                    def ready(i):
                        n = n0 + i
                        per = loads(n, 0, N_X)
                        before = loads(n, -n0, 0) if x is main else (c0 - 1) * per
                        pe.wait_ge(si[n % R], e * (16 * per) + 16 * (before + loads(n, 0, i) + 1))

                    def loads(n, i0, i1):
                        return sum((n0 + i) % R == n % R for i in range(i0, i1))

                    for c in range(CH):
                        if c == 0:
                            pe.wait_ge(x["xg"], e + c0)
                        for up in range(2):
                            n = n0 + 2 * c + up
                            ready(2 * c + up)
                            Q = (Q0, Q1)[c % 2]
                            if up == 0:
                                pe.wait_ge(x["hid"], e * CH + (c0 * CH + c - 1))
                            if c == 1 and up == 0:
                                pe.wait_ge(x["hadd"], e * KT + c0 * KT)
                            w = slab(n)
                            for j in range(2):
                                for k in range(KT):
                                    last = mmul(Q[:, up, j * CAP:(j + 1) * CAP], w[:, k, j * 128:(j + 1) * 128], xg[:, k, :],
                                                start=(k == 0), stop=(k == KT - 1))
                            last.then_inc(sd, 1)
                        if c == 2:
                            pe.wait_ge(x["selw"], e + (c0 + 1))
                            for t, (t0, t1) in enumerate(TT):
                                last = nc.tensor.transpose(PJ[0:CAP, 0, t0:t1], selw[0:t1 - t0, t, :], ID[0:t1 - t0, 0:t1 - t0])
                            last.then_inc(x["selt_pe"], 1)
                    pe.wait_ge(x["sel"], e + (c0 + 1))
                    pe.wait_ge(x["selt"], e + (c0 + 1))
                    gather(x)
                    pe.wait_ge(x["hid"], e * CH + (c0 * CH + CH))
                    pe.wait_ge(x["yg"], e + c0)
                    for d in range(FT // 2):
                        n = n0 + 2 * CH + d
                        ready(2 * CH + d)
                        w = slab2(n)
                        for r in range(2):
                            for c in range(2):
                                last = mmul(Q2[0:CAP, c, :], hidx[:, 2 * d + r, :], w[:, r, c * 512:(c + 1) * 512],
                                            start=(d == 0 and r == 0), stop=(d == FT // 2 - 1 and r == 1))
                        last.then_inc(sd, 1 + N_SKIP if d == FT // 2 - 1 else 1)
                    pe.wait_ge(x["yg"], e + (c0 + 1))
                    pe.wait_ge(x["xg"], e + (c0 + 1))
                    for p in range(KT // 2):
                        if p >= 2:
                            pe.wait_ge(x["hadd"], e * KT + (c0 * KT + 2 * p - 2))
                        for j in range(2):
                            t = 2 * p + j
                            last = mmul((PJ, Q1)[p % 2][:, j, 0:T], yg[0:CAP, t * 128:(t + 1) * 128], selt[0:CAP, :], start=True, stop=True)
                        last.then_inc(x["scat"], 2)

                if l == 0:
                    swiglu(n3)
                    n4 = n3 + N_FF
                else:
                    for t, (t0, t1) in enumerate(TT):
                        for k in range(KT):
                            u_ready(None if t else 3 * l + 1, k)
                            last = nc.tensor.transpose((Q0, Q1, Q2)[t][0:t1 - t0, k // 4, (k % 4) * 128:(k % 4 + 1) * 128], u[:, k, t0:t1], ID[:, :])
                    last.then_inc(*rt_pe.did(0, "utok"))
                    for t, (t0, t1) in enumerate(TT):
                        for k in range(KT):
                            last = mmul(PJ[0:t1 - t0, 0, t * 8:(t + 1) * 8], u[:, k, t0:t1], wr[:, k, :], start=(k == 0), stop=(k == KT - 1))
                    last.then_inc(*rt_pe.did(0, "logit"))
                    pe.wait_ge(*rt_dve.at(0, "M"))
                    M = rt[:, :, 28:36]
                    for t, (t0, t1) in enumerate(TT):
                        w = t1 - t0
                        for j in range(t):
                            mmul(PJ[0:w, 1, t * 8:(t + 1) * 8], ONES[:, 0:w], M[:, j, :], start=(j == 0), stop=False)
                        mmul(PJ[0:w, 1, t * 8:(t + 1) * 8], STR[0:w, 0:w], M[0:w, t, :], start=(t == 0), stop=True)
                    for t, (t0, t1) in enumerate(TT):
                        last = mmul(PJ[:, 1, 24:32], ONES[0:t1 - t0, :], M[0:t1 - t0, t, :], start=(t == 0), stop=(t == 2))
                    last.then_inc(*rt_pe.did(0, "rank"))
                    pe.wait_ge(*rt_act.at(0, "utok2"))
                    pe.wait_ge(*rt_dve.at(0, "flag"))

                    def start(x):
                        pe.sem_inc(x["scat"], KT)
                        pe.sem_inc(x["selt_pe"], 1)
                        pe.wait_ge(x["sel"], 1)
                        gather(x)

                    start(main)
                    with pe.Fori(0, NE) as e:
                        expert(e, main, n3, 1)
                    with pe.If(pe.value_load(flag[0:1, 0:1], min_val=0, max_val=1)):
                        pe.wait_ge(main["hadd"], (NE + 1) * KT)
                        pe.sem_inc(over["slab_done"], R)
                        start(over)
                        for g in range(1, GROUPS):
                            with pe.Fori(0, NE) as e:
                                expert(e, over, NE * N_XV * (g - 1) + R, NE * (g - 1) + 1)
                    for i in range(KT):
                        norm_tile(3 * l + 2, i)
                    n4 = n3 + NE * N_XV
                pe.wait_ge(ple_in, 16 * (l + 1))
                first_slab.append(n4)
                for i in range(8):
                    logits(1)
                    products(1)
                    if i:
                        norm_tile(3 * l + 3, i - 1)
                norm_tile(3 * l + 3, KT - 1)

        @block.scalar
        def _(act):
            av = nc.scalar.activation
            act.dma_start(h[:, :, :], xT.rearrange("k p t -> p k t")).then_inc(h_in, 16)

            def norm_tile(k, i):
                act.wait_ge(*h_tile(k, i))
                av(sqh[:, i, :], h[:, i, :], ACT.Square).then_inc(*norm_act.did(k, f"sq{i}"))

            def norm_root(k):
                act.wait_ge(*norm_pe.at(k, "ss"))
                if k == 0:
                    act.wait_ge(consts_in, N_CONSTS)
                av(rstd[:, :], Q0[:, 0, 0:T], ACT.Sqrt, bias=EPSC[:, 0:1], scale=1.0 / DM).then_inc(*norm_act.did(k, "root"))
                act.wait_ge(*norm_act.at(k, "root"))

            def norm(k):
                for i in range(KT):
                    norm_tile(k, i)
                norm_root(k)

            tiles = []
            for name in PROJ:
                if name[:-1] in ("gdn_in", "ssd_in"):
                    tiles += [(name[:-1], 2 * int(name[-1]) + j) for j in range(2)]
                elif name == "ml_qk":
                    tiles += [("mlq", 0), ("mlk", 0)]
                else:
                    tiles += [(name, 0), (name, 1)]
            dst = {"hg_q": hgq, "hg_v": hgv, "ml_v": mlv, "gdn_z": gz, "hg_g": hgg, "ssd_z": sz, "ml_o": mlo}

            def conv_act(l, g, c):
                m = (2 * l + g) * 6 + c
                act.wait_ge(conv_tap, 8 * (m + 1))
                av(C6[g][:, c, :], cacc[g][:, m % 2, :], ACT.Silu).then_inc(conv_silu, 1)

            cacc = (XROW, tt(0))

            def head_norm(l, steps, dve, pe_, o, sq, rn, src):
                act.wait_ge(*dve.at(l, src))
                av(sq, o, ACT.Square).then_inc(*steps.did(l, "osq"))
                act.wait_ge(*steps.at(l, "osq"))
                act.wait_ge(*pe_.at(l, "nss"))
                av(rn, Q1[:, :, 0:T], ACT.Sqrt, bias=EPSC[:, 0:1], scale=1.0 / 64).then_inc(*steps.did(l, "root"))
                act.wait_ge(*steps.at(l, "root"))

            for l in range(DEPTH):
                if l == 0:
                    for i in range(KT):
                        norm_tile(0, i)
                    act.wait_ge(*setup_dve.at(0, "sub"))
                    av(lbt[:, 3:5, :], lbt[:, 1:3, :], ACT.Exp).then_inc(*setup_act.did(0, "exp"))
                    act.wait_ge(*setup_act.at(0, "exp"))
                    norm_root(0)
                tile, ltile = [0], [0]

                def proj(k):
                    for i in range(tile[0], tile[0] + k):
                        name, j = tiles[i]
                        m = 2 * N_PROJ * l + i
                        if i % 2 == 0:
                            act.wait_ge(proj_pe, m // 2 + 1)
                        else:
                            act.wait_ge(slab_done, BASE[l] + i // 2 + 1)
                        P = PJ[:, i % 2, 0:T]
                        if name in ("gdn_in", "ssd_in"):
                            if i == 0:
                                act.wait_ge(*pads.at(l, "zero"))
                            if name == "ssd_in" and j == 0:
                                act.wait_ge(conv_new, 4 * l + 2)
                                act.wait_ge(conv_tap, 96 * l + 48)
                            av(XP[:, j, 3:3 + SEQ], P[:, 0:SEQ], ACT.Copy)
                            last = av(XP[:, j, 3 + SEQ:XPW].rearrange("p (b t) -> p b t", b=NB)[:, :, 3:3 + DS],
                                      P[:, SEQ:T].rearrange("p (b t) -> p b t", b=NB), ACT.Copy)
                        elif name in ("mlq", "mlk"):
                            for hd in range(4):
                                d = (mlq if name == "mlq" else mlk)[64 * (hd % 2):64 * (hd % 2) + 32, hd // 2, :]
                                last = av(d, PJ[32 * hd:32 * hd + 32, i % 2, 0:T], ACT.Copy, scale=1.0 if name == "mlq" else 32 ** -0.5)
                        elif name == "hg_f":
                            av(sf[:, j, :], P, ACT.Sigmoid)
                            last = av(sfn[:, j, :], P, ACT.Sigmoid, scale=-1.0)
                        else:
                            fn = {"gdn_z": ACT.Silu, "hg_g": ACT.Silu, "ssd_z": ACT.Silu, "ml_o": ACT.Sigmoid}.get(name, ACT.Copy)
                            last = av(dst[name][:, j, :], P, fn)
                        last.then_inc(proj_ev, 1)
                    tile[0] += k

                def logits(k):
                    for i in range(ltile[0], ltile[0] + k):
                        m = 40 * l + i
                        act.wait_ge(gat_pe, m + 1)
                        if m >= 8:
                            act.wait_ge(gat_mul, m - 7)
                            if adds(m - 8):
                                act.wait_ge(gat_dve, adds(m - 8))
                        av(sg(m), PJ[:, 0, 0:T], ACT.Sigmoid).then_inc(gat_act, 1)
                    ltile[0] += k

                proj(2)
                for c in range(4):
                    conv_act(l, 0, c)
                    proj(1)
                conv_act(l, 0, 4)
                conv_act(l, 0, 5)
                act.wait_ge(*gp_dve.at(l, "smb"))
                av(beta[:, :, :], smb[:, 0, :, :], ACT.Sigmoid).then_inc(*gp_act.did(l, "beta"))
                act.wait_ge(*gp_act.at(l, "beta"))
                av(sm1[:, :, 0:2], pr(l, "alog").rearrange("p (a q) -> p a q", a=2), ACT.Exp).then_inc(*gp_act.did(l, "ea"))
                act.wait_ge(*gp_act.at(l, "ea"))
                act.wait_ge(*gp_dve.at(l, "spi"))
                av(sp3[:, 1, :], sp3[:, 0, :], ACT.Abs).then_inc(*gp_act.did(l, "abs"))
                act.wait_ge(*gp_act.at(l, "abs"))
                av(sp3[:, 2, :], sp3[:, 1, :], ACT.Exp, scale=-1.0).then_inc(*gp_act.did(l, "e"))
                act.wait_ge(*gp_act.at(l, "e"))
                proj(2)
                act.wait_ge(*gp_dve.at(l, "u1"))
                av(sp3[:, 4, :], sp3[:, 3, :], ACT.Ln).then_inc(*gp_act.did(l, "ln"))
                act.wait_ge(*gp_act.at(l, "ln"))
                proj(2)
                act.wait_ge(*gp_dve.at(l, "gt"))
                av(egt[:, :, :, :], gt[:, :, :, :], ACT.Exp).then_inc(*gp_act.did(l, "egt"))
                act.wait_ge(*gp_act.at(l, "egt"))
                for m, Q in ((0, Q0), (1, Q2), (2, Q0)):
                    if m == 2:
                        proj(1)
                    act.wait_ge(*gp_pe.at(l, f"gr{m}"))
                    av(GR[m], Q[:, :, 0:T], ACT.Copy).then_inc(*gp_act.did(l, f"gr{m}"))
                    act.wait_ge(*gp_act.at(l, f"gr{m}"))

                proj(1)
                C = C6[0]
                act.wait_ge(conv_silu, 12 * l + 6)
                sq4 = sl(0, 2).rearrange("p (c t) -> p c t", c=4)
                av(sq4, C[:, 0:4, :], ACT.Square).then_inc(*gd_act.did(l, "sq"))
                act.wait_ge(*gd_act.at(l, "sq"))
                act.wait_ge(*gd_pe.at(l, "l2"))
                av(sq4[:, 0:2, :], Q0[:, :, 0:T], ACT.Sqrt, bias=EPSC[:, 1:2], scale=64.0).then_inc(*gd_act.did(l, "rootq"))
                act.wait_ge(*gd_act.at(l, "rootq"))
                av(sq4[:, 2:4, :], Q1[:, :, 0:T], ACT.Sqrt, bias=EPSC[:, 0:1], scale=1.0).then_inc(*gd_act.did(l, "rootk"))
                act.wait_ge(*gd_act.at(l, "rootk"))
                proj(2)
                act.wait_ge(*gd_dve.at(l, "dmin"))
                av(tt(2), tt(2), ACT.Exp).then_inc(*gd_act.did(l, "dexp"))
                act.wait_ge(*gd_act.at(l, "dexp"))
                act.wait_ge(*gp_act.at(l, "gr2"))
                av(GR[0], GR[0], ACT.Exp).then_inc(*gd_act.did(l, "egrow"))
                act.wait_ge(*gd_act.at(l, "egrow"))
                proj(3)
                for j in range(6):
                    proj(2 if j > 1 else 1)
                    conv_act(l, 1, j)
                act.wait_ge(*gd_pe.at(l, "skt"))
                av(tt(1), Q0[:, :, 0:T], ACT.Copy).then_inc(*gd_act.did(l, "skt"))
                act.wait_ge(*gd_act.at(l, "skt"))
                proj(3)
                act.wait_ge(*hg_dve.at(l, "pre"))
                av(sf, sf, ACT.Ln).then_inc(*hg_act.did(l, "lf"))
                act.wait_ge(*hg_act.at(l, "lf"))
                logits(2)
                head_norm(l, gd_act, gd_dve, gd_pe, tt(9), tt(3), tt(8), "o")
                logits(1)

                act.wait_ge(*hg_pe.at(l, "lftok"))
                av(tt(0), Q0[:, :, 0:T], ACT.Copy).then_inc(*hg_act.did(l, "lft"))
                act.wait_ge(*hg_act.at(l, "lft"))
                act.wait_ge(*hg_pe.at(l, "vtok"))
                av(tt(1), Q1[:, :, 0:T], ACT.Copy).then_inc(*hg_act.did(l, "vt"))
                act.wait_ge(*hg_act.at(l, "vt"))
                logits(1)
                X = sl(6, 2)[:, 0:1024].rearrange("p (r j t) -> p r j t", r=2, j=8)
                for n in range(10):
                    b, q = n // 2, n % 2
                    act.wait_ge(*hg_pe.at(l, f"x{n}"))
                    if n >= 2:
                        act.wait_ge(*hg_dve.at(l, f"z{n - 2}"))
                    av(X[:, n % 2], Q2[:, n % 2, :].rearrange("p (j t) -> p j t", j=8), ACT.Exp).then_inc(*hg_act.did(l, f"x{n}"))
                    act.wait_ge(*hg_act.at(l, f"x{n}"))
                    o, i_ = (egc[:, q, b:b + 1], X[:, n % 2, 6, BL - 1:BL]) if b < NPB else (egc[:, q, NPB:], X[:, n % 2, 6, DS - 1::DS])
                    av(o, i_, ACT.Copy).then_inc(*hg_act.did(l, f"e{n}"))
                    act.wait_ge(*hg_act.at(l, f"e{n}"))
                    if 1 <= n <= 8:
                        logits(1)
                act.wait_ge(*hg_pe.at(l, "kw"))
                av(tt(5), Q0[:, :, 0:T], ACT.Copy).then_inc(*hg_act.did(l, "kw"))
                act.wait_ge(*hg_act.at(l, "kw"))
                act.wait_ge(*sd_dve.at(l, "dmin"))
                av(tt(12), tt(12), ACT.Exp).then_inc(*sd_act.did(l, "dexp"))
                act.wait_ge(*sd_act.at(l, "dexp"))
                av(GR[1], GR[1], ACT.Exp).then_inc(*sd_act.did(l, "egrow"))
                act.wait_ge(*sd_act.at(l, "egrow"))
                logits(1)
                head_norm(l, hg_act, hg_dve, hg_pe, tt(6), tt(7), tt(8), "o")
                logits(1)

                act.wait_ge(*sd_pe.at(l, "xtok"))
                act.wait_ge(*sd_dve.at(l, "xw"))
                av(tt(0), Q0[:, :, 0:T], ACT.Copy).then_inc(*sd_act.did(l, "xt"))
                act.wait_ge(*sd_act.at(l, "xt"))
                BTK = sl(4, 2).rearrange("p (q b n) -> p q b n", q=2, b=NBLK)
                act.wait_ge(*sd_pe.at(l, "btok"))
                av(BTK[:, :, 0:NPB, :], Q1[:, :, :].rearrange("p q (b n) -> p q b n", n=128), ACT.Copy).then_inc(*sd_act.did(l, "btp"))
                act.wait_ge(*sd_act.at(l, "btp"))
                av(BTK[:, :, NPB, :], Q2[:, :, 0:128], ACT.Copy).then_inc(*sd_act.did(l, "bts"))
                act.wait_ge(*sd_act.at(l, "bts"))
                logits(2)
                HT = sl(8)[:, 0:256].rearrange("p (q t) -> p q t", q=2)
                HTS = sl(9, 2)[:, 0:1024].rearrange("p (b t) -> p b t", b=NB)
                for c in range(NPB):
                    act.wait_ge(*sd_pe.at(l, f"t{c}"))
                    av(HT, Q2[:, :, 0:128], ACT.Copy).then_inc(*sd_act.did(l, f"t{c}"))
                    act.wait_ge(*sd_act.at(l, f"t{c}"))
                    logits(1)
                for q in range(2):
                    act.wait_ge(*sd_pe.at(l, f"t_{q}"))
                    av(HTS, Q2[:, :, :].rearrange("p a (b n) -> p (a b) n", n=128), ACT.Copy).then_inc(*sd_act.did(l, f"t_{q}"))
                    act.wait_ge(*sd_act.at(l, f"t_{q}"))
                    logits(1)
                logits(1)
                act.wait_ge(*sd_dve.at(l, "yz"))
                av(tt(10), tt(9), ACT.Square).then_inc(*sd_act.did(l, "osq"))
                act.wait_ge(*sd_act.at(l, "osq"))
                act.wait_ge(*sd_pe.at(l, "nss"))
                av(tt(8)[:, 0, :], Q1[:, 0, 0:T], ACT.Sqrt, bias=EPSC[:, 0:1], scale=1.0 / 256).then_inc(*sd_act.did(l, "root"))
                act.wait_ge(*sd_act.at(l, "root"))
                logits(1)

                act.wait_ge(*ml_pe.at(l, "vtok"))
                act.wait_ge(*sd_dve.at(l, "br"))
                av(tt(0), Q0[:, :, 0:T], ACT.Copy).then_inc(*ml_act.did(l, "vt"))
                act.wait_ge(*ml_act.at(l, "vt"))
                act.wait_ge(*ml_dve.at(l, "min"))
                av(tt(2), tt(11), ACT.Exp).then_inc(*ml_act.did(l, "wexp"))
                act.wait_ge(*ml_act.at(l, "wexp"))
                act.wait_ge(*ml_dve.at(l, "wpre"))
                av(tt(5), tt(5), ACT.Exp).then_inc(*ml_act.did(l, "win"))
                act.wait_ge(*ml_act.at(l, "win"))
                av(wend[:, :, :], wend[:, :, :], ACT.Exp).then_inc(*ml_act.did(l, "wend"))
                act.wait_ge(*ml_act.at(l, "wend"))
                act.wait_ge(*ml_dve.at(l, "mt"))
                av(tt(6), tt(6), ACT.Exp, scale=-1.0).then_inc(*ml_act.did(l, "emt"))
                act.wait_ge(*ml_act.at(l, "emt"))
                logits(NPB)
                act.wait_ge(*ml_pe.at(l, "os"))
                av(tt(7), Q2[:, :, 0:T], ACT.Abs).then_inc(*ml_act.did(l, "dab"))
                act.wait_ge(*ml_act.at(l, "dab"))
                logits(2)
                head_norm(l, ml_act, ml_dve, ml_pe, tt(9), tt(7), tt(8), "oo")
                logits(2)

                norm(3 * l + 1)

                n3 = BASE[l] + N_PROJ + N_GATED + N_OUT

                def expert(e, x, n0, c0):
                    for c in range(CH):
                        act.wait_ge(x["slab_done"], e * N_XV + (n0 + 2 * c + 1))
                        act.wait_ge(x["hid"], e * CH + (c0 * CH + c - 1))
                        av(sgx[:, c % 2, :], (Q0, Q1)[c % 2][:, 0, 0:2 * CAP], ACT.Silu).then_inc(x["silu"], 1)
                        if c == 4:
                            act.wait_ge(x["selt_pe"], e + (c0 + 1))
                            av(selt[0:CAP, :], PJ[0:CAP, 0, 0:T], ACT.Copy).then_inc(x["selt"], 1)
                    act.wait_ge(x["xg_pe"], e + (c0 + 1))
                    av(xg.rearrange("p (a k) t -> p a (k t)", a=2), PJ[:, :, 0:4 * CAP], ACT.Copy).then_inc(x["xg"], 1)
                    act.wait_ge(x["slab_done"], e * N_XV + (n0 + N_XV))
                    av(yg[0:CAP, :].rearrange("p (a c) -> p a c", a=2), Q2[0:CAP, :, :], ACT.Copy).then_inc(x["yg"], 1)

                if l == 0:
                    for c in range(CH):
                        act.wait_ge(slab_done, n3 + 2 * c + 1)
                        if c >= 2:
                            act.wait_ge(ff_dve, c - 1)
                        av(ffs[:, c % 2], (Q0, PJ)[c % 2][:, :, 0:T], ACT.Silu).then_inc(ff_act, 1)
                else:
                    act.wait_ge(*rt_pe.at(0, "utok"))
                    for t, (t0, t1) in enumerate(TT):
                        av(utok[0:t1 - t0, t, :].rearrange("p (a c) -> p a c", a=2), (Q0, Q1, Q2)[t][0:t1 - t0, :, :], ACT.Copy)\
                            .then_inc(*rt_act.did(0, f"utok{t}"))
                    act.wait_ge(*rt_dve.at(0, "d"))
                    av(rt[:, :, 24:25], rt[:, :, 24:25], ACT.Exp).then_inc(*rt_act.did(0, "e"))

                    def start(x):
                        act.sem_inc(x["silu"], CH)
                        act.sem_inc(x["yg"], 1)
                        act.sem_inc(x["selt"], 1)
                        act.wait_ge(x["xg_pe"], 1)
                        av(xg.rearrange("p (a k) t -> p a (k t)", a=2), PJ[:, :, 0:4 * CAP], ACT.Copy).then_inc(x["xg"], 1)

                    start(main)
                    with act.Fori(0, NE) as e:
                        expert(e, main, n3, 1)
                    act.wait_ge(*rt_dve.at(0, "flag"))
                    with act.If(act.value_load(flag[0:1, 0:1], min_val=0, max_val=1)):
                        start(over)
                        for g in range(1, GROUPS):
                            with act.Fori(0, NE) as e:
                                expert(e, over, NE * N_XV * (g - 1) + R, NE * (g - 1) + 1)
                norm(3 * l + 2)
                for i in range(8):
                    logits(1)
                    if i:
                        norm_tile(3 * l + 3, i - 1)
                norm_tile(3 * l + 3, KT - 1)
                norm_root(3 * l + 3)

        @block.vector
        def _(dve):
            v = nc.vector

            def norm(k):
                dve.wait_ge(*norm_act.at(k, "root"))
                v.reciprocal(rstd[:, :], rstd[:, :]).then_inc(*norm_dve.did(k, "rstd"))
                dve.wait_ge(*norm_dve.at(k, "rstd"))
                l = min(k // 3, DEPTH - 1)
                g = pr(l, "g_final" if k == N_NORM - 1 else ("g_mix", "g_ffn", "g_ple")[k % 3])
                for i in range(KT):
                    last = v.scalar_tensor_tensor(out=u[:, i, :], in0=h[:, i, :], scalar=g[:, i:i + 1], in1=rstd[:, :],
                                                  op0=ALU.mult, op1=ALU.mult)
                    if i % 2:
                        last.then_inc(*norm_dve.did(k, f"u{i // 2}"))

            dve.wait_ge(consts_in, N_CONSTS)
            dve.wait_ge(h_in, 16)
            lb = pr(0, "lb").rearrange("p (d q) -> p d q", d=2)
            v.tensor_tensor(lbt[:, 0, :], lb[:, 0, :], lb[:, 1, :], ALU.max).then_inc(*setup_dve.did(0, "max"))
            dve.wait_ge(*setup_dve.at(0, "max"))
            v.tensor_tensor(lbt[:, 1:3, :], lb, lbt[:, 0:1, :].to_broadcast([128, 2, 2]), ALU.subtract).then_inc(*setup_dve.did(0, "sub"))
            dve.wait_ge(*setup_dve.at(0, "sub"))
            dve.wait_ge(*setup_act.at(0, "exp"))
            v.tensor_tensor(lbt[:, 5, :], lbt[:, 3, :], lbt[:, 4, :], ALU.add).then_inc(*setup_dve.did(0, "sum"))
            dve.wait_ge(*setup_dve.at(0, "sum"))
            v.reciprocal(lbt[:, 6, :], lbt[:, 5, :]).then_inc(*setup_dve.did(0, "rcp"))
            dve.wait_ge(*setup_dve.at(0, "rcp"))
            v.memset(lbv[:, 0, 0, :], 0.0)
            v.tensor_tensor(lbv[:, 1, 0, :], lbt[:, 4, :], lbt[:, 6, :], ALU.mult).then_inc(*setup_dve.did(0, "sm"))
            dve.wait_ge(*setup_dve.at(0, "sm"))
            v.tensor_scalar(lbv[:, :, 1, :], lbv[:, :, 0, :], -1.0, 1.0, ALU.mult, ALU.add).then_inc(*setup_dve.did(0, "lb"))
            dve.wait_ge(*setup_dve.at(0, "lb"))
            v.memset(cf[:, 2, :], -1.0).then_inc(*setup_dve.did(0, "one"))
            dve.wait_ge(*setup_dve.at(0, "one"))

            cacc = (XROW, tt(0))

            for l in range(DEPTH):
                norm(3 * l)
                v.memset(XP[:, :, 0:3], 0.0)
                for i in range(2):
                    v.memset(mlq[64 * i + 32:64 * i + 64, :, :], 0.0)
                    last = v.memset(mlk[64 * i + 32:64 * i + 64, :, :], 0.0)
                last.then_inc(*pads.did(l, "zero"))
                dve.wait_ge(*pads.at(l, "zero"))
                dve.wait_ge(layer_in, PER_L_IN * (l + 1))

                samp = XP[:, :, 3 + SEQ:XPW].rearrange("p c (b t) -> p c b t", b=NB)

                def conv_halo(g):
                    for c in range(6):
                        last = v.tensor_copy(samp[:, c, :, 0:3], sconv[:, g, c, :, :])
                    last.then_inc(halo, 1)
                    dve.wait_ge(halo, 2 * l + g + 1)

                def conv(g, c):
                    cw = pr(l, "scw" if g else "gcw").rearrange("p (c j) -> p c j", c=6)
                    cb = pr(l, "scb" if g else "gcb")
                    m = (2 * l + g) * 6 + c
                    dve.wait_ge(proj_ev, 2 * N_PROJ * l + 2 * PROJ.index("ssd_in0" if g else "gdn_in0") + c + 1)
                    if m >= 2:
                        dve.wait_ge(conv_silu, m - 1)
                    a = cacc[g]
                    ap_, as_ = a[:, m % 2, 0:SEQ], a[:, m % 2, SEQ:T].rearrange("p (b t) -> p b t", b=NB)
                    v.tensor_scalar(ap_, XP[:, c, 0:SEQ], cw[:, c, 0:1], cb[:, c:c + 1], ALU.mult, ALU.add).then_inc(conv_tap, 1)
                    v.tensor_scalar(as_, samp[:, c, :, 0:DS], cw[:, c, 0:1], cb[:, c:c + 1], ALU.mult, ALU.add).then_inc(conv_tap, 1)
                    for j in range(1, 4):
                        dve.wait_ge(conv_tap, 8 * m + 2 * j - 1)
                        v.scalar_tensor_tensor(out=ap_, in0=XP[:, c, j:j + SEQ], scalar=cw[:, c, j:j + 1], in1=ap_,
                                               op0=ALU.mult, op1=ALU.add).then_inc(conv_tap, 1)
                        dve.wait_ge(conv_tap, 8 * m + 2 * j)
                        v.scalar_tensor_tensor(out=as_, in0=samp[:, c, :, j:j + DS], scalar=cw[:, c, j:j + 1], in1=as_,
                                               op0=ALU.mult, op1=ALU.add).then_inc(conv_tap, 1)

                def conv_last(g):
                    v.tensor_copy(cs[:, g, :, 0, :], XP[:, :, SEQ:SEQ + 3]).then_inc(conv_new, 1)
                    for c in range(6):
                        last = v.tensor_copy(cs[:, g, c, 1:, :], samp[:, c, :, DS:DS + 3])
                    last.then_inc(conv_new, 1)
                    dve.wait_ge(conv_tap, 48 * (2 * l + g + 1))
                    dve.wait_ge(conv_new, 2 * (2 * l + g + 1))

                ptile = [0]

                def products(k, dst=merged):
                    for i in range(ptile[0], ptile[0] + k):
                        n, t = i // 8, i % 8
                        m = 40 * l + i
                        n1 = BASE[l] + N_PROJ + (5 * n if n < 4 else N_GATED + N_OUT + (NE * N_XV if l else N_FF))
                        dve.wait_ge(gat_act, m + 1)
                        if t % 2 == 0:
                            dve.wait_ge(prod_pe, m // 2 + 1)
                        else:
                            dve.wait_ge(slab_done, n1 + t // 2 + 1)
                        if n == 0:
                            v.tensor_tensor(dst[:, t, :], sg(m), PJ[:, prod_bank(i), 0:T], ALU.mult).then_inc(gat_mul, 1)
                        else:
                            v.tensor_tensor(sg(m), sg(m), PJ[:, prod_bank(i), 0:T], ALU.mult).then_inc(gat_mul, 1)
                            dve.wait_ge(gat_mul, m + 1)
                            if adds(m - 1):
                                dve.wait_ge(gat_dve, adds(m - 1))
                            v.tensor_tensor(dst[:, t, :], dst[:, t, :], sg(m), ALU.add).then_inc(gat_dve, 1)
                    ptile[0] += k

                conv_halo(0)
                for c in range(6):
                    conv(0, c)
                conv_last(0)

                dve.wait_ge(*gp_pe.at(l, "small"))
                SMP = Q1[:, 0, 0:50].rearrange("p (b g q) -> p g q b", b=NBLK, g=5)
                gb = pr(l, "gb").rearrange("p (g q) -> p g q", g=5)
                v.tensor_tensor(smb[:, :, :, :], SMP, gb.unsqueeze(3).to_broadcast([128, 5, 2, NBLK]), ALU.add).then_inc(*gp_dve.did(l, "smb"))
                dve.wait_ge(*gp_dve.at(l, "smb"))
                smf = smb[:, :, :, :].rearrange("p g q b -> p (g q b)")
                w = 2 * NBLK
                spi, e_, u1, ln, d = sp3[:, 0, :], sp3[:, 2, :], sp3[:, 3, :], sp3[:, 4, :], sp3[:, 5, :]
                v.tensor_copy(spi[:, 0:2 * w], smf[:, w:3 * w]).then_inc(*gp_dve.did(l, "spc"))
                dve.wait_ge(*gp_dve.at(l, "spc"))
                v.tensor_scalar(spi[:, 2 * w:3 * w], smf[:, 4 * w:5 * w], -1.0, None, ALU.mult).then_inc(*gp_dve.did(l, "spi"))
                dve.wait_ge(*gp_dve.at(l, "spi"))
                dve.wait_ge(*gp_act.at(l, "e"))
                v.tensor_scalar(u1, e_, 1.0, None, ALU.add).then_inc(*gp_dve.did(l, "u1"))
                dve.wait_ge(*gp_dve.at(l, "u1"))
                v.tensor_scalar(d, u1, -1.0, None, ALU.add).then_inc(*gp_dve.did(l, "d"))
                dve.wait_ge(*gp_dve.at(l, "d"))
                z = sp3[:, 1, :]
                v.tensor_scalar(z, d, 0.0, None, ALU.is_equal).then_inc(*gp_dve.did(l, "z"))
                dve.wait_ge(*gp_dve.at(l, "z"))
                dve.wait_ge(*gp_act.at(l, "ln"))
                v.tensor_tensor(d, d, z, ALU.add).then_inc(*gp_dve.did(l, "dz"))
                dve.wait_ge(*gp_dve.at(l, "dz"))
                v.tensor_tensor(ln, ln, z, ALU.add).then_inc(*gp_dve.did(l, "lz"))
                dve.wait_ge(*gp_dve.at(l, "lz"))
                v.reciprocal(d, d).then_inc(*gp_dve.did(l, "rd"))
                dve.wait_ge(*gp_dve.at(l, "rd"))
                v.tensor_tensor(ln, ln, e_, ALU.mult).then_inc(*gp_dve.did(l, "le"))
                dve.wait_ge(*gp_dve.at(l, "le"))
                v.tensor_tensor(ln, ln, d, ALU.mult).then_inc(*gp_dve.did(l, "lp"))
                dve.wait_ge(*gp_dve.at(l, "lp"))
                v.scalar_tensor_tensor(out=spi, in0=spi, scalar=0.0, in1=ln, op0=ALU.max, op1=ALU.add).then_inc(*gp_dve.did(l, "sp"))
                dve.wait_ge(*gp_dve.at(l, "sp"))
                dve.wait_ge(*gp_act.at(l, "ea"))
                v.tensor_scalar(cf[:, 0:2, :], sm1[:, :, 0:2], -1.0, None, ALU.mult).then_inc(*gp_dve.did(l, "cf"))
                dve.wait_ge(*gp_dve.at(l, "cf"))
                v.tensor_tensor(G[:, :, :].rearrange("p b g -> p g b"), spi.rearrange("p (g b) -> p g b", b=NBLK),
                                cf[:, :, :].rearrange("p m q -> p (m q)").unsqueeze(2).to_broadcast([128, 6, NBLK]),
                                ALU.mult).then_inc(*gp_dve.did(l, "G"))
                dve.wait_ge(*gp_dve.at(l, "G"))
                dt = spi[:, w:2 * w].rearrange("p (q b) -> p q b", q=2)
                dve.wait_ge(*gp_pe.at(l, "gam"))
                v.tensor_copy(gt[:, :, :, :], Q1[:, 1, 0:60].rearrange("p (w b g) -> p w b g", w=2, b=NBLK)).then_inc(*gp_dve.did(l, "gt"))
                dve.wait_ge(*gp_dve.at(l, "gt"))
                dve.wait_ge(*gp_pe.at(l, "ig"))
                dve.wait_ge(*gp_act.at(l, "gr2"))
                dve.wait_ge(conv_silu, 12 * l + 6)
                v.tensor_tensor(XROW, Q2[:, :, 0:T], GR[2], ALU.subtract).then_inc(*gp_dve.did(l, "xrow"))
                dve.wait_ge(*gp_dve.at(l, "xrow"))

                def decay(steps, D, m):
                    v.tensor_tensor(bt(D), bt(GR[m]), bcol(gcol(gt, 0, m)), ALU.subtract).then_inc(*steps.did(l, "dsub"))
                    dve.wait_ge(*steps.at(l, "dsub"))
                    v.tensor_scalar(D, D, 0.0, None, ALU.min).then_inc(*steps.did(l, "dmin"))
                    dve.wait_ge(*steps.at(l, "dmin"))

                def decay_mask(steps, act_, D):
                    dve.wait_ge(*act_.at(l, "dexp"))
                    v.tensor_tensor(D, D, TRIM.unsqueeze(1).to_broadcast([128, 2, T]), ALU.mult).then_inc(*steps.did(l, "D"))
                    dve.wait_ge(*steps.at(l, "D"))

                def norm_gate(steps, act_, o, rn, w_, z_, br):
                    dve.wait_ge(*act_.at(l, "osq"))
                    v.scalar_tensor_tensor(out=o, in0=o, scalar=w_, in1=z_, op0=ALU.mult, op1=ALU.mult)\
                     .then_inc(*steps.did(l, "on"))
                    dve.wait_ge(*steps.at(l, "on"))
                    dve.wait_ge(*act_.at(l, "root"))
                    v.reciprocal(rn, rn).then_inc(*steps.did(l, "rn2"))
                    dve.wait_ge(*steps.at(l, "rn2"))
                    v.tensor_tensor(BR[:, br], o, rn, ALU.mult).then_inc(*steps.did(l, "br"))
                    dve.wait_ge(*steps.at(l, "br"))

                C = C6[0]
                LT, QKD, VB, KB, KW, Tm, U, W, AL, SV, SKT = [tt(i) for i in (3, 4, 5, 6, 7, 8, 9, 10, 11, 0, 1)]
                QE, UU, D = tt(2), tt(12), tt(2)
                sq4 = sl(0, 2).rearrange("p (c t) -> p c t", c=4)
                dve.wait_ge(*gd_act.at(l, "rootk"))
                v.reciprocal(sq4, sq4).then_inc(*gd_dve.did(l, "rn"))
                dve.wait_ge(*gd_dve.at(l, "rn"))
                v.tensor_tensor(C[:, 0:4, :], C[:, 0:4, :], sq4, ALU.mult).then_inc(*gd_dve.did(l, "qk"))
                dve.wait_ge(*gd_dve.at(l, "qk"))
                decay(gd_dve, D, 0)
                decay_mask(gd_dve, gd_act, D)
                dve.wait_ge(*gp_act.at(l, "egt"))
                v.tensor_tensor(sm1[:, :, :], beta[:, :, :], gcol(egt, 0, 0), ALU.mult).then_inc(*gd_dve.did(l, "bg"))
                dve.wait_ge(*gd_dve.at(l, "bg"))
                dve.wait_ge(*gd_pe.at(l, "ktok"))
                v.tensor_tensor(bt(KB), bt(Q0[:, :, 0:T]), bcol(sm1[:, :, :]), ALU.mult).then_inc(*gd_dve.did(l, "kb"))
                dve.wait_ge(*gd_dve.at(l, "kb"))
                v.tensor_tensor(bt(KW), bt(Q0[:, :, 0:T]), bcol(gcol(egt, 1, 0)), ALU.mult).then_inc(*gd_dve.did(l, "kw"))
                dve.wait_ge(*gd_dve.at(l, "kw"))
                dve.wait_ge(*gd_pe.at(l, "vtok"))
                v.tensor_tensor(bt(VB), bt(Q1[:, :, 0:T]), bcol(beta[:, :, :]), ALU.mult).then_inc(*gd_dve.did(l, "vb"))
                dve.wait_ge(*gd_dve.at(l, "vb"))
                dve.wait_ge(*gd_pe.at(l, "kk"))
                v.tensor_tensor(LT, Q2[:, :, 0:T], D, ALU.mult).then_inc(*gd_dve.did(l, "lt"))
                dve.wait_ge(*gd_dve.at(l, "lt"))
                dve.wait_ge(*gd_pe.at(l, "qk"))
                v.tensor_tensor(QKD, Q0[:, :, 0:T], D, ALU.mult).then_inc(*gd_dve.did(l, "qkd"))
                dve.wait_ge(*gd_dve.at(l, "qkd"))
                for i in range(2):
                    idl = ID[LN[i], LN[i]].unsqueeze(1).unsqueeze(1).to_broadcast([64, 2, NBLK, 64])
                    v.tensor_copy(bt(Tm)[LN[i]], idl)
                    last = v.tensor_copy(bt(U)[LN[i]], idl)
                last.then_inc(*gd_dve.did(l, "init"))
                dve.wait_ge(*gd_dve.at(l, "init"))
                dve.wait_ge(*gd_act.at(l, "egrow"))
                v.tensor_tensor(QE, C[:, 0:2, :], GR[0], ALU.mult).then_inc(*gd_dve.did(l, "qe"))
                dve.wait_ge(*gd_dve.at(l, "qe"))
                conv_halo(1)
                for j in range(6):
                    nb = NBLK if j < 3 else NPB
                    n = nb * BL
                    dve.wait_ge(*gd_dve.at(l, "qe"))
                    v.tensor_tensor(bt(AL)[:, :, 0:NPB, :], bt(LT)[:, :, 0:NPB, :],
                                    LM[:, 0, j, :].unsqueeze(1).unsqueeze(1).to_broadcast([128, 2, NPB, BL]), ALU.mult)
                    last = v.tensor_tensor(AL[:, :, SEQ:T], LT[:, :, SEQ:T], LM[:, 1, j, :].unsqueeze(1).to_broadcast([128, 2, BL]), ALU.mult)
                    last.then_inc(*gd_dve.did(l, f"al{j}"))
                    dve.wait_ge(*gd_dve.at(l, f"al{j}"))
                    dve.wait_ge(*gd_pe.at(l, f"w{j}"))
                    v.tensor_tensor(bt(W)[:, :, 0:nb], bt(Q0[:, :, 0:T])[:, :, 0:nb], bcol(beta[:, :, :])[:, :, 0:nb], ALU.mult)\
                     .then_inc(*gd_dve.did(l, f"wb{j}"))
                    dve.wait_ge(*gd_dve.at(l, f"wb{j}"))
                    dve.wait_ge(*gd_pe.at(l, f"tu{j}"))
                    v.tensor_tensor(Tm[:, :, 0:n], Tm[:, :, 0:n], Q1[:, :, 0:n], ALU.subtract).then_inc(*gd_dve.did(l, f"t{j}"))
                    dve.wait_ge(*gd_dve.at(l, f"t{j}"))
                    v.tensor_tensor(U[:, :, 0:n], U[:, :, 0:n], Q2[:, :, 0:n], ALU.subtract).then_inc(*gd_dve.did(l, f"u{j}"))
                    dve.wait_ge(*gd_dve.at(l, f"u{j}"))
                    conv(1, j)
                conv_last(1)
                dve.wait_ge(*gd_pe.at(l, "sv"))
                dve.wait_ge(conv_silu, 12 * (l + 1))
                v.tensor_copy(SV, Q1[:, :, 0:T]).then_inc(*gd_dve.did(l, "sv"))
                dve.wait_ge(*gd_dve.at(l, "sv"))
                v.memset(Sp[:, 0, :, 0:64], 0.0).then_inc(*gd_dve.did(l, "zero"))
                dve.wait_ge(*gd_dve.at(l, "zero"))
                EG = GR[0]

                def state(c, steps, pe_, dcol, q1=Q1, w=64, o=0):
                    dve.wait_ge(*pe_.at(l, f"k{c}"))
                    for q in range(2):
                        last = v.scalar_tensor_tensor(out=Sp[:, (c + 1) % 2, q, 0:w], in0=Sp[:, c % 2, q, 0:w], scalar=dcol(q, c),
                                                      in1=q1[:, q, o:o + w], op0=ALU.mult, op1=ALU.add)
                        if steps is ml_dve:
                            last = v.scalar_tensor_tensor(out=nst[:, (c + 1) % 2, q:q + 1], in0=nst[:, c % 2, q:q + 1],
                                                          scalar=dcol(q, c), in1=q1[:, q, 64:65], op0=ALU.mult, op1=ALU.add)
                    last.then_inc(*steps.did(l, f"s{c}"))
                    dve.wait_ge(*steps.at(l, f"s{c}"))

                def end_col(EG):
                    return lambda q, c: EG[:, q, (c + 1) * BL - 1:(c + 1) * BL]

                for c in range(NPB):
                    dve.wait_ge(*gd_pe.at(l, f"p{c}"))
                    v.tensor_tensor(UU[:, :, tk(c)], SV[:, :, tk(c)], Q2[:, :, 0:64], ALU.subtract).then_inc(*gd_dve.did(l, f"u{c}_"))
                    dve.wait_ge(*gd_dve.at(l, f"u{c}_"))
                    state(c, gd_dve, gd_pe, end_col(EG))
                SX = sl(5, 2)[:, 0:1024].rearrange("p (q b t) -> p q b t", q=2, b=NB)
                UX = sl(10, 2)[:, 0:1024].rearrange("p (q b t) -> p q b t", q=2, b=NB)
                dve.wait_ge(*gd_act.at(l, "skt"))

                def spread_t(out, src):
                    return v.tensor_tensor(out, src[:, :, SEQ:T].unsqueeze(2).to_broadcast([128, 2, NB, 64]),
                                           BT.unsqueeze(1).to_broadcast([128, 2, NB, 64]), ALU.mult)

                def spread_s(out, src):
                    return v.tensor_tensor(out, src[:, :, SEQ:T].unsqueeze(2).to_broadcast([128, 2, NB, 64]),
                                           BM.unsqueeze(1).unsqueeze(3).to_broadcast([128, 2, NB, 64]), ALU.mult)

                spread_t(SX, SKT).then_inc(*gd_dve.did(l, "sx"))
                dve.wait_ge(*gd_dve.at(l, "sx"))
                dve.wait_ge(*gd_pe.at(l, "ps"))
                v.tensor_tensor(UU[:, :, SEQ:T], SV[:, :, SEQ:T], Q2[:, :, 0:64], ALU.subtract).then_inc(*gd_dve.did(l, "us"))
                dve.wait_ge(*gd_dve.at(l, "us"))
                spread_s(UX, UU).then_inc(*gd_dve.did(l, "ux"))
                dve.wait_ge(*gd_dve.at(l, "ux"))
                dve.wait_ge(proj_ev, 2 * N_PROJ * (l + 1))
                for q in range(2):
                    last = v.tensor_scalar(sf[:, q, :], sf[:, q, :], lbv[:, l, 1, q:q + 1], lbv[:, l, 0, q:q + 1], ALU.mult, ALU.add)
                last.then_inc(*hg_dve.did(l, "pre"))
                dve.wait_ge(*hg_dve.at(l, "pre"))
                for q in range(2):
                    last = v.tensor_scalar(sfn[:, q, :], sfn[:, q, :], lbv[:, l, 1, q:q + 1], None, ALU.mult)
                last.then_inc(*hg_dve.did(l, "kin"))
                dve.wait_ge(*hg_dve.at(l, "kin"))

                def sample_state(steps, pe_, S, dec, q1=Q1):
                    dve.wait_ge(*pe_.at(l, "ks"))
                    v.tensor_tensor(S[:, :, :, :], S[:, :, :, :], dec.unsqueeze(3).to_broadcast([128, 2, NB, 64]), ALU.mult)\
                     .then_inc(*steps.did(l, "sd"))
                    dve.wait_ge(*steps.at(l, "sd"))
                    return v.tensor_tensor(S[:, :, :, :], S[:, :, :, :], q1[:, :, :].rearrange("p q (b v) -> p q b v", b=NB), ALU.add)

                dve.wait_ge(*gd_pe.at(l, "os"))
                v.tensor_copy(tt(9), Q0[:, :, 0:T]).then_inc(*gd_dve.did(l, "o"))
                dve.wait_ge(*gd_dve.at(l, "o"))
                sample_state(gd_dve, gd_pe, stg, EG[:, :, SEQ + DS - 1::DS]).then_inc(*gd_dve.did(l, "ss"))
                dve.wait_ge(*gd_dve.at(l, "ss"))
                norm_gate(gd_dve, gd_act, tt(9), tt(8), pr(l, "gnorm"), gz, 0)
                dve.wait_ge(*gd_dve.at(l, "br"))

                ATT, QEh, KWC = tt(2), tt(3), tt(4)
                X = sl(6, 2)[:, 0:1024].rearrange("p (r j t) -> p r j t", r=2, j=8)
                ZQ = sl(8, 2)[:, 0:768].rearrange("p (r j t) -> p r j t", r=2, j=6)
                ZK = sl(10, 2)[:, 0:768].rearrange("p (r j t) -> p r j t", r=2, j=6)
                MA = sl(12)[:, 0:448].rearrange("p (j t) -> p j t", j=7)
                for n in range(11):
                    if n < 10:
                        b, q = n // 2, n % 2
                        dve.wait_ge(*hg_act.at(l, f"x{n}"))
                        if n >= 2:
                            dve.wait_ge(*hg_pe.at(l, f"a{n - 2}"))
                        kb_, qb_ = sfn[:, q, tk(b)].unsqueeze(1), hgq[:, q, tk(b)].unsqueeze(1)
                        v.tensor_tensor(ZK[:, n % 2], X[:, n % 2, 0:6, :], kb_.to_broadcast([128, 6, BL]), ALU.mult)
                        v.tensor_tensor(ZQ[:, n % 2], X[:, n % 2, 0:6, :], qb_.to_broadcast([128, 6, BL]), ALU.mult)
                        v.tensor_tensor(QEh[:, q, tk(b)], X[:, n % 2, 6, :], hgq[:, q, tk(b)], ALU.mult)
                        v.tensor_tensor(KWC[:, q, tk(b)], X[:, n % 2, 7, :], sfn[:, q, tk(b)], ALU.mult).then_inc(*hg_dve.did(l, f"z{n}"))
                        dve.wait_ge(*hg_dve.at(l, f"z{n}"))
                    if 1 <= n <= 8:
                        products(1)
                    if n:
                        n, b, q = n - 1, (n - 1) // 2, (n - 1) % 2
                        dve.wait_ge(*hg_pe.at(l, f"a{n}"))
                        v.tensor_tensor(MA, Q1[:, n % 2, 0:448].rearrange("p (j t) -> p j t", j=7), LM[:, kind(b), :, :], ALU.mult)\
                         .then_inc(*hg_dve.did(l, f"m{n}"))
                        dve.wait_ge(*hg_dve.at(l, f"m{n}"))
                        v.tensor_reduce(ATT[:, q, tk(b)], MA.rearrange("p j t -> p t j"), AX.X, ALU.add).then_inc(*hg_dve.did(l, f"r{n}"))
                        dve.wait_ge(*hg_dve.at(l, f"r{n}"))
                dve.wait_ge(out_sem, 16 * (13 * l + 2))
                v.memset(Sp[:, 0, :, 0:64], 0.0).then_inc(*hg_dve.did(l, "zero"))
                dve.wait_ge(*hg_dve.at(l, "zero"))
                dve.wait_ge(*hg_act.at(l, "e9"))
                decay(sd_dve, tt(12), 1)
                for c in range(NPB):
                    state(c, hg_dve, hg_pe, lambda q, c: egc[:, q, c:c + 1])
                    if c == 1:
                        decay_mask(sd_dve, sd_act, tt(12))
                        v.tensor_tensor(sm1[:, :, :], dt, gcol(egt, 1, 1), ALU.mult).then_inc(*sd_dve.did(l, "wdt"))
                        dve.wait_ge(*sd_dve.at(l, "wdt"))
                spread_s(UX, tt(1)).then_inc(*hg_dve.did(l, "ux"))
                dve.wait_ge(*hg_dve.at(l, "ux"))
                dve.wait_ge(*hg_pe.at(l, "os"))
                v.tensor_copy(tt(6), Q0[:, :, 0:T]).then_inc(*hg_dve.did(l, "o"))
                dve.wait_ge(*hg_dve.at(l, "o"))
                sample_state(hg_dve, hg_pe, sth, egc[:, :, NPB:]).then_inc(*hg_dve.did(l, "ss"))
                dve.wait_ge(*hg_dve.at(l, "ss"))
                norm_gate(hg_dve, hg_act, tt(6), tt(8), pr(l, "hnorm"), hgg, 1)
                dve.wait_ge(*hg_dve.at(l, "br"))

                C = C6[1]
                XT, XW, AT, D = tt(0), tt(1), tt(2), tt(12)
                XWX = sl(6, 2)[:, 0:1024].rearrange("p (q b t) -> p q b t", q=2, b=NB)
                dve.wait_ge(*sd_pe.at(l, "xtok"))
                v.tensor_tensor(bt(XW), bt(Q0[:, :, 0:T]), bcol(sm1[:, :, :]), ALU.mult).then_inc(*sd_dve.did(l, "xw"))
                dve.wait_ge(*sd_dve.at(l, "xw"))
                products(2)
                dve.wait_ge(*sd_pe.at(l, "cb"))
                v.tensor_tensor(AT, Q0[:, :, 0:T], D, ALU.mult).then_inc(*sd_dve.did(l, "att0"))
                dve.wait_ge(*sd_dve.at(l, "att0"))
                v.tensor_tensor(bt(AT), bt(AT), bcol(dt), ALU.mult).then_inc(*sd_dve.did(l, "att"))
                dve.wait_ge(*sd_dve.at(l, "att"))
                spread_s(XWX, XW).then_inc(*sd_dve.did(l, "xx"))
                dve.wait_ge(*sd_dve.at(l, "xx"))
                dve.wait_ge(out_sem, 16 * (13 * l + 4))
                v.memset(Sp[:, 0, :, :], 0.0).then_inc(*sd_dve.did(l, "zero"))
                dve.wait_ge(*sd_dve.at(l, "zero"))
                dve.wait_ge(*sd_act.at(l, "egrow"))
                EG = GR[1]
                products(2)
                MR, WPRE = tt(12), tt(11)
                v.memset(mm[:, 0, :], 0.0).then_inc(*ml_dve.did(l, "m0"))
                dve.wait_ge(*ml_dve.at(l, "m0"))
                ends = slice(SEQ + DS - 1, T, DS)

                def sample_max():
                    first = XROW[:, :, SEQ::DS]
                    v.tensor_tensor(first, first, stmm[:, :, :], ALU.max).then_inc(*ml_dve.did(l, "inj"))
                    dve.wait_ge(*ml_dve.at(l, "inj"))
                    for q in range(2):
                        last = v.tensor_tensor_scan(MR[:, q, SEQ:T], RESET[:, :], XROW[:, q, SEQ:T], -3.0e38, ALU.add, ALU.max)
                    last.then_inc(*ml_dve.did(l, "scs"))
                    dve.wait_ge(*ml_dve.at(l, "scs"))
                    v.tensor_tensor(mms[:, :, :], MR[:, :, ends], GR[2][:, :, ends], ALU.add).then_inc(*ml_dve.did(l, "mms"))
                    dve.wait_ge(*ml_dve.at(l, "mms"))

                def end_weights():
                    v.tensor_tensor(xtk[:, :, :], smb[:, 3, :, :], gcol(gt, 0, 2), ALU.subtract).then_inc(*ml_dve.did(l, "xtk"))
                    dve.wait_ge(*ml_dve.at(l, "xtk"))
                    v.tensor_tensor(bt(WPRE), bcol(xtk[:, :, :]), bt(MR), ALU.subtract).then_inc(*ml_dve.did(l, "sub"))
                    dve.wait_ge(*ml_dve.at(l, "sub"))
                    v.tensor_scalar(WPRE, WPRE, 0.0, None, ALU.min).then_inc(*ml_dve.did(l, "min"))
                    dve.wait_ge(*ml_dve.at(l, "min"))
                    v.tensor_tensor(msel[:, :, :], MR[:, :, ends], BM.unsqueeze(1).to_broadcast([128, 2, NB]), ALU.mult).then_inc(*ml_dve.did(l, "selm"))
                    dve.wait_ge(*ml_dve.at(l, "selm"))
                    v.tensor_reduce(wend[:, :, NPB:NBLK], msel[:, :, :], AX.X, ALU.add).then_inc(*ml_dve.did(l, "sel"))
                    dve.wait_ge(*ml_dve.at(l, "sel"))
                    v.tensor_tensor(wend[:, :, 0:NPB], xtk[:, :, 0:NPB], MR[:, :, BL - 1:SEQ:BL], ALU.subtract)
                    v.tensor_tensor(wend[:, :, NPB:], xtk[:, :, NPB:], wend[:, :, NPB:], ALU.subtract).then_inc(*ml_dve.did(l, "we0"))
                    dve.wait_ge(*ml_dve.at(l, "we0"))

                for c in range(NPB):
                    products(1)
                    dve.wait_ge(*ml_dve.at(l, f"mm{c - 1}" if c else "m0"))
                    for q in range(2):
                        last = v.tensor_tensor_scan(MR[:, q, tk(c)], ONES[:, 0:BL], XROW[:, q, tk(c)], mm[:, c, q:q + 1], ALU.mult, ALU.max)
                    last.then_inc(*ml_dve.did(l, f"sc{c}"))
                    dve.wait_ge(*ml_dve.at(l, f"sc{c}"))
                    e0 = (c + 1) * BL - 1
                    v.tensor_tensor(mm[:, c + 1, :], MR[:, :, e0], GR[2][:, :, e0], ALU.add).then_inc(*ml_dve.did(l, f"mm{c}"))
                    dve.wait_ge(*ml_dve.at(l, f"mm{c}"))
                    state(c, sd_dve, sd_pe, end_col(EG), Q2, 128, 128)
                for q in range(2):
                    (end_weights if q else sample_max)()
                    dve.wait_ge(*sd_pe.at(l, f"k_{q}"))
                    v.tensor_tensor(sts[:, q], sts[:, q], EG[:, q, SEQ + DS - 1::DS].unsqueeze(2).to_broadcast([128, NB, 128]), ALU.mult)\
                     .then_inc(*sd_dve.did(l, f"sd{q}"))
                    dve.wait_ge(*sd_dve.at(l, f"sd{q}"))
                    v.tensor_tensor(sts[:, q], sts[:, q], Q2[:, :, :].rearrange("p a (b n) -> p (a b) n", n=128), ALU.add)\
                     .then_inc(*sd_dve.did(l, f"ss{q}"))
                    dve.wait_ge(*sd_dve.at(l, f"ss{q}"))
                Y = tt(9)
                v.tensor_tensor(Y, Q1[:, :, 0:T], EG, ALU.mult).then_inc(*sd_dve.did(l, "y0"))
                dve.wait_ge(*sd_dve.at(l, "y0"))
                v.tensor_tensor(Y, Y, Q0[:, :, 0:T], ALU.add).then_inc(*sd_dve.did(l, "y1"))
                dve.wait_ge(*sd_dve.at(l, "y1"))
                for q in range(2):
                    last = v.scalar_tensor_tensor(out=Y[:, q, :], in0=C[:, q, :], scalar=pr(l, "ssd_d")[:, q:q + 1], in1=Y[:, q, :],
                                                  op0=ALU.mult, op1=ALU.add)
                last.then_inc(*sd_dve.did(l, "y2"))
                dve.wait_ge(*sd_dve.at(l, "y2"))
                v.tensor_tensor(Y, Y, sz, ALU.mult).then_inc(*sd_dve.did(l, "yz"))
                dve.wait_ge(*sd_dve.at(l, "yz"))
                dve.wait_ge(*sd_act.at(l, "root"))
                v.reciprocal(tt(8)[:, 0, :], tt(8)[:, 0, :]).then_inc(*sd_dve.did(l, "rn2"))
                dve.wait_ge(*sd_dve.at(l, "rn2"))
                for q in range(2):
                    last = v.scalar_tensor_tensor(out=BR[:, 2, q, :], in0=Y[:, q, :], scalar=pr(l, "snorm")[:, q:q + 1],
                                                  in1=tt(8)[:, 0, :], op0=ALU.mult, op1=ALU.mult)
                last.then_inc(*sd_dve.did(l, "br"))
                dve.wait_ge(*sd_dve.at(l, "br"))

                WT, QW, KWm, WIN, EMT = tt(2), tt(3), tt(4), tt(5), tt(6)
                products(2)
                v.tensor_tensor(bt(WIN)[:, :, 0:NPB, :], mm[:, 0:NPB, :].rearrange("p c q -> p q c").unsqueeze(3).to_broadcast([128, 2, NPB, BL]),
                                bt(MR)[:, :, 0:NPB, :], ALU.subtract)
                v.tensor_tensor(WIN[:, :, SEQ:T].rearrange("p q (b t) -> p q b t", b=NB), stmm[:, :, :].unsqueeze(3).to_broadcast([128, 2, NB, DS]),
                                MR[:, :, SEQ:T].rearrange("p q (b t) -> p q b t", b=NB), ALU.subtract).then_inc(*ml_dve.did(l, "wpre"))
                dve.wait_ge(*ml_dve.at(l, "wpre"))
                v.tensor_tensor(EMT, MR, GR[2], ALU.add).then_inc(*ml_dve.did(l, "mt"))
                dve.wait_ge(*ml_dve.at(l, "mt"))
                dve.wait_ge(*ml_act.at(l, "win"))
                v.tensor_tensor(QW, mlq, WIN, ALU.mult).then_inc(*ml_dve.did(l, "qw"))
                dve.wait_ge(*ml_dve.at(l, "qw"))
                dve.wait_ge(*ml_act.at(l, "wexp"))
                v.tensor_tensor(WT, WT, TRIM.unsqueeze(1).to_broadcast([128, 2, T]), ALU.mult).then_inc(*ml_dve.did(l, "wt0"))
                dve.wait_ge(*ml_dve.at(l, "wt0"))
                dve.wait_ge(*ml_pe.at(l, "kq"))
                v.tensor_tensor(WT, WT, Q2[:, :, 0:T], ALU.mult).then_inc(*ml_dve.did(l, "wt"))
                dve.wait_ge(*ml_dve.at(l, "wt"))
                dve.wait_ge(*ml_act.at(l, "wend"))
                v.tensor_tensor(bt(KWm), bt(Q1[:, :, 0:T]), bcol(wend[:, :, :]), ALU.mult).then_inc(*ml_dve.did(l, "kw"))
                dve.wait_ge(*ml_dve.at(l, "kw"))
                v.memset(nst[:, 0, :], 0.0).then_inc(*ml_dve.did(l, "kw0"))
                dve.wait_ge(*ml_dve.at(l, "kw0"))
                dve.wait_ge(out_sem, 16 * (13 * l + 6))
                v.memset(Sp[:, 0, :, 0:64], 0.0).then_inc(*ml_dve.did(l, "zero"))
                dve.wait_ge(*ml_dve.at(l, "zero"))
                for c in range(NPB):
                    state(c, ml_dve, ml_pe, end_col(WIN))
                    products(1 if c else 2)
                dve.wait_ge(*ml_act.at(l, "vt"))
                spread_s(UX, tt(0)).then_inc(*ml_dve.did(l, "ux"))
                dve.wait_ge(*ml_dve.at(l, "ux"))
                products(1)
                dve.wait_ge(*ml_act.at(l, "dab"))
                v.tensor_tensor(tt(7), tt(7), EMT, ALU.max).then_inc(*ml_dve.did(l, "dmx"))
                dve.wait_ge(*ml_dve.at(l, "dmx"))
                v.reciprocal(tt(7), tt(7)).then_inc(*ml_dve.did(l, "drc"))
                dve.wait_ge(*ml_dve.at(l, "drc"))
                v.tensor_tensor(tt(9), Q0[:, :, 0:T], tt(7), ALU.mult).then_inc(*ml_dve.did(l, "oo"))
                dve.wait_ge(*ml_dve.at(l, "oo"))
                sample_state(ml_dve, ml_pe, stm, WIN[:, :, ends])
                v.tensor_tensor(stn[:, :, :], stn[:, :, :], WIN[:, :, ends], ALU.mult).then_inc(*ml_dve.did(l, "sn0"))
                dve.wait_ge(*ml_dve.at(l, "sn0"))
                v.tensor_tensor(stn[:, :, :], stn[:, :, :], Q2[:, :, 400:400 + NB], ALU.add).then_inc(*ml_dve.did(l, "ss"))
                dve.wait_ge(*ml_dve.at(l, "ss"))
                norm_gate(ml_dve, ml_act, tt(9), tt(8), pr(l, "mnorm"), mlo, 3)
                dve.wait_ge(*ml_dve.at(l, "br"))

                products(8)
                for t in range(8):
                    if t % 2 == 0:
                        dve.wait_ge(out_pe, 4 * l + t // 2 + 1)
                    else:
                        dve.wait_ge(slab_done, BASE[l] + N_PROJ + N_GATED + t // 2 + 1)
                    last = v.tensor_tensor(h[:, t, :], h[:, t, :], PJ[:, t % 2, 0:T], ALU.add).then_inc(out_ev, 1)
                dve.wait_ge(out_ev, 8 * l + 8)
                dve.sem_inc(h_done, 1)
                norm(3 * l + 1)

                n3 = BASE[l] + N_PROJ + N_GATED + N_OUT

                def choose(out, i, x, name, weighted):
                    for t, (t0, t1) in enumerate(TT):
                        w = t1 - t0
                        last = v.tensor_scalar(out[0:w, t, :], IOTA[0:w, 0:CAP], RK[0:w, t, bass.ds(i, 1)],
                                               CB[0:w, t, bass.ds(i, 1)] if weighted else None, ALU.is_equal,
                                               *([ALU.mult] if weighted else []))
                    last.then_inc(x[name], 1)

                def expert(e, x, n0, c0, turn0):
                    dve.wait_ge(x["selt_pe"], e + c0)
                    choose(selw, e + turn0, x, "selw", True)
                    dve.wait_ge(x["xg_pe"], e + c0)
                    choose(sel, e + (turn0 + 1), x, "sel", False)
                    for c in range(CH):
                        dve.wait_ge(x["silu"], e * CH + (c0 * CH + c + 1))
                        dve.wait_ge(x["slab_done"], e * N_XV + (n0 + 2 * c + 2))
                        v.tensor_tensor(hidx[:, 2 * c:2 * c + 2, :], sgx[:, c % 2, :].rearrange("p (f t) -> p f t", f=2),
                                        (Q0, Q1)[c % 2][:, 1, 0:2 * CAP].rearrange("p (f t) -> p f t", f=2), ALU.mult).then_inc(x["hid"], 1)
                    for p in range(KT // 2):
                        dve.wait_ge(x["scat"], e * KT + (c0 * KT + 2 * p + 2))
                        hp = h[:, 2 * p:2 * p + 2, :]
                        v.tensor_tensor(hp, hp, (PJ, Q1)[p % 2][:, :, 0:T], ALU.add).then_inc(x["hadd"], 2)
                    dve.wait_ge(x["hadd"], e * KT + (c0 * KT + KT))

                if l == 0:
                    for c in range(CH):
                        dve.wait_ge(ff_act, c + 1)
                        dve.wait_ge(slab_done, n3 + 2 * c + 2)
                        v.tensor_tensor(hid[:, 2 * c:2 * c + 2, :], ffs[:, c % 2], (Q1, Q2)[c % 2][:, :, 0:T], ALU.mult).then_inc(ff_dve, 1)
                    for t in range(8):
                        if t % 2 == 0:
                            last_d = max(d for d, x in enumerate(DOWN) if x[0] == t // 2)
                            dve.wait_ge(slab_done, n3 + FT + last_d + 1)
                        v.tensor_tensor(h[:, t, :], h[:, t, :], (PJ, Q2)[t // 2 % 2][:, t % 2, 0:T], ALU.add).then_inc(dn_dve, 1)
                    dve.wait_ge(dn_dve, 8)
                else:
                    LG, MX, IX = rt[:, :, 0:8], rt[:, :, 8:16], rt[:, :, 16:24]
                    OH = [rt[:, :, 40:48], rt[:, :, 48:56]]
                    M, CM = rt[:, :, 28:36], rt[:, :, 56:64]

                    def did(name, ins):
                        ins.then_inc(*rt_dve.did(0, name))
                        dve.wait_ge(*rt_dve.at(0, name))

                    dve.wait_ge(*rt_pe.at(0, "logit"))
                    v.tensor_copy(rt[:, 0:2, 0:8], PJ[:, 0, 0:16].rearrange("p (t e) -> p t e", t=2))
                    v.tensor_copy(rt[0:64, 2, 0:8], PJ[0:64, 0, 16:24])
                    did("lg", v.memset(rt[64:128, 2, 0:8], 0.0))
                    for t in range(3):
                        last = v.max(MX[:, t, :], LG[:, t, :])
                    did("max", last)
                    for t in range(3):
                        last = v.max_index(ridx[:, t, :], MX[:, t, :], LG[:, t, :])
                    did("idx", last)
                    did("idf", v.tensor_copy(IX, ridx[:, :, :]))
                    did("d", v.tensor_tensor(rt[:, :, 24:25], MX[:, :, 1:2], MX[:, :, 0:1], ALU.subtract))
                    dve.wait_ge(*rt_act.at(0, "e"))
                    did("s", v.tensor_scalar(rt[:, :, 25:26], rt[:, :, 24:25], 1.0, None, ALU.add))
                    did("r", v.reciprocal(rt[:, :, 26:27], rt[:, :, 25:26]))
                    did("w2", v.tensor_tensor(rt[:, :, 27:28], rt[:, :, 24:25], rt[:, :, 26:27], ALU.mult))
                    for c in range(2):
                        did(f"oh{c}", v.tensor_tensor(OH[c], IOTA[:, 0:8].unsqueeze(1).to_broadcast([128, 3, 8]),
                                                      IX[:, :, c:c + 1].to_broadcast([128, 3, 8]), ALU.is_equal))
                    did("M", v.tensor_tensor(M, OH[0], OH[1], ALU.add))
                    v.tensor_tensor(OH[0], OH[0], rt[:, :, 26:27].to_broadcast([128, 3, 8]), ALU.mult)
                    did("ohw", v.tensor_tensor(OH[1], OH[1], rt[:, :, 27:28].to_broadcast([128, 3, 8]), ALU.mult))
                    for g in range(GROUPS + 1):
                        last = v.tensor_tensor(CB[:, :, 8 * g:8 * g + 8], OH[0], OH[1], ALU.add)
                    did("comb", last)
                    dve.wait_ge(*rt_pe.at(0, "rank"))
                    v.memset(RK[64:128, 2, 0:NE * GROUPS], -1000.0)
                    v.memset(RK[:, :, NE * GROUPS:], -1000.0)
                    v.scalar_tensor_tensor(out=CM[:, 0:2, :], in0=PJ[:, 1, 0:16].rearrange("p (t e) -> p t e", t=2), scalar=1.0,
                                           in1=M[:, 0:2, :], op0=ALU.add, op1=ALU.mult)
                    did("rk0", v.scalar_tensor_tensor(out=CM[0:64, 2, :], in0=PJ[0:64, 1, 16:24], scalar=1.0, in1=M[0:64, 2, :],
                                                      op0=ALU.add, op1=ALU.mult))
                    did("rk1", v.tensor_reduce(rt[:, 1, 36:37], PJ[:, 1, 24:32], AX.X, ALU.max))
                    for g in range(GROUPS):
                        v.tensor_scalar(RK[:, 0:2, 8 * g:8 * g + 8], CM[:, 0:2, :], -1.0 - CAP * g, None, ALU.add)
                        last = v.tensor_scalar(RK[0:64, 2, 8 * g:8 * g + 8], CM[0:64, 2, :], -1.0 - CAP * g, None, ALU.add)
                    did("RK", last)
                    did("cnt", v.tensor_scalar(rt[:, 2, 36:37], rt[:, 1, 36:37], float(CAP), None, ALU.is_gt))
                    did("flag", v.tensor_copy(flag[:, :], rt[:, 2, 36:37]))


                    def start(x):
                        dve.sem_inc(x["hid"], CH)
                        dve.sem_inc(x["hadd"], KT)
                        dve.sem_inc(x["selw"], 1)

                    start(main)
                    choose(sel, 0, main, "sel", False)
                    with dve.Fori(0, NE) as e:
                        expert(e, main, n3, 1, 0)
                    with dve.If(dve.value_load(flag[0:1, 0:1], min_val=0, max_val=1)):
                        dve.wait_ge(main["selt_pe"], NE + 1)
                        dve.wait_ge(main["xg_pe"], NE + 1)
                        start(over)
                        choose(sel, NE, over, "sel", False)
                        for g in range(1, GROUPS):
                            with dve.Fori(0, NE) as e:
                                expert(e, over, NE * N_XV * (g - 1) + R, NE * (g - 1) + 1, NE * g)
                dve.sem_inc(h_done, 1)
                norm(3 * l + 2)
                products(8, h)
                dve.wait_ge(gat_dve, 32 * (l + 1))
                dve.sem_inc(h_done, 1)
            norm(N_NORM - 1)



_INS = ["xT", "pT", "cst", "par", "slabs", "xslabs", "wsm", "wr", "st_conv", "st_gdn", "st_hg", "st_ssd", "st_mlc", "st_mln", "st_mlm"]
_OUTS = [("y", (KT, 128, T)), ("conv", (DEPTH, 128, 2, 6, 1 + NB, 3)),
         ("gdn_p", (DEPTH, 128, 2, 64)), ("gdn_s", (DEPTH, 128, 2, NB, 64)),
         ("hg_p", (DEPTH, 128, 2, 64)), ("hg_s", (DEPTH, 128, 2, NB, 64)),
         ("ssd_p", (DEPTH, 128, 2, 128)), ("ssd_s", (DEPTH, 128, 2, NB, 128)),
         ("mlc_p", (DEPTH, 128, 2, 64)), ("mlc_s", (DEPTH, 128, 2, NB, 64)),
         ("mln_p", (DEPTH, 128, 2)), ("mln_s", (DEPTH, 128, 2, NB)),
         ("mlm_p", (DEPTH, 128, 2)), ("mlm_s", (DEPTH, 128, 2, NB))]


def constants():
    out = np.zeros((128, N_CST), np.float32)

    def put(name, a):
        o, w = CST[name]
        out[:, o:o + w] = np.broadcast_to(a.reshape(a.shape[0], -1), (128, w))

    s, t = np.arange(64)[:, None], np.arange(64)[None, :]
    E, LM, TRI = np.zeros((2, 8, 64, 64)), np.zeros((2, 7, 64, 64)), np.zeros((2, 64, 64))
    for k in range(2):
        same = np.ones((64, 64), bool) if k == 0 else (s // DS == t // DS)
        TRI[k] = (s <= t) & same
        E[k, 6], E[k, 7] = TRI[k], (s > t) & same
        for j in range(6 if k == 0 else 3):
            w = 2 ** j
            base = t // (2 * w) * (2 * w) + w
            right = t >= base
            E[k, j] = np.where(right, (s >= base) & (s <= t), (s > t) & (s < base))
            LM[k, j] = (s // (2 * w) == t // (2 * w)) & (s % (2 * w) < w) & (t % (2 * w) >= w)
        LM[k, 6] = s == t
    put("E", np.tile(E.transpose(2, 0, 1, 3), (2, 1, 1, 1)))
    put("LM", np.tile(LM.transpose(2, 0, 1, 3), (2, 1, 1, 1)))
    put("TRIM", np.tile(np.concatenate([TRI[0]] * NPB + [TRI[1]], axis=1), (2, 1)))
    put("ID", np.eye(128))
    put("BLK", np.kron(np.eye(2), np.ones((64, 64))))
    put("ONES", np.ones((128, 128)))
    put("BT", np.array([[t[0] // DS == b for b in range(NB)]]).astype(np.float32))
    put("BM", np.tile((s // DS == np.arange(NB)[None, :]), (2, 1)))
    put("RESET", np.where(t % DS == 0, -3.0e38, 0.0))
    put("IOTA", np.arange(128)[None, :])
    put("STR", np.arange(128)[:, None] < np.arange(128)[None, :])
    put("EPS", np.array([[EPS, 64 * EPS]]))
    return out


def lanes(a):
    a = a.reshape(a.shape[:-1] + (2, 2))
    return np.repeat(np.moveaxis(a, -1, 0), 64, axis=0)


def parameters(w, l):
    out = np.zeros((128, N_PAR), np.float32)

    def put(name, a):
        o, n = PAR[name]
        out[:, o:o + n] = a.reshape(128, n)

    for name, src in (("g_mix", w["g_mix"][l]), ("g_ffn", w["g_ffn"][l]), ("g_ple", w["g_ple"][l]), ("g_final", w["g_final"])):
        put(name, src.reshape(KT, 128).T)
    put("gcw", w["gdn_conv_w"][l].reshape(4, 6, 128).transpose(2, 1, 0))
    put("scw", w["ssd_conv_w"][l].reshape(4, 6, 128).transpose(2, 1, 0))
    put("scb", w["ssd_conv_b"][l].reshape(6, 128).T)
    for name, src in (("gnorm", "gdn_norm"), ("hnorm", "hgrn_norm"), ("mnorm", "ml_norm")):
        put(name, np.tile(w[src][l], 2))
    put("snorm", w["ssd_norm"][l].reshape(2, 128).T)
    put("ssd_d", lanes(w["ssd_d"][l]))
    z = np.zeros(4, np.float32)
    put("gb", lanes(np.stack([z, w["gdn_dt_bias"][l], w["ssd_dt_bias"][l], w["ml_ig_b"][l], w["ml_fg_b"][l]])))
    put("alog", lanes(np.stack([w["gdn_a_log"][l], w["ssd_a_log"][l]])))
    put("lb", w["hgrn_lb"].reshape(DEPTH, 2, 128).transpose(2, 0, 1))
    return out


def cut(slabs, n, w):
    k = w.shape[0] // 128
    for c in range(w.shape[1] // 256):
        slabs[n + c].reshape(128, 8, 256)[:, 0:k] = w[:, c * 256:(c + 1) * 256].reshape(k, 128, 256).transpose(1, 0, 2)
    return n + w.shape[1] // 256


def cut_rows(slabs, n, w):
    slabs[n].reshape(128, 2, 1024)[:] = w.reshape(2, 128, 1024).transpose(1, 0, 2)
    return n + 1


def cut_ff(slabs, n, wg, wu, wd):
    for c in range(FF // 256):
        n = cut(slabs, n, wg[:, c * 256:(c + 1) * 256])
        n = cut(slabs, n, wu[:, c * 256:(c + 1) * 256])
    for s, k0, k1 in DOWN:
        n = cut(slabs, n, wd[k0 * 128:k1 * 128, s * 256:(s + 1) * 256])
    return n


def kernel(**inputs):
    import concourse.bacc as _bacc
    from concourse.bass_utils import run_bass_kernel_spmd as _run

    w = {k: np.asarray(a) for k, a in inputs.items()}
    slabs = np.zeros((DEPTH * (N_PROJ + N_GATED + N_OUT + 5) + N_FF, 128, SLAB), np.float32)
    xslabs = np.zeros((NE * N_X, 128, SLAB), np.float32)
    starts = {"gdn_in0": 0, "gdn_in1": 256, "gdn_in2": 512, "gdn_z": 776, "hg_q": 1032, "hg_f": 1288, "hg_v": 1544,
              "hg_g": 1800, "ssd_z": 2056, "ssd_in0": 2312, "ssd_in1": 2568, "ssd_in2": 2824, "ml_qk": 3084,
              "ml_v": 3340, "ml_o": 3604}
    n = 0
    for l in range(DEPTH):
        wi = w["w_in"][l]
        for name in PROJ:
            n = cut(slabs, n, wi[:, starts[name]:starts[name] + 256])
        for b in range(4):
            n = cut(slabs, n, wi[:, 3860 + b * DM:3860 + (b + 1) * DM])
            n = cut_rows(slabs, n, w["w_branch"][l, b])
        n = cut(slabs, n, w["w_out"][l])
        if l % 2 == 0:
            n = cut_ff(slabs, n, w["w_ff_gate"][0], w["w_ff_up"][0], w["w_ff_down"][0])
        else:
            m = 0
            for e in range(NE):
                for c in range(CH):
                    for part in ("w_ex_gate", "w_ex_up"):
                        m = cut(xslabs, m, w[part][0, e][:, c * 256:(c + 1) * 256])
                for c in range(FT // 2):
                    m = cut_rows(xslabs, m, w["w_ex_down"][0, e][c * 256:(c + 1) * 256])
        n = cut(slabs, n, w["w_ple_gate"][l])
        n = cut_rows(slabs, n, w["w_ple"][l])
    assert n == len(slabs)

    def tokens(p, s):
        return np.concatenate([p.reshape(SEQ, -1), s.reshape(NB * DS, -1)]).T

    small = np.concatenate([w["w_in"][:, :, 768:776], w["w_in"][:, :, 3080:3084], w["w_in"][:, :, 3596:3604]], axis=2)
    conv = np.stack([w["state_gdn_conv"], w["state_ssd_conv"]], axis=1)

    def heads(a):
        L, B, H, K, V = a.shape
        return a.reshape(L, B, 2, 2, K, V).transpose(0, 3, 4, 2, 1, 5).reshape(L, 2 * K, 2, B, V)

    mlc = np.zeros((DEPTH, NB, 4, 64, 64), np.float32)
    mlc[:, :, :, 0:32] = w["state_mlstm_c"]
    mln = np.zeros((DEPTH, NB, 4, 64, 1), np.float32)
    mln[:, :, :, 0:32, 0] = w["state_mlstm_n"]
    arrays = {
        "xT": tokens(w["x_prompt"], w["x_sample"]).reshape(KT, 128, T),
        "pT": np.stack([tokens(w["p_prompt"][l], w["p_sample"][l]).reshape(2, 128, T).transpose(1, 0, 2) for l in range(DEPTH)]),
        "cst": constants(),
        "par": np.stack([parameters(w, l) for l in range(DEPTH)]),
        "slabs": slabs, "xslabs": xslabs,
        "wsm": small.reshape(DEPTH, KT, 128, 20).transpose(0, 2, 1, 3),
        "wr": w["w_router"][0].reshape(KT, 128, NE).transpose(1, 0, 2),
        "st_conv": conv.reshape(DEPTH, 2, NB, 3, 6, 128).transpose(0, 5, 1, 4, 2, 3),
        "st_gdn": heads(w["state_gdn"]), "st_hg": heads(w["state_hgrn"]), "st_ssd": heads(w["state_ssd"]),
        "st_mlc": heads(mlc), "st_mln": heads(mln)[..., 0],
        "st_mlm": np.stack([lanes(w["state_mlstm_m"][l]).transpose(0, 2, 1) for l in range(DEPTH)]),
    }
    arrays = {f"in_{k}_dram": np.ascontiguousarray(a) for k, a in arrays.items()}
    nc = _bacc.Bacc("TRN2", target_bir_lowering=False, num_devices=1)
    args = [nc.dram_tensor(f"in_{k}_dram", arrays[f"in_{k}_dram"].shape, F32, kind="ExternalInput").ap() for k in _INS]
    args += [nc.dram_tensor(f"out_{k}_dram", shape, F32, kind="ExternalOutput").ap() for k, shape in _OUTS]
    trunk_kernel(nc, *args)
    r = _run(nc, [arrays], core_ids=[0])
    o = {k: np.asarray(r.results[0][f"out_{k}_dram"]).reshape(shape) for k, shape in _OUTS}

    y = o["y"].reshape(DM, T).T
    cv = o["conv"].transpose(0, 2, 4, 5, 3, 1).reshape(DEPTH, 2, 1 + NB, 3, 768)

    def back(a, k=64):
        L, _, _, B, V = a.shape
        return np.ascontiguousarray(a.reshape(L, 2, 64, 2, B, V).transpose(0, 4, 3, 1, 2, 5).reshape(L, B, 4, 64, V)[:, :, :, 0:k])

    def states(sfx):
        one = (lambda a: a[:, :, :, None]) if sfx == "p" else (lambda a: a)
        c = cv[:, :, 0:1] if sfx == "p" else cv[:, :, 1:]
        m = one(o["mlm_" + sfx])
        return (np.ascontiguousarray(c[:, 0]), back(one(o["gdn_" + sfx])), back(one(o["hg_" + sfx])), np.ascontiguousarray(c[:, 1]),
                back(one(o["ssd_" + sfx])), back(one(o["mlc_" + sfx]), 32), back(one(o["mln_" + sfx])[..., None], 32)[..., 0],
                np.ascontiguousarray(m.reshape(DEPTH, 2, 64, 2, -1)[:, :, 0].transpose(0, 3, 2, 1).reshape(DEPTH, -1, 4)))

    return (np.ascontiguousarray(y[0:SEQ]).reshape(1, SEQ, DM), np.ascontiguousarray(y[SEQ:]).reshape(NB, DS, DM),
            *states("p"), *states("s"))
```
